# Optimizing a Trainium2 kernel written in Bass

```python
import math
import jax
import jax.numpy as jnp
from jax import lax
import numpy as np

D_MODEL = 1024
BATCH = 1
SEQ = 2048
DEPTH = 2
DEC_BATCH = 8
DEC_SEQ = 1
PAST_LEN = 2048
PAGE_SIZE = 128

N_HEADS = 16
HEAD_DIM = 64
N_KV_HEADS = 4
Q_PER_KV = N_HEADS // N_KV_HEADS
IDX_HEADS = 8
IDX_DIM = 64
IDX_SCALE = (IDX_HEADS * IDX_DIM) ** -0.5
TOPK_MAX = 256
ROPE_THETA = 500000.0
ROPE_FRACTION = 4
Q_BLOCK = 128
ATTN_SIZES = (N_HEADS * HEAD_DIM, N_KV_HEADS * HEAD_DIM, N_KV_HEADS * HEAD_DIM,
              IDX_HEADS * IDX_DIM, IDX_DIM, IDX_HEADS)
ATTN_PROJ = sum(ATTN_SIZES)
ATTN_SPLITS = tuple(int(s) for s in np.cumsum(ATTN_SIZES)[:-1])
D_RNN = D_MODEL
RG_BLOCKS = 8
RG_BLOCK_W = D_RNN // RG_BLOCKS
CONV_W = 4
RG_C = 8.0
N_GROUPS = 4
EXPERTS_PER_GROUP = 8
N_EXPERTS = N_GROUPS * EXPERTS_PER_GROUP
TOPK_IN_GROUP = 2
D_EXPERT = 256
MOE_BLOCK = 128
N_ATTN = (DEPTH + 1) // 2
N_REC = DEPTH // 2
EPS = 1e-6

kernel_name = 'dsa_rglru_hier_moe_adaln_step'

def rmsnorm(x, g):
    xf = x.astype(jnp.float32)
    xf = xf * lax.rsqrt(jnp.mean(xf * xf, axis=-1, keepdims=True) + EPS)
    return (xf * g.astype(jnp.float32)).astype(x.dtype)

def modulate(x, g, shift, scale):
    return rmsnorm(x, g) * (1 + scale[:, None, :]) + shift[:, None, :]

def adaln(c, w, b):
    return jnp.split(jax.nn.silu(c) @ w + b, 6, axis=-1)

def rope_partial(x, pos):
    d = x.shape[-1]
    rot = d // ROPE_FRACTION
    half = rot // 2
    inv = jnp.exp(-math.log(ROPE_THETA) * jnp.arange(half, dtype=jnp.float32) * (2.0 / rot))
    ang = pos.astype(jnp.float32)[:, None] * inv[None, :]
    cos = jnp.cos(ang)[None, :, None, :].astype(x.dtype)
    sin = jnp.sin(ang)[None, :, None, :].astype(x.dtype)
    x1, x2, rest = x[..., :half], x[..., half:rot], x[..., rot:]
    return jnp.concatenate([x1 * cos - x2 * sin, x1 * sin + x2 * cos, rest], axis=-1)

def gather_rows(arr, idx):
    return jax.vmap(lambda a, i: a[i])(arr, idx)

def attn_project(h, w_in, pos):
    B, T, _ = h.shape
    q, k, v, qi, ki, wi = jnp.split(h @ w_in, ATTN_SPLITS, axis=-1)
    q = rope_partial(q.reshape(B, T, N_HEADS, HEAD_DIM), pos)
    k = rope_partial(k.reshape(B, T, N_KV_HEADS, HEAD_DIM), pos)
    v = v.reshape(B, T, N_KV_HEADS, HEAD_DIM)
    qi = rope_partial(qi.reshape(B, T, IDX_HEADS, IDX_DIM), pos)
    ki = rope_partial(ki[:, :, None, :], pos)[:, :, 0]
    return q, k, v, qi, ki, wi

def indexer_scores(qi, wi, ki, q_pos, k_pos):
    dots = jnp.einsum('bqhd,bsd->bqhs', qi.astype(jnp.float32), ki.astype(jnp.float32))
    s = jnp.einsum('bqhs,bqh->bqs', jax.nn.relu(dots), wi.astype(jnp.float32) * IDX_SCALE)
    return jnp.where(k_pos[None, None, :] <= q_pos[None, :, None], s, -jnp.inf)

def sparse_attend(q, k_sel, v_sel, valid):
    B, Q = q.shape[:2]
    qg = q.reshape(B, Q, N_KV_HEADS, Q_PER_KV, HEAD_DIM)
    s = jnp.einsum('bqngd,bqknd->bqngk', qg, k_sel).astype(jnp.float32) * (HEAD_DIM ** -0.5)
    s = jnp.where(valid[:, :, None, None, :], s, -jnp.inf)
    p = jax.nn.softmax(s, axis=-1).astype(v_sel.dtype)
    o = jnp.einsum('bqngk,bqknd->bqngd', p, v_sel)
    return o.reshape(B, Q, N_HEADS * HEAD_DIM)

def dsa_prompt(q, k, v, qi, ki, wi):
    B, T = q.shape[:2]
    topk = min(TOPK_MAX, T // 4)
    nblk = T // Q_BLOCK
    k_pos = jnp.arange(T)

    def block(args):
        qb, qib, wib, start = args
        q_pos = start + jnp.arange(Q_BLOCK)
        sc = indexer_scores(qib, wib, ki, q_pos, k_pos)
        _, idx = lax.top_k(sc, topk)
        valid = idx <= q_pos[None, :, None]
        return sparse_attend(qb, gather_rows(k, idx), gather_rows(v, idx), valid)

    def to_blocks(a):
        return a.reshape(B, nblk, Q_BLOCK, *a.shape[2:]).swapaxes(0, 1)

    out = lax.map(block, (to_blocks(q), to_blocks(qi), to_blocks(wi),
                          jnp.arange(nblk) * Q_BLOCK))
    return out.swapaxes(0, 1).reshape(B, T, N_HEADS * HEAD_DIM)

def dsa_sample(q, k_new, v_new, qi, ki_new, wi, cache_k_l, cache_v_l, cache_ki_l, page_table):
    DB, DQ = q.shape[:2]
    past = page_table.shape[1] * PAGE_SIZE
    L = past + DQ
    topk = min(TOPK_MAX, L // 4)
    ki_past = cache_ki_l[page_table].reshape(DB, past, IDX_DIM)
    ki_all = jnp.concatenate([ki_past, ki_new.astype(ki_past.dtype)], axis=1)
    q_pos = past + jnp.arange(DQ)
    sc = indexer_scores(qi, wi, ki_all, q_pos, jnp.arange(L))
    _, idx = lax.top_k(sc, topk)
    valid = idx <= q_pos[None, :, None]
    is_new = (idx >= past)[..., None, None]
    pidx = jnp.minimum(idx, past - 1)
    phys = gather_rows(page_table, pidx // PAGE_SIZE)
    off = pidx % PAGE_SIZE
    nidx = jnp.clip(idx - past, 0, DQ - 1)
    k_sel = jnp.where(is_new, gather_rows(k_new, nidx), cache_k_l[phys, off])
    v_sel = jnp.where(is_new, gather_rows(v_new, nidx), cache_v_l[phys, off])
    return sparse_attend(q, k_sel, v_sel, valid)

def rglru_block(h, conv_buf, h0, w_in, conv_w, conv_b, w_a, b_a, w_x, b_x, lam, w_out):
    B, T, _ = h.shape
    gate_in, xb = jnp.split(h @ w_in, 2, axis=-1)
    gate = jax.nn.gelu(gate_in)
    xcat = jnp.concatenate([conv_buf.astype(xb.dtype), xb], axis=1)
    xc = conv_b + sum(xcat[:, j:j + T] * conv_w[j] for j in range(CONV_W))
    new_buf = xcat[:, T:]
    xcb = xc.reshape(B, T, RG_BLOCKS, RG_BLOCK_W)
    r = jax.nn.sigmoid(jnp.einsum('btnc,ncd->btnd', xcb, w_a).reshape(B, T, D_RNN) + b_a)
    i = jax.nn.sigmoid(jnp.einsum('btnc,ncd->btnd', xcb, w_x).reshape(B, T, D_RNN) + b_x)
    log_a = -RG_C * r.astype(jnp.float32) * jax.nn.softplus(-lam.astype(jnp.float32))
    a = jnp.exp(log_a)
    u = jnp.sqrt(-jnp.expm1(2.0 * log_a)) * (i * xc).astype(jnp.float32)

    def step(hc, au):
        hc = au[0] * hc + au[1]
        return hc, hc

    hT, hs = lax.scan(step, h0.astype(jnp.float32), (a.swapaxes(0, 1), u.swapaxes(0, 1)))
    y = hs.swapaxes(0, 1).astype(h.dtype) * gate
    return y @ w_out, hT.astype(h.dtype), new_buf

def dispatch_experts(x, eidx, ew, w1, w2):
    N, K = eidx.shape
    D = x.shape[-1]
    A = N * K
    blk = max(8, min(MOE_BLOCK, A // N_EXPERTS))
    nb = -(-A // blk) + N_EXPERTS
    flat_e = eidx.reshape(A)
    flat_t = jnp.repeat(jnp.arange(N), K)
    flat_w = ew.reshape(A)
    order = jnp.argsort(flat_e)
    se, st, sw = flat_e[order], flat_t[order], flat_w[order]
    counts = jnp.bincount(flat_e, length=N_EXPERTS)
    start = jnp.cumsum(counts) - counts
    padded = (counts + blk - 1) // blk * blk
    pend = jnp.cumsum(padded)
    pstart = pend - padded
    dest = pstart[se] + (jnp.arange(A) - start[se])
    row_tok = jnp.full((nb * blk,), N, jnp.int32).at[dest].set(st)
    blk_expert = jnp.minimum(jnp.searchsorted(pend, jnp.arange(nb) * blk, side='right'), N_EXPERTS - 1)
    x_pad = jnp.concatenate([x, jnp.zeros((1, D), x.dtype)], axis=0)
    xb = x_pad[row_tok].reshape(nb, blk, D)

    def run(args):
        xi, e = args
        g, u = jnp.split(xi @ w1[e], 2, axis=-1)
        return (jax.nn.silu(g) * u) @ w2[e]

    yb = lax.map(run, (xb, blk_expert)).reshape(nb * blk, D)
    return jnp.zeros((N, D), x.dtype).at[st].add(yb[dest] * sw[:, None])

def hier_moe(h, wg, bg, we, be, w1, w2):
    B, T, D = h.shape
    x = h.reshape(B * T, D)
    g_logits = (x @ wg + bg).astype(jnp.float32)
    grp = jnp.argmax(g_logits, axis=-1)
    g_w = jnp.take_along_axis(jax.nn.softmax(g_logits, axis=-1), grp[:, None], axis=-1)
    e_logits = (x @ we + be).astype(jnp.float32).reshape(B * T, N_GROUPS, EXPERTS_PER_GROUP)
    e_in = jnp.take_along_axis(e_logits, grp[:, None, None], axis=1)[:, 0]
    top_w, top_i = lax.top_k(jax.nn.softmax(e_in, axis=-1), TOPK_IN_GROUP)
    top_w = top_w / jnp.sum(top_w, axis=-1, keepdims=True) * g_w
    eidx = grp[:, None] * EXPERTS_PER_GROUP + top_i
    y = dispatch_experts(x, eidx, top_w.astype(x.dtype), w1, w2)
    return y.reshape(B, T, D)

def setup_inputs(seed: int = 0) -> dict:
    key = jax.random.key(seed)
    ks = iter(jax.random.split(key, 40))
    f32 = jnp.float32

    def nrm(shape, scale):
        return jax.random.normal(next(ks), shape, f32) * scale

    n_pages = PAST_LEN // PAGE_SIZE
    n_pool = (DEC_BATCH * n_pages * 5 + 3) // 4
    page_table = jax.random.permutation(next(ks), n_pool)[:DEC_BATCH * n_pages]
    page_table = page_table.reshape(DEC_BATCH, n_pages).astype(jnp.int32)
    a0 = jax.random.uniform(next(ks), (N_REC, D_RNN), f32, 0.9, 0.999)
    s0 = a0 ** (1.0 / RG_C)
    lam = jnp.log(s0) - jnp.log1p(-s0)
    return {
        'x_prompt': nrm((BATCH, SEQ, D_MODEL), 1.0),
        'x_sample': nrm((DEC_BATCH, DEC_SEQ, D_MODEL), 1.0),
        'cache_k': nrm((N_ATTN, n_pool, PAGE_SIZE, N_KV_HEADS, HEAD_DIM), 1.0),
        'cache_v': nrm((N_ATTN, n_pool, PAGE_SIZE, N_KV_HEADS, HEAD_DIM), 1.0),
        'cache_kidx': nrm((N_ATTN, n_pool, PAGE_SIZE, IDX_DIM), 1.0),
        'state_h': nrm((N_REC, DEC_BATCH, D_RNN), 0.5),
        'state_conv': nrm((N_REC, DEC_BATCH, CONV_W - 1, D_RNN), 1.0),
        'page_table': page_table,
        'c_prompt': nrm((BATCH, D_MODEL), 1.0),
        'c_sample': nrm((DEC_BATCH, D_MODEL), 1.0),
        'ada_w': nrm((DEPTH, D_MODEL, 6 * D_MODEL), 0.5 * D_MODEL ** -0.5),
        'ada_b': nrm((DEPTH, 6 * D_MODEL), 0.02),
        'norm_mix_g': 1.0 + nrm((DEPTH, D_MODEL), 0.02),
        'norm_ffn_g': 1.0 + nrm((DEPTH, D_MODEL), 0.02),
        'norm_final_g': 1.0 + nrm((D_MODEL,), 0.02),
        'attn_w_in': nrm((N_ATTN, D_MODEL, ATTN_PROJ), D_MODEL ** -0.5),
        'attn_w_out': nrm((N_ATTN, N_HEADS * HEAD_DIM, D_MODEL), (N_HEADS * HEAD_DIM) ** -0.5),
        'rec_w_in': nrm((N_REC, D_MODEL, 2 * D_RNN), D_MODEL ** -0.5),
        'rec_conv_w': nrm((N_REC, CONV_W, D_RNN), CONV_W ** -0.5),
        'rec_conv_b': nrm((N_REC, D_RNN), 0.02),
        'rec_w_a': nrm((N_REC, RG_BLOCKS, RG_BLOCK_W, RG_BLOCK_W), RG_BLOCK_W ** -0.5),
        'rec_b_a': nrm((N_REC, D_RNN), 0.02),
        'rec_w_x': nrm((N_REC, RG_BLOCKS, RG_BLOCK_W, RG_BLOCK_W), RG_BLOCK_W ** -0.5),
        'rec_b_x': nrm((N_REC, D_RNN), 0.02),
        'rec_lambda': lam,
        'rec_w_out': nrm((N_REC, D_RNN, D_MODEL), D_RNN ** -0.5),
        'moe_w_group': nrm((DEPTH, D_MODEL, N_GROUPS), D_MODEL ** -0.5),
        'moe_b_group': nrm((DEPTH, N_GROUPS), 0.01),
        'moe_w_expert': nrm((DEPTH, D_MODEL, N_EXPERTS), D_MODEL ** -0.5),
        'moe_b_expert': nrm((DEPTH, N_EXPERTS), 0.01),
        'moe_w1': nrm((DEPTH, N_EXPERTS, D_MODEL, 2 * D_EXPERT), D_MODEL ** -0.5),
        'moe_w2': nrm((DEPTH, N_EXPERTS, D_EXPERT, D_MODEL), D_EXPERT ** -0.5),
    }

def reference(x_prompt, x_sample, cache_k, cache_v, cache_kidx, state_h, state_conv, page_table,
              c_prompt, c_sample, ada_w, ada_b, norm_mix_g, norm_ffn_g, norm_final_g,
              attn_w_in, attn_w_out, rec_w_in, rec_conv_w, rec_conv_b, rec_w_a, rec_b_a,
              rec_w_x, rec_b_x, rec_lambda, rec_w_out, moe_w_group, moe_b_group,
              moe_w_expert, moe_b_expert, moe_w1, moe_w2):
    xp, xs = x_prompt, x_sample
    pos_p = jnp.arange(xp.shape[1])
    pos_s = PAST_LEN + jnp.arange(xs.shape[1])
    k_p, v_p, ki_p, h_p, cv_p = [], [], [], [], []
    k_s, v_s, ki_s, h_s, cv_s = [], [], [], [], []
    for l in range(DEPTH):
        sh1p, sc1p, g1p, sh2p, sc2p, g2p = adaln(c_prompt, ada_w[l], ada_b[l])
        sh1s, sc1s, g1s, sh2s, sc2s, g2s = adaln(c_sample, ada_w[l], ada_b[l])
        hp = modulate(xp, norm_mix_g[l], sh1p, sc1p)
        hs = modulate(xs, norm_mix_g[l], sh1s, sc1s)
        if l % 2 == 0:
            a = l // 2
            q, k, v, qi, ki, wi = attn_project(hp, attn_w_in[a], pos_p)
            op = dsa_prompt(q, k, v, qi, ki, wi) @ attn_w_out[a]
            k_p.append(k)
            v_p.append(v)
            ki_p.append(ki)
            q, k, v, qi, ki, wi = attn_project(hs, attn_w_in[a], pos_s)
            os_ = dsa_sample(q, k, v, qi, ki, wi, cache_k[a], cache_v[a], cache_kidx[a],
                             page_table) @ attn_w_out[a]
            k_s.append(k)
            v_s.append(v)
            ki_s.append(ki)
        else:
            r = l // 2
            rw = (rec_w_in[r], rec_conv_w[r], rec_conv_b[r], rec_w_a[r], rec_b_a[r],
                  rec_w_x[r], rec_b_x[r], rec_lambda[r], rec_w_out[r])
            B = xp.shape[0]
            op, hT, buf = rglru_block(hp, jnp.zeros((B, CONV_W - 1, D_RNN), hp.dtype),
                                      jnp.zeros((B, D_RNN), hp.dtype), *rw)
            h_p.append(hT)
            cv_p.append(buf)
            os_, hT, buf = rglru_block(hs, state_conv[r], state_h[r], *rw)
            h_s.append(hT)
            cv_s.append(buf)
        xp = xp + g1p[:, None, :] * op
        xs = xs + g1s[:, None, :] * os_
        mw = (moe_w_group[l], moe_b_group[l], moe_w_expert[l], moe_b_expert[l], moe_w1[l], moe_w2[l])
        xp = xp + g2p[:, None, :] * hier_moe(modulate(xp, norm_ffn_g[l], sh2p, sc2p), *mw)
        xs = xs + g2s[:, None, :] * hier_moe(modulate(xs, norm_ffn_g[l], sh2s, sc2s), *mw)
    y_prompt = rmsnorm(xp, norm_final_g)
    y_sample = rmsnorm(xs, norm_final_g)
    return (y_prompt, y_sample,
            jnp.stack(k_p), jnp.stack(v_p), jnp.stack(ki_p), jnp.stack(h_p), jnp.stack(cv_p),
            jnp.stack(k_s), jnp.stack(v_s), jnp.stack(ki_s), jnp.stack(h_s), jnp.stack(cv_s))


_drawn_inputs = setup_inputs


def setup_inputs(seed=0):
    import zlib

    import numpy as np

    out = dict(_drawn_inputs(seed))
    spreads = {}
    factors = {'norm_final_g': 2.859,
     'rec_b_a': 8.0,
     'rec_b_x': 6.579,
     'moe_b_group': 8.0,
     'moe_b_expert': 8.0}
    for name, (base, spread) in spreads.items():
        noise = np.random.default_rng([zlib.crc32(name.encode()), seed]).standard_normal(out[name].shape)
        drawn = base * np.exp(spread * noise) if base else spread * noise
        out[name] = jnp.asarray(drawn.astype(out[name].dtype))
    for name, factor in factors.items():
        out[name] = (out[name] * factor).astype(out[name].dtype)
    return out
```

```python
import math
from contextlib import ExitStack

import concourse.bass as bass
import numpy as np
from concourse import mybir

F32 = mybir.dt.float32
BF16 = mybir.dt.bfloat16
I32 = mybir.dt.int32
ALU = mybir.AluOpType
ACT = mybir.ActivationFunctionType
AX = mybir.AxisListType

P = 128
D = 1024
KC = D // P
SEQ = 2048
NT = SEQ // P
NS = 8
PAST = 2048
PAGE = 128
NPAGE = PAST // PAGE
H, DH, NKV = 16, 64, 4
GQ = H // NKV
IH, IDIM = 8, 64
IDX_SCALE = float((IH * IDIM) ** -0.5)
TOPK = 256
ROT = DH // 4
HALF = ROT // 2
C_K, C_V, C_QI, C_KI, C_WI, C_END = 1024, 1280, 1536, 2048, 2112, 2120
EPS = 1e-6
CONV_W = 4
RG_C = 8.0
NE, NG, EPG = 32, 4, 8
FE = 256
BLK = 128
NTOK = SEQ + NS
NB = -(-(2 * NTOK) // BLK) + NE
MASKED = -1.0e30
TAKEN = -3.0e38
BIG = 1.0e30


class Semaphores:

    def __init__(self, nc, whole_run, pool_dma=()):
        self.nc, self.ctx, self.all = nc, ExitStack(), []
        self.whole_run, self.pool_dma = whole_run, pool_dma

    def __enter__(self):
        return self

    def __call__(self, name):
        held = self.whole_run if name.split("_", 1)[1] in self.pool_dma else self.ctx
        self.all.append(held.enter_context(self.nc.semaphore(name)))
        return self.all[-1]

    def __exit__(self, *failure):
        if failure[0] is None:
            for s in self.all:
                self.nc.sync.sem_clear(s)
            self.nc.all_engine_barrier()
        self.ctx.close()


class Chain:

    def __init__(self, eng, sem):
        self.eng, self.sem, self.base, self.n = eng, sem, 0, 0

    def __call__(self, ins):
        self.n += 1
        ins.then_inc(self.sem, 1)
        self.eng.wait_ge(self.sem, self.base + self.n)

    def enter(self, i, per):
        self.outer, self.per = self.base + self.n, per
        self.base, self.n = self.outer + i * per, 0

    def leave(self, turns):
        assert self.n == self.per, (self.n, self.per)
        self.base, self.n = self.outer + turns * self.per, 0


def two_by_two(eng, body):
    with eng.Fori(0, NT // 2) as j:
        body(j * 2, 0, P)
        body(j * 2 + 1, 1, P)
    body(NT, 0, NS)


def rows_of(prompt, sample, t, rows):
    return prompt[bass.ds(t * P, P)] if rows == P else sample[0:NS]


def phase_modulation(nc, T):
    with ExitStack() as ctx, Semaphores(nc, T["whole_run"]) as sems:
        def sb(name, shape, dt=F32):
            return ctx.enter_context(nc.sbuf_tensor("modulation_" + name, shape, dt))

        def sem(name):
            return sems("modulation_" + name)

        R = 1 + NS
        cond = sb("cond", [R, D])
        cond_tanh = sb("cond_tanh", [R, D])
        condT = sb("condT", [P, KC, R])
        bias = sb("bias", [R, 2, 6 * D])
        slab = sb("slab", [P, 4, KC, 512])
        res = sb("res", [R, 2, 512])
        ident = T["ident"]
        psT = ctx.enter_context(nc.psum_tensor("modulation_psT", [P, KC, R], F32))
        ps = ctx.enter_context(nc.psum_tensor("modulation_ps", [P, 2, 512], F32))
        cond_in, bias_in = sem("cond_in"), sem("bias_in")
        slab_in = [sem(f"slab_in{i}") for i in range(4)]
        tanh_done, silu_done, turned, condT_done, bias_done = (sem(n) for n in ("tanh", "silu", "turned", "condT", "biasd"))
        slab_used, summed, res_out0, res_out1 = (sem(n) for n in ("slab_used", "summed", "res_out0", "res_out1"))
        res_out = [res_out0, res_out1]
        ident_done = sem("ident")

        with nc.Block() as block:
            @block.sync
            def _(sp):
                sp.dma_start(cond[0:1, :], T["c_prompt"]).then_inc(cond_in, 16)
                sp.dma_start(cond[1:R, :], T["c_sample"]).then_inc(cond_in, 16)
                for l in range(2):
                    sp.dma_start(bias[:, l, :], T["ada_b"][l:l + 1, :].broadcast_to([R, 6 * D])).then_inc(bias_in, 16)
                for l in range(2):
                    w = T["ada_w"][l].rearrange("(k p) n -> p k n", p=P)
                    with sp.Fori(0, 3) as j:
                        for u in range(4):
                            sp.wait_ge(slab_used, l * 12 + j * 4 + u + 1)
                            sp.dma_start(slab[:, u], w[:, :, bass.ds((j * 4 + u) * 512, 512)]).then_inc(slab_in[u], 16)

            @block.gpsimd
            def _(pool):
                pool.memset(T["power"][:, 0:1], -0.5).then_inc(ident_done, 1)
                pool.memset(T["power"][:, 1:2], 0.5).then_inc(ident_done, 1)
                pool.memset(T["power"][:, 2:3], EPS).then_inc(ident_done, 1)
                pool.memset(ident[:, :], 0.0).then_inc(ident_done, 1)
                pool.wait_ge(ident_done, 4)
                pool.affine_select(out=ident[:, :], in_=ident[:, :], compare_op=ALU.not_equal, fill=1.0,
                                   base=0, pattern=[[-1, P]], channel_multiplier=1).then_inc(ident_done, 1)

            @block.scalar
            def _(act):
                act.wait_ge(cond_in, 32)
                act.activation(cond_tanh[:, :], cond[:, :], ACT.Tanh, scale=0.5).then_inc(tanh_done, 1)
                for l in range(2):
                    with act.Fori(0, 3) as j:
                        for u in range(4):
                            n = j * 4 + u
                            act.wait_ge(summed, 2 + l * 12 + n + 1)
                            act.dma_start(T["mods"][l, bass.ds(n, 1)].rearrange("a r d -> r a d"),
                                          res[:, u % 2:u % 2 + 1, :]).then_inc(res_out[u % 2], 16)
                act.wait_ge(res_out[0], 12 * 16)
                act.wait_ge(res_out[1], 12 * 16)

            @block.vector
            def _(dve):
                dve.sem_inc(summed, 2)
                dve.wait_ge(tanh_done, 1)
                dve.scalar_tensor_tensor(cond[:, :], cond_tanh[:, :], 1.0, cond[:, :], ALU.add, ALU.mult).then_inc(silu_done, 1)
                dve.wait_ge(turned, 1)
                dve.tensor_scalar(condT[:, :, :], psT[:, :, :], 0.5, None, ALU.mult).then_inc(condT_done, 1)
                dve.wait_ge(bias_in, 32)
                for chunk in (1, 4):
                    dve.tensor_scalar(bias[:, :, chunk * D:(chunk + 1) * D], bias[:, :, chunk * D:(chunk + 1) * D],
                                      1.0, None, ALU.add).then_inc(bias_done, 1)
                dve.wait_ge(bias_done, 2)
                for l in range(2):
                    with dve.Fori(0, 3) as j:
                        for u in range(4):
                            n = j * 4 + u
                            dve.wait_ge(slab_used, 4 + l * 12 + n + 1)
                            dve.wait_ge(res_out[u % 2], (l * 6 + j * 2 + u // 2) * 16)
                            dve.tensor_tensor(res[:, u % 2], ps[0:R, u % 2, :], bias[:, l, bass.ds(n * 512, 512)],
                                              ALU.add).then_inc(summed, 1)

            @block.tensor
            def _(pe):
                pe.sem_inc(slab_used, 4)
                pe.wait_ge(silu_done, 1)
                pe.wait_ge(ident_done, 5)
                for k in range(KC):
                    last = pe.transpose(psT[:, k, :], cond[:, k * P:(k + 1) * P], ident[0:R, 0:R])
                last.then_inc(turned, 1)
                pe.wait_ge(condT_done, 1)
                for l in range(2):
                    with pe.Fori(0, 3) as j:
                        for u in range(4):
                            pe.wait_ge(slab_in[u], (l * 3 + j + 1) * 16)
                            pe.wait_ge(summed, l * 12 + j * 4 + u + 1)
                            for k in range(KC):
                                last = pe.matmul(ps[0:R, u % 2, :], condT[:, k, :], slab[:, u, k, :], start=(k == 0), stop=(k == KC - 1))
                            last.then_inc(slab_used, 1)


def norm_rstd(pool, link, rs, ss, power):
    link(pool.tensor_tensor(rs, ss, power[:, 2:3], ALU.add))
    return pool.tensor_tensor(rs, rs, power[:, 0:1], ALU.pow)


def norm_modulate(dve, link, h, x, rs, gain, shift):
    link(dve.scalar_tensor_tensor(h, x, rs, gain, ALU.mult, ALU.mult))
    return dve.tensor_tensor(h, h, shift, ALU.add)


def load_modulation(eng, T, l, chunk, prompt_tile, sample_tile, sem):
    for half in range(2):
        cols = slice(half * 512, half * 512 + 512)
        eng.dma_start(prompt_tile[:, cols], T["mods"][l, chunk * 2 + half, 0:1, :].broadcast_to([P, 512])).then_inc(sem, 16)
        eng.dma_start(sample_tile[0:NS, cols], T["mods"][l, chunk * 2 + half, 1:1 + NS, :]).then_inc(sem, 16)


def phase_project(nc, T):
    with ExitStack() as ctx, Semaphores(nc, T["whole_run"], ("w_in", "out_done0", "out_done1")) as sems:
        def sb(name, shape, dt=F32):
            return ctx.enter_context(nc.sbuf_tensor("project_" + name, shape, dt))

        def sem(name):
            return sems("project_" + name)

        w = sb("w", [P, KC, C_END])
        gain = sb("gain", [P, 2, D])
        shift = sb("shift", [P, 2, D])
        x = sb("x", [P, 2, D])
        h = sb("h", [P, 2, D])
        hT = sb("hT", [P, 2, KC, P])
        proj = sb("proj", [P, 2, C_END])
        rope = sb("rope", [P, NT + 1, 2 * ROT])
        rot = sb("rot", [P, 29, ROT])
        ss = sb("ss", [P, 2])
        rs = sb("rs", [P, 2])
        ident, KT, kiT, V1 = T["ident"], T["KT"], T["kiT"], T["V1"]
        psT = ctx.enter_context(nc.psum_tensor("project_psT", [P, KC, P], F32))
        pj = ctx.enter_context(nc.psum_tensor("project_pj", [P, 4, 512], F32))
        psK = ctx.enter_context(nc.psum_tensor("project_psK", [P, 4, P], F32))

        w_in, mod_in, zeroed = sem("w_in"), sem("mod_in"), sem("zeroed")
        x_in = [sem("x_in0"), sem("x_in1")]
        out_done = [sem("out_done0"), sem("out_done1")]
        squared, x_used, h_turned, hT_ready, proj_done, evac, roped, k_turned, kT_copied, v_copied, vec = (
            sem(n) for n in ("squared", "x_used", "h_turned", "hT_ready", "proj_done", "evac", "roped",
                             "k_turned", "kT_copied", "v_copied", "vec"))
        rstd_done, pool_chain = sem("rstd_done"), sem("pool_chain")
        CH = [(0, 512), (512, 1024), (1024, 1536), (1536, 2048), (2048, C_END)]
        NCH = len(CH)

        with nc.Block() as block:
            @block.sync
            def _(sp):
                load_modulation(sp, T, 0, 1, gain[:, 0], gain[:, 1], mod_in)
                load_modulation(sp, T, 0, 0, shift[:, 0], shift[:, 1], mod_in)
                sp.dma_start(rope[:, 0:NT], T["rope"][0:SEQ].rearrange("(t p) r -> p t r", p=P)).then_inc(mod_in, 16)
                sp.dma_start(rope[0:NS, NT], T["rope"][SEQ:SEQ + NS]).then_inc(mod_in, 16)
                sp.dma_start(h[:, 0, :], T["norm_mix_g"][0:1, :].broadcast_to([P, D])).then_inc(mod_in, 16)

                def body(t, b, rows):
                    sp.wait_ge(x_used, t + 1)
                    sp.dma_start(x[0:rows, b], rows_of(T["x_prompt"], T["x_sample"], t, rows)).then_inc(x_in[b], 16)
                two_by_two(sp, body)

            @block.gpsimd
            def _(pool):
                for k in range(KC):
                    pool.dma_start(w[:, k, :], T["attn_w_in"].rearrange("(k p) n -> p k n", p=P)[:, k, :]).then_inc(w_in, 16)
                pool.memset(V1[:, :, :, DH:P], 1.0).then_inc(v_copied, 1)

                link = Chain(pool, pool_chain)

                def body(t, b, rows):
                    pool.wait_ge(w_in, 16 * KC)
                    pool.wait_ge(squared, t + 1)
                    norm_rstd(pool, link, rs[0:rows, b:b + 1], ss[0:rows, b:b + 1],
                              T["power"][0:rows]).then_inc(rstd_done, 1)

                def store(t, b, rows):
                    pool.wait_ge(roped, t + 1)
                    pool.wait_ge(w_in, 16 * KC)
                    if rows == P:
                        pool.tensor_copy(V1[:, bass.ds(t, 1), :, 0:DH],
                                         proj[:, b:b + 1, C_V:C_QI].rearrange("p a (n d) -> p a n d", d=DH)).then_inc(v_copied, 1)
                    k_out, v_out, ki_out, q_out = (
                        (T["k_prompt"][bass.ds(t * P, P)], T["v_prompt"][bass.ds(t * P, P)],
                         T["kidx_prompt"][bass.ds(t * P, P)], T["qs"][bass.ds(t * P, P)]) if rows == P else
                        (T["k_sample"][:, :], T["v_sample"][:, :], T["kidx_sample"][:, :], T["qs"][SEQ:SEQ + NS]))
                    for dst, c0, c1 in ((k_out, C_K, C_V), (v_out, C_V, C_QI), (ki_out, C_KI, C_WI),
                                        (q_out[:, 0:C_K], 0, C_K), (q_out[:, C_K:C_K + 512], C_QI, C_KI),
                                        (q_out[:, C_K + 512:C_K + 520], C_WI, C_END)):
                        pool.dma_start(dst, proj[0:rows, b, c0:c1]).then_inc(out_done[b], 16)
                with pool.Fori(0, NT // 2) as j:
                    link.enter(j, 2)
                    body(j * 2, 0, P)
                    body(j * 2 + 1, 1, P)
                    store(j * 2, 0, P)
                    store(j * 2 + 1, 1, P)
                    link.leave(NT // 2)
                body(NT, 0, NS)
                store(NT, 0, NS)
                pool.wait_ge(v_copied, 1 + NT)
                for b in range(2):
                    pool.wait_ge(out_done[b], 16 * 6 * (NT // 2 + 1 - b))

            @block.scalar
            def _(act):
                def body(t, b, rows):
                    act.wait_ge(x_in[b], (t - b) * 8 + 16)
                    act.wait_ge(proj_done, t * NCH + NCH)
                    act.activation(hT[0:rows, b].rearrange("p k n -> p (k n)"), x[0:rows, b], ACT.Square, scale=D ** -0.5,
                                   accum_out=ss[0:rows, b:b + 1]).then_inc(squared, 1)
                    act.wait_ge(h_turned, 2 + t + 1)
                    act.wait_ge(squared, t + 1)
                    act.activation(hT[:, b, :, 0:rows], psT[:, :, 0:rows], ACT.Copy).then_inc(hT_ready, 1)
                    for c, (c0, c1) in enumerate(CH):
                        act.wait_ge(proj_done, 2 * NCH + t * NCH + c + 1)
                        if c == 0:
                            act.wait_ge(out_done[b], (t - b) * 48)
                            act.wait_ge(k_turned, t + 1)
                            act.wait_ge(v_copied, t)
                        bank = c % 4
                        act.activation(proj[0:rows, b, c0:c1], pj[0:rows, bank, 0:c1 - c0], ACT.Copy).then_inc(evac, 1)
                    if rows == P:
                        act.wait_ge(k_turned, 2 + t + 1)
                        act.activation(KT[:, :, bass.ds(t * P, P)], psK[:, 0:2, :], ACT.Copy).then_inc(kT_copied, 1)
                        act.wait_ge(zeroed, 2)
                        for half in range(2):
                            act.activation(kiT[half * DH:(half + 1) * DH, half, bass.ds(t * P, P)], psK[0:DH, 2, :],
                                           ACT.Copy).then_inc(kT_copied, 1)
                act.sem_inc(evac, 4)
                two_by_two(act, body)

            @block.vector
            def _(dve):
                link = Chain(dve, vec)
                dve.sem_inc(x_used, 2)
                dve.memset(kiT[DH:P, 0, :], 0.0).then_inc(zeroed, 1)
                dve.memset(kiT[0:DH, 1, :], 0.0).then_inc(zeroed, 1)
                dve.wait_ge(mod_in, 16 * 11)
                for b in range(2):
                    link(dve.tensor_tensor(gain[:, b], gain[:, b], h[:, 0], ALU.mult)) if b == 0 else link(
                        dve.tensor_tensor(gain[0:NS, b], gain[0:NS, b], h[0:NS, 0], ALU.mult))

                def normed(t, b, rows):
                    s = 0 if rows == P else 1
                    dve.wait_ge(rstd_done, t + 1)
                    dve.wait_ge(h_turned, 2 + t - 1)
                    norm_modulate(dve, link, h[0:rows, b], x[0:rows, b], rs[0:rows, b:b + 1],
                                  gain[0:rows, s], shift[0:rows, s]).then_inc(x_used, 1)

                def body(t, b, rows):
                    normed(t, b, rows)
                    dve.wait_ge(evac, 4 + t * NCH + NCH)
                    for c0, nh, r0 in ((0, H + NKV, 0), (C_QI, IH + 1, H + NKV)):
                        head = proj[0:rows, b, c0:c0 + nh * DH].rearrange("p (h d) -> p h d", d=DH)
                        tmp = rot[0:rows, r0:r0 + nh, :]

                        def table(a):
                            v = rope[0:rows, bass.ds(t, 1), a:a + HALF]
                            return v.broadcast_to([rows, nh, HALF])
                        dve.tensor_tensor(tmp[:, :, 0:HALF], head[:, :, HALF:ROT], table(2 * HALF), ALU.mult).then_inc(vec, 1)
                        dve.tensor_tensor(tmp[:, :, HALF:ROT], head[:, :, 0:HALF], table(3 * HALF), ALU.mult).then_inc(vec, 1)
                        link.n += 2
                        dve.wait_ge(vec, link.base + link.n)
                        link(dve.tensor_tensor(head[:, :, 0:HALF], head[:, :, 0:HALF], table(0), ALU.mult))
                        link(dve.tensor_tensor(head[:, :, HALF:ROT], head[:, :, HALF:ROT], table(HALF), ALU.mult))
                        last = dve.tensor_tensor(head[:, :, 0:ROT], head[:, :, 0:ROT], tmp, ALU.add)
                        if r0 == 0:
                            link(last)
                    last.then_inc(roped, 1)
                with dve.Fori(0, NT // 2) as j:
                    link.enter(j, 2 * (1 + 9))
                    body(j * 2, 0, P)
                    body(j * 2 + 1, 1, P)
                    link.leave(NT // 2)
                body(NT, 0, NS)

            @block.tensor
            def _(pe):
                pe.sem_inc(proj_done, 2 * NCH)
                pe.sem_inc(k_turned, 2)
                pe.sem_inc(h_turned, 2)
                pe.wait_ge(w_in, 16 * KC)

                def body(t, b, rows):
                    pe.wait_ge(x_used, 2 + t + 1)
                    pe.wait_ge(hT_ready, t)
                    for k in range(KC):
                        last = pe.transpose(psT[:, k, 0:rows], h[0:rows, b, k * P:(k + 1) * P], ident[0:rows, 0:rows])
                    last.then_inc(h_turned, 1)
                    pe.wait_ge(hT_ready, t + 1)
                    for c, (c0, c1) in enumerate(CH):
                        bank = c % 4
                        pe.wait_ge(evac, 4 + t * NCH if c < 4 else 4 + t * NCH + 1)
                        for k in range(KC):
                            last = pe.matmul(pj[0:rows, bank, 0:c1 - c0], hT[:, b, k, 0:rows], w[:, k, c0:c1],
                                             start=(k == 0), stop=(k == KC - 1))
                        last.then_inc(proj_done, 1)
                    if rows == P:
                        pe.wait_ge(roped, t + 1)
                        pe.wait_ge(kT_copied, 3 * t)
                        for n in range(NKV // 2):
                            pe.transpose(psK[:, n, :], proj[:, b, C_K + n * P:C_K + (n + 1) * P], ident[:, :])
                        pe.transpose(psK[0:DH, 2, :], proj[:, b, C_KI:C_WI], ident[:, :]).then_inc(k_turned, 1)
                two_by_two(pe, body)


GROUP = 4
NGRP = NT // GROUP


def cum(per, pos):
    g, i = pos
    return sum(GROUP * p for p in per[:g]) + i * per[g]


def following(pos):
    g, i = pos
    return (g, i + 1) if not isinstance(i, int) or i + 1 < GROUP else (g + 1, 0)


def over_groups(eng, body):
    for g in range(NGRP):
        with eng.Fori(0, GROUP - 1) as i:
            body((g, i))
        body((g, GROUP - 1))


def phase_attend(nc, T):
    with ExitStack() as ctx, Semaphores(nc, T["whole_run"], ("y_out",)) as sems:
        def sb(name, shape, dt=F32):
            return ctx.enter_context(nc.sbuf_tensor("attend_" + name, shape, dt))

        def sem(name):
            return sems("attend_" + name)

        ident, KT, kiT, V1 = T["ident"], T["KT"], T["kiT"], T["V1"]
        KTb = sb("KTb", [P, NKV // 2, SEQ], BF16)
        w_out = sb("w_out", [P, KC, D])
        gate = sb("gate", [P, D])
        identb4 = sb("identb4", [P, GQ, P], BF16)
        onesb = sb("onesb", [P, P], BF16)
        causal = sb("causal", [P, 7 * P])
        q_rows = sb("q_rows", [P, D])
        qi_rows = sb("qi_rows", [P, 520])
        wi = sb("wi", [P, IH])
        qT = sb("qT", [P, H, P])
        qTb = sb("qTb", [P, H, P], BF16)
        qiT = sb("qiT", [P, IH // 2, P])
        score = sb("score", [P, SEQ])
        relu = sb("relu", [P, 4, 512])
        top8 = sb("top8", [P, 8])
        hide = sb("hide", [P, SEQ], BF16)
        mx = sb("mx", [P, H, 2])
        negmax = sb("negmax", [P, H])
        diag = sb("diag", [P, H, P], BF16)
        PT = sb("PT", [P, 4, 512])
        oT = sb("oT", [P, KC, P])
        total = sb("total", [P, KC, P])
        x = sb("x", [P, D])
        y = sb("y", [P, D])
        big = ctx.enter_context(nc.psum_tensor("attend_big", [P, 4, 512], F32))
        dots = ctx.enter_context(nc.psum_tensor("attend_dots", [P, 2, 512], F32))
        po = ctx.enter_context(nc.psum_tensor("attend_po", [P, 2, 512], F32))

        (const_in, q_in, qi_in, x_in, q_turned, qT_ready, qi_turned, qiT_ready, unit_filled, maxed, negmax_done,
         diag_done, dotted, relud, summed, scored, hidden, st_filled, exped, pv_done, o_copied, o_normed,
         projected, y_copied, y_done, y_out, consts, spare) = (sem(n) for n in (
             "const_in", "q_in", "qi_in", "x_in", "q_turned", "qT_ready", "qi_turned", "qiT_ready", "unit_filled",
             "maxed", "negmax_done", "diag_done", "dotted", "relud", "summed", "scored", "hidden", "st_filled",
             "exped", "pv_done", "o_copied", "o_normed", "projected", "y_copied", "y_done",
             "y_out", "consts", "spare"))
        L = [512 * (g + 1) for g in range(NGRP)]
        U = [H * (1 if l <= 1024 else 2) for l in L]
        I = [IH * l // 512 for l in L]
        S = [NKV * l // P for l in L]

        def tile(pos):
            return cum([1] * NGRP, pos)

        with nc.Block() as block:
            @block.sync
            def _(sp):
                for k in range(KC):
                    sp.dma_start(w_out[:, k, :], T["attn_w_out"][k * P:(k + 1) * P, :]).then_inc(const_in, 16)
                for half in range(2):
                    sp.dma_start(gate[:, half * 512:half * 512 + 512],
                                 T["mods"][0, 4 + half, 0:1, :].broadcast_to([P, 512])).then_inc(const_in, 16)
                sp.dma_start(qi_rows[:, :], T["qs"][0:P, D:D + 520]).then_inc(qi_in, 16)

                def body(pos):
                    t = tile(pos)
                    sp.wait_ge(q_turned, t)
                    sp.dma_start(q_rows[:, :], T["qs"][bass.ds(t * P, P), 0:D]).then_inc(q_in, 16)
                    sp.wait_ge(y_done, t)
                    sp.dma_start(x[:, :], T["x_prompt"][bass.ds(t * P, P), :]).then_inc(x_in, 16)
                    if following(pos)[0] < NGRP:
                        sp.wait_ge(scored, t + 1)
                        sp.wait_ge(qi_turned, t + 1)
                        sp.dma_start(qi_rows[:, :], T["qs"][bass.ds(t * P + P, P), D:D + 520]).then_inc(qi_in, 16)
                over_groups(sp, body)

            @block.gpsimd
            def _(pool):
                pool.memset(onesb[:, :], 1.0).then_inc(consts, 1)
                pool.memset(causal[:, :], 0.0).then_inc(consts, 1)
                pool.wait_ge(consts, 2)
                pool.affine_select(out=causal[:, :], in_=causal[:, :], compare_op=ALU.is_ge, fill=MASKED,
                                   base=3 * P, pattern=[[-1, 7 * P]], channel_multiplier=1).then_inc(consts, 1)
                for n in range(GQ):
                    pool.tensor_copy(identb4[:, n, :], ident[:, :]).then_inc(consts, 1)
                for n in range(NKV // 2):
                    pool.tensor_copy(KTb[:, n, :], KT[:, n, :]).then_inc(consts, 1)
                pool.memset(qT[:, :, :], 0.0).then_inc(consts, 1)
                pool.memset(qTb[:, :, :], 0.0).then_inc(consts, 1)

                def body(pos):
                    t = tile(pos)
                    pool.wait_ge(negmax_done, t + 1)
                    pool.tensor_tensor(diag[:, :, :], identb4[:, 0:1, :].broadcast_to([P, H, P]),
                                       negmax[:, :].rearrange("p (h a) -> p h a", a=1).broadcast_to([P, H, P]), ALU.mult).then_inc(diag_done, 1)
                    pool.wait_ge(y_copied, 2 * (t + 1))
                    pool.tensor_tensor(y[:, :], y[:, :], gate[:, :], ALU.mult)
                    pool.drain()
                    pool.wait_ge(x_in, 16 * (t + 1))
                    pool.tensor_tensor(y[:, :], y[:, :], x[:, :], ALU.add).then_inc(y_done, 1)
                    pool.wait_ge(y_done, t + 1)
                    pool.sem_inc(spare, 1)
                    pool.dma_start(T["xa"][bass.ds(t * P, P), :], y[:, :]).then_inc(y_out, 16)
                pool.wait_ge(const_in, 16 * (KC + 2))
                over_groups(pool, body)
                pool.wait_ge(y_out, 16 * NT)

            @block.scalar
            def _(act):
                act.sem_inc(relud, 2)
                act.sem_inc(exped, 4)

                def index(pos):
                    t = tile(pos)
                    act.wait_ge(qi_turned, t + 1)
                    act.activation(qiT[:, :, :], dots[:, 0, :].rearrange("p (k q) -> p k q", q=P), ACT.Copy).then_inc(qiT_ready, 1)
                    for k in range(I[pos[0]]):
                        n = cum(I, pos) + k
                        act.wait_ge(dotted, n + 1)
                        act.wait_ge(summed, n + 1)
                        act.activation(relu[:, k % 4, :], dots[:, k % 2, :], ACT.Relu).then_inc(relud, 1)

                def body(pos):
                    t = tile(pos)
                    g = pos[0]
                    act.wait_ge(q_turned, t + 1)
                    turned = big[:, 0:2, :].rearrange("p a (k q) -> p (a k) q", q=P)
                    act.wait_ge(consts, 7 + GQ)
                    for n in range(NKV):
                        at = slice((n % 2) * DH, (n % 2 + 1) * DH)
                        for half in range(2):
                            for dst in (qT, qTb):
                                act.activation(dst[at, n * GQ + half:(n + 1) * GQ:2, :],
                                               turned[half * DH:(half + 1) * DH, n * GQ // 2:(n + 1) * GQ // 2], ACT.Copy,
                                               scale=DH ** -0.5).then_inc(qT_ready, 1)
                    if following(pos)[0] < NGRP:
                        index(following(pos))

                    def copy_out(n):
                        act.wait_ge(pv_done, 4 + cum(S, pos) + (n + 1) * S[g] // NKV)
                        if n == 0:
                            act.wait_ge(projected, 2 * t)
                        heads = po[:, n % 2, :].rearrange("p (h q) -> p h q", q=P)
                        for half in range(2):
                            for dst, a in ((oT, 0), (total, DH)):
                                act.activation(dst[half * DH:(half + 1) * DH, n * GQ // 2:(n + 1) * GQ // 2, :],
                                               heads[a:a + DH, half:GQ:2, :], ACT.Copy).then_inc(o_copied, 1)
                    per = S[g] // NKV
                    for k in range(S[g]):
                        act.wait_ge(st_filled, cum(S, pos) + k + 1)
                        act.wait_ge(pv_done, cum(S, pos) + k + 1)
                        act.activation(PT[:, k % 4, :], big[:, k % 4, :], ACT.Exp).then_inc(exped, 1)
                        if k % per == 2 and k >= per:
                            copy_out(k // per - 1)
                    copy_out(NKV - 1)
                    for half in range(2):
                        act.wait_ge(projected, 2 * t + half + 1)
                        if half == 0:
                            act.wait_ge(y_out, 16 * t)
                        act.activation(y[:, half * 512:half * 512 + 512], big[:, 2 + half, :], ACT.Copy).then_inc(y_copied, 1)
                index((0, 0))
                over_groups(act, body)

            @block.vector
            def _(dve):
                dve.sem_inc(maxed, 2)
                dve.sem_inc(summed, 4)
                dve.wait_ge(consts, 7 + GQ)

                def normalise(pos):
                    dve.wait_ge(o_copied, 4 * NKV * (tile(pos) + 1))
                    dve.reciprocal(total[:, :, :], total[:, :, :])
                    dve.drain()
                    dve.tensor_tensor(oT[:, :, :], oT[:, :, :], total[:, :, :], ALU.mult).then_inc(o_normed, 1)

                def index(pos, before):
                    g, t, n0 = pos[0], tile(pos), cum(I, pos)
                    w = L[g]
                    dve.wait_ge(qi_in, 16 * (t + 1))
                    dve.tensor_scalar(wi[:, :], qi_rows[:, 512:520], IDX_SCALE, None, ALU.mult)
                    dve.drain()
                    for k in range(I[g]):
                        h, b = divmod(k, w // 512)
                        dst = score[:, b * 512:(b + 1) * 512]
                        dve.wait_ge(relud, 2 + n0 + k + 1)
                        if h == 0:
                            dve.tensor_scalar(dst, relu[:, k % 4, :], wi[:, 0:1], None, ALU.mult).then_inc(summed, 1)
                        else:
                            dve.wait_ge(summed, 4 + n0 + k - w // 512 + 1)
                            dve.scalar_tensor_tensor(dst, relu[:, k % 4, :], wi[:, h:h + 1], dst, ALU.mult, ALU.add).then_inc(summed, 1)
                    dve.drain()
                    unseen = causal[:, bass.ds(384 - pos[1] * P, 512)]
                    dve.tensor_tensor(score[:, w - 512:w], score[:, w - 512:w], unseen, ALU.add).then_inc(scored, 1)
                    with dve.Fori(0, TOPK // 8):
                        dve.drain()
                        dve.max(top8[:, :], score[:, 0:w])
                        dve.drain()
                        dve.match_replace(score[:, 0:w], top8[:, :], score[:, 0:w], TAKEN)
                    if before is not None:
                        normalise(before)
                    dve.drain()
                    dve.wait_ge(pv_done, 4 + n_before(pos))
                    dve.tensor_scalar(hide[:, 0:w], score[:, 0:w], TAKEN / 2, -BIG, ALU.is_gt, ALU.mult)
                    dve.drain()
                    dve.tensor_tensor(hide[:, w - 512:w], hide[:, w - 512:w], unseen, ALU.add).then_inc(hidden, 1)

                def n_before(pos):
                    return cum(S, pos)

                def body(pos):
                    g, t = pos[0], tile(pos)
                    nu = U[g] // H
                    for k in range(U[g]):
                        h, u = divmod(k, nu)
                        wide = min(1024, L[g] - 1024 * u)
                        dve.wait_ge(unit_filled, cum(U, pos) + k + 1)
                        dve.tensor_reduce(mx[:, h, u:u + 1], big[:, 2 * (k % 2):2 * (k % 2) + wide // 512, :], AX.XY, ALU.max).then_inc(maxed, 1)
                    dve.drain()
                    dve.tensor_reduce(negmax[:, :], mx[:, :, 0:nu], AX.X, ALU.max, negate=True).then_inc(negmax_done, 1)
                    if following(pos)[0] < NGRP:
                        index(following(pos), pos)
                    else:
                        normalise(pos)
                index((0, 0), None)
                over_groups(dve, body)

            @block.tensor
            def _(pe):
                pe.sem_inc(pv_done, 4)
                pe.wait_ge(consts, 7 + GQ)
                pe.wait_ge(const_in, 16 * (KC + 2))

                def index(pos):
                    g, t, n0 = pos[0], tile(pos), cum(I, pos)
                    nb = L[g] // 512
                    pe.wait_ge(qi_in, 16 * (t + 1))
                    pe.wait_ge(relud, 2 + n0)
                    for k in range(IH // 2):
                        last = pe.transpose(dots[:, 0, k * P:(k + 1) * P], qi_rows[:, k * P:(k + 1) * P], ident[:, :])
                    last.then_inc(qi_turned, 1)
                    pe.wait_ge(qiT_ready, t + 1)
                    for k in range(I[g]):
                        h, b = divmod(k, nb)
                        pe.wait_ge(relud, n0 + k + 1)
                        pe.matmul(dots[:, k % 2, :], qiT[:, h // 2, :], kiT[:, h % 2, b * 512:(b + 1) * 512], start=True, stop=True).then_inc(dotted, 1)

                def body(pos):
                    g, t = pos[0], tile(pos)
                    pe.wait_ge(q_in, 16 * (t + 1))
                    pe.wait_ge(y_copied, 2 * t)
                    turned = big[:, 0:2, :].rearrange("p a (k q) -> p (a k) q", q=P)
                    for k in range(KC):
                        last = pe.transpose(turned[:, k, :], q_rows[:, k * P:(k + 1) * P], ident[:, :])
                    last.then_inc(q_turned, 1)
                    pe.wait_ge(qT_ready, 4 * NKV * (t + 1))
                    pe.wait_ge(hidden, t + 1)
                    nu = U[g] // H
                    for k in range(U[g]):
                        h, u = divmod(k, nu)
                        wide = min(1024, L[g] - 1024 * u)
                        pe.wait_ge(maxed, cum(U, pos) + k + 1)
                        for b in range(wide // 512):
                            keys = slice(u * 1024 + b * 512, u * 1024 + b * 512 + 512)
                            bank = big[:, 2 * (k % 2) + b, :]
                            pe.matmul(bank, identb4[:, 0, :], hide[:, keys], start=True, stop=False)
                            last = pe.matmul(bank, qTb[:, h, :], KTb[:, h // GQ // 2, keys], start=False, stop=True)
                        last.then_inc(unit_filled, 1)
                    if following(pos)[0] < NGRP:
                        index(following(pos))
                    per = S[g] // NKV
                    pe.wait_ge(diag_done, t + 1)
                    pe.wait_ge(maxed, 2 + cum(U, pos) + U[g])

                    def transposed(k):
                        n, b = divmod(k, per)
                        pe.wait_ge(exped, cum(S, pos) + k + 1)
                        bank = big[:, k % 4, :]
                        keys = slice(b * P, (b + 1) * P)
                        pe.matmul(bank, hide[:, keys], identb4[:, :, :].rearrange("p a q -> p (a q)"), start=True, stop=False)
                        pe.matmul(bank, onesb[:, :], diag[:, n * GQ:(n + 1) * GQ, :].rearrange("p a q -> p (a q)"), start=False, stop=False)
                        pe.matmul(bank, KT[:, n // 2, keys], qT[:, n * GQ:(n + 1) * GQ, :].rearrange("p a q -> p (a q)"),
                                  start=False, stop=True).then_inc(st_filled, 1)

                    def with_values(k):
                        n, b = divmod(k, per)
                        pe.wait_ge(exped, 4 + cum(S, pos) + k + 1)
                        if b == 0:
                            pe.wait_ge(o_copied, 4 * (NKV * t + max(n - 1, 0)))
                        pe.matmul(po[:, n % 2, :], V1[:, b, n, :], PT[:, k % 4, :], start=(b == 0), stop=(b == per - 1)).then_inc(pv_done, 1)
                    for k in range(S[g] + 2):
                        if k < S[g]:
                            transposed(k)
                        if k >= 2:
                            with_values(k - 2)
                    pe.wait_ge(o_normed, t + 1)
                    for half in range(2):
                        for k in range(KC):
                            last = pe.matmul(big[:, 2 + half, :], oT[:, k, :], w_out[:, k, half * 512:half * 512 + 512],
                                             start=(k == 0), stop=(k == KC - 1))
                        last.then_inc(projected, 1)
                index((0, 0))
                over_groups(pe, body)


SLOTS = NPAGE + 1
NKEY = SLOTS * P


def load_pages(eng, table, cache, b, dst, sem):
    for j in range(NPAGE):
        page = eng.value_load(table[0:1, bass.ds(b * NPAGE + j, 1)], min_val=0, max_val=cache.shape[0] - 1)
        eng.dma_start(dst[:, j, :], cache[bass.ds(page, 1)].rearrange("a t c -> (a t) c")).then_inc(sem, 16)


def phase_sample_index(nc, T):
    with ExitStack() as ctx, Semaphores(nc, T["whole_run"]) as sems:
        def sb(name, shape, dt=F32):
            return ctx.enter_context(nc.sbuf_tensor("index_" + name, shape, dt))

        def sem(name):
            return sems("index_" + name)

        ident = T["ident"]
        pairs = (SLOTS + 1) // 2
        table = sb("table", [1, NS * NPAGE], I32)
        qi_rows = sb("qi_rows", [NS * IH, IDIM])
        weights = sb("weights", [P, NS, IH])
        kis = sb("kis", [P, 2, 2 * pairs, IDIM])
        kiT = sb("kiT", [P, pairs, P])
        qi2 = sb("qi2", [P, NS, 2 * IH])
        weighed = sb("weighed", [P, SLOTS, IH])
        score = sb("score", [P, NS, SLOTS])
        unseen = sb("unseen", [P, SLOTS])
        turned = sb("turned", [P, 2, P])
        rows = sb("rows", [NS, NKEY])
        top8 = sb("top8", [NS, 8])
        ps_kiT = ctx.enter_context(nc.psum_tensor("index_ps_kiT", [P, 3, 512], F32))
        ps_dot = ctx.enter_context(nc.psum_tensor("index_ps_dot", [P, 512], F32))
        ps_misc = ctx.enter_context(nc.psum_tensor("index_ps_misc", [P, 4, P], F32))
        (table_in, in_, zeroed, kis_used, spare, kiT_ready, dotted, summed, q_turned, q_ready, masked, sc_turned,
         sc_copied, sc_out, rows_in, hidden, hide_out) = (sem(n) for n in (
             "table_in", "in", "zeroed", "kis_used", "spare", "kiT_ready", "dotted", "summed", "q_turned",
             "q_ready", "masked", "sc_turned", "sc_copied", "sc_out", "rows_in", "hidden", "hide_out"))
        kis_in = [sem("kis_in0"), sem("kis_in1")]
        first = 7 * SLOTS

        with nc.Block() as block:
            @block.sync
            def _(sp):
                sp.dma_start(table[0:1, :], T["page_table"].rearrange("b (o j) -> o b j", o=1)).then_inc(table_in, 16)
                for b in range(NS):
                    sp.dma_start(qi_rows[b * IH:(b + 1) * IH, :],
                                 T["qs"][SEQ + b:SEQ + b + 1, D:D + 512].rearrange("a (h d) -> (a h) d", d=IDIM)).then_inc(in_, 16)
                sp.dma_start(weights[:, :, :], T["qs"][SEQ:SEQ + NS, D + 512:D + 520].rearrange("b (o h) -> o b h", o=1)
                             .broadcast_to([P, NS, IH])).then_inc(in_, 16)
                sp.wait_ge(table_in, 16)
                sp.wait_ge(zeroed, 3)
                with sp.Fori(0, NS // 2) as j:
                    for u in range(2):
                        b = j * 2 + u
                        sp.wait_ge(kis_used, b + 1)
                        sp.sem_inc(spare, 1)
                        load_pages(sp, table, T["cache_kidx"], b, kis[:, u], kis_in[u])
                        sp.dma_start(kis[0:1, u, NPAGE, :], T["kidx_sample"][bass.ds(b, 1), :]).then_inc(kis_in[u], 16)
                for k, (a, z) in enumerate(((0, first), (first, NS * SLOTS))):
                    sp.wait_ge(sc_copied, k + 1)
                    sp.dma_start(T["scores_s"][a:z, :], turned[0:z - a, k, :]).then_inc(sc_out, 16)
                sp.wait_ge(sc_out, 32)
                sp.dma_start(rows[:, :], T["scores_s"].rearrange("(b j) k -> b (j k)", b=NS)).then_inc(rows_in, 16)
                sp.wait_ge(hidden, 1)
                sp.dma_start(T["hide_s"], rows[:, :]).then_inc(hide_out, 16)
                sp.wait_ge(hide_out, 16)

            @block.gpsimd
            def _(pool):
                pool.memset(unseen[:, :], 0.0).then_inc(masked, 1)
                pool.wait_ge(masked, 1)
                pool.affine_select(out=unseen[:, :], in_=unseen[:, :], compare_op=ALU.is_ge, fill=MASKED,
                                   base=PAST, pattern=[[-P, SLOTS]], channel_multiplier=-1).then_inc(masked, 1)

            @block.scalar
            def _(act):
                with act.Fori(0, NS) as b:
                    act.wait_ge(kis_used, 2 + b + 1)
                    act.activation(kiT[:, 0:8, :], ps_kiT[:, 0:2, :].rearrange("p a (k q) -> p (a k) q", q=P), ACT.Copy).then_inc(kiT_ready, 1)
                    act.activation(kiT[:, 8, :], ps_kiT[:, 2, 0:P], ACT.Copy).then_inc(kiT_ready, 1)

            @block.vector
            def _(dve):
                dve.memset(kis[:, :, NPAGE:, :], 0.0).then_inc(zeroed, 1)
                dve.memset(qi2[0:DH, :, IH:], 0.0).then_inc(zeroed, 1)
                dve.memset(qi2[DH:P, :, 0:IH], 0.0).then_inc(zeroed, 1)
                dve.wait_ge(in_, 16 * (NS + 1))
                dve.tensor_scalar(weights[:, :, :], weights[:, :, :], IDX_SCALE, None, ALU.mult)
                dve.wait_ge(q_turned, 1)
                for half in range(2):
                    dve.tensor_copy(qi2[half * DH:(half + 1) * DH, :, half * IH:(half + 1) * IH],
                                    ps_misc[0:IDIM, 0, 0:NS * IH].rearrange("p (b h) -> p b h", h=IH)).then_inc(q_ready, 1)
                dve.drain()
                with dve.Fori(0, NS) as b:
                    dve.wait_ge(dotted, b + 1)
                    dve.scalar_tensor_tensor(weighed[:, :, :], ps_dot[:, 0:SLOTS * IH].rearrange("p (j h) -> p j h", h=IH), 0.0,
                                             weights[:, bass.ds(b, 1), :].broadcast_to([P, SLOTS, IH]), ALU.max, ALU.mult).then_inc(summed, 1)
                    dve.drain()
                    dve.tensor_reduce(score[:, bass.ds(b, 1), :].rearrange("p a j -> p (a j)"), weighed[:, :, :], AX.X, ALU.add)
                    dve.drain()
                dve.wait_ge(masked, 2)
                dve.tensor_tensor(score[:, :, :], score[:, :, :], unseen[:, :].rearrange("p (a j) -> p a j", a=1).broadcast_to([P, NS, SLOTS]),
                                  ALU.add).then_inc(masked, 1)
                for k, n in enumerate((first, NS * SLOTS - first)):
                    dve.wait_ge(sc_turned, 2)
                    dve.tensor_copy(turned[0:n, k, :], ps_misc[0:n, 1 + k, :]).then_inc(sc_copied, 1)
                dve.wait_ge(rows_in, 16)
                with dve.Fori(0, TOPK // 8):
                    dve.drain()
                    dve.max(top8[:, :], rows[:, :])
                    dve.drain()
                    dve.match_replace(rows[:, :], top8[:, :], rows[:, :], TAKEN)
                dve.drain()
                dve.tensor_scalar(rows[:, :], rows[:, :], TAKEN / 2, -BIG, ALU.is_gt, ALU.mult).then_inc(hidden, 1)

            @block.tensor
            def _(pe):
                pe.sem_inc(kis_used, 2)
                pe.wait_ge(in_, 16 * (NS + 1))
                pe.transpose(ps_misc[0:IDIM, 0, 0:NS * IH], qi_rows[:, :], ident[0:NS * IH, 0:NS * IH]).then_inc(q_turned, 1)
                pe.wait_ge(q_ready, 2)
                pe.wait_ge(zeroed, 3)
                with pe.Fori(0, NS // 2) as j:
                    for u in range(2):
                        b = j * 2 + u
                        pe.wait_ge(kis_in[u], (j + 1) * 16 * (NPAGE + 1))
                        pe.wait_ge(kiT_ready, 2 * b)
                        for k in range(pairs):
                            last = pe.transpose(ps_kiT[:, k // 4, (k % 4) * P:(k % 4 + 1) * P],
                                                kis[:, u, 2 * k:2 * k + 2, :].rearrange("p a d -> p (a d)"), ident[:, :])
                            if k == pairs - 1:
                                last.then_inc(kis_used, 1)
                        pe.wait_ge(kiT_ready, 2 * b + 2)
                        pe.wait_ge(summed, b)
                        for k in range(pairs):
                            last = pe.matmul(ps_dot[:, k * 2 * IH:(k + 1) * 2 * IH], kiT[:, k, :],
                                             qi2[:, bass.ds(b, 1), :].rearrange("p a h -> p (a h)"), start=True, stop=True)
                        last.then_inc(dotted, 1)
                pe.wait_ge(masked, 3)
                flat = score[:, :, :].rearrange("p b j -> p (b j)")
                pe.transpose(ps_misc[0:first, 1, :], flat[:, 0:first], ident[:, :]).then_inc(sc_turned, 1)
                pe.transpose(ps_misc[0:NS * SLOTS - first, 2, :], flat[:, first:], ident[:, :]).then_inc(sc_turned, 1)


def phase_sample_attend(nc, T):
    with ExitStack() as ctx, Semaphores(nc, T["whole_run"], ("v_in0", "v_in1")) as sems:
        def sb(name, shape, dt=F32):
            return ctx.enter_context(nc.sbuf_tensor("sample_" + name, shape, dt))

        def sem(name):
            return sems("sample_" + name)

        ident = T["ident"]
        table = sb("table", [1, NS * NPAGE], I32)
        q_rows = sb("q_rows", [NS * H, DH])
        qB = sb("qB", [P, 2, NS, H])
        qb = sb("qb", [P, 2, H])
        K = sb("K", [P, 2, SLOTS, NKV * DH])
        V = sb("V", [P, 2, SLOTS, NKV * DH])
        KT = sb("KT", [P, 2, NKEY])
        hide = sb("hide", [H, 2, NKEY])
        s = sb("s", [H, NKEY])
        negmax = sb("negmax", [H, 1])
        total = sb("total", [H, 1])
        PT = sb("PT", [P, SLOTS, H])
        own = sb("own", [H, NKV, DH])
        o_all = sb("o_all", [H, NKV, DH])
        o = sb("o", [H, DH])
        w_out = sb("w_out", [P, KC, D])
        o_rows = sb("o_rows", [NS, D])
        oT = sb("oT", [P, KC, NS])
        x = sb("x", [NS, D])
        y = sb("y", [NS, D])
        gate = sb("gate", [NS, D])
        ps_kT = ctx.enter_context(nc.psum_tensor("sample_ps_kT", [P, 2, 512], F32))
        ps_s = ctx.enter_context(nc.psum_tensor("sample_ps_s", [P, 2, 512], F32))
        ps_pT = ctx.enter_context(nc.psum_tensor("sample_ps_pT", [P, 512], F32))
        ps_o = ctx.enter_context(nc.psum_tensor("sample_ps_o", [P, 512], F32))
        ps_y = ctx.enter_context(nc.psum_tensor("sample_ps_y", [P, 2, 512], F32))
        (table_in, q_in, end_in, zeroed, q_turned, qB_ready, qb_ready, k_turned, kT_ready, s_dotted, s_summed, maxed,
         exped, p_turned, pT_ready, pv_done, o_taken, o_ready, o_out, own_done, rows_in, o_turned, oT_ready, projected,
         y_ready, y_out) = (sem(n) for n in (
             "table_in", "q_in", "end_in", "zeroed", "q_turned", "qB_ready", "qb_ready", "k_turned", "kT_ready",
             "s_dotted", "s_summed", "maxed", "exped", "p_turned", "pT_ready", "pv_done", "o_taken", "o_ready",
             "o_out", "own_done", "rows_in", "o_turned", "oT_ready", "projected", "y_ready", "y_out"))
        k_in = [sem("k_in0"), sem("k_in1")]
        v_in = [sem("v_in0"), sem("v_in1")]
        spare = sem("spare")
        GRP = [4, 4, 4, 4, 1]
        NGR = len(GRP)

        with nc.Block() as block:
            @block.sync
            def _(sp):
                sp.dma_start(table[0:1, :], T["page_table"].rearrange("b (o j) -> o b j", o=1)).then_inc(table_in, 16)
                for b in range(NS):
                    sp.dma_start(q_rows[b * H:(b + 1) * H, :],
                                 T["qs"][SEQ + b:SEQ + b + 1, 0:D].rearrange("a (h d) -> (a h) d", d=DH)).then_inc(q_in, 16)
                sp.wait_ge(table_in, 16)
                sp.wait_ge(zeroed, 4)
                with sp.Fori(0, NS // 2) as j:
                    for u in range(2):
                        b = j * 2 + u
                        sp.wait_ge(k_turned, 2 * NGR * (b + 1))
                        sp.sem_inc(spare, 1)
                        sp.wait_ge(s_summed, NGR * (b + 1))
                        sp.sem_inc(spare, 1)
                        load_pages(sp, table, T["cache_k"], b, K[:, u], k_in[u])
                        sp.dma_start(K[0:1, u, NPAGE, :], T["k_sample"][bass.ds(b, 1), :]).then_inc(k_in[u], 16)
                        sp.dma_start(hide[:, u, :], T["hide_s"][bass.ds(b, 1), :].broadcast_to([H, NKEY])).then_inc(k_in[u], 16)
                for k in range(KC):
                    sp.dma_start(w_out[:, k, :], T["attn_w_out"][k * P:(k + 1) * P, :]).then_inc(end_in, 16)
                sp.dma_start(x[:, :], T["x_sample"]).then_inc(end_in, 16)
                for half in range(2):
                    sp.dma_start(gate[:, half * 512:half * 512 + 512], T["mods"][0, 4 + half, 1:1 + NS, :]).then_inc(end_in, 16)
                sp.wait_ge(o_out, 16 * NS)
                sp.dma_start(o_rows[:, :], T["o_s"]).then_inc(rows_in, 16)
                sp.wait_ge(y_ready, 1)
                sp.dma_start(T["xa"][SEQ:SEQ + NS, :], y[:, :]).then_inc(y_out, 16)
                sp.wait_ge(y_out, 16)

            @block.gpsimd
            def _(pool):
                pool.memset(own[:, :, :], 1.0).then_inc(own_done, 1)
                pool.wait_ge(own_done, 1)
                pool.affine_select(out=own[:, :, :], in_=own[:, :, :], compare_op=ALU.is_ge, fill=0.0,
                                   base=0, pattern=[[-GQ, NKV], [0, DH]], channel_multiplier=1).then_inc(own_done, 1)
                pool.wait_ge(own_done, 2)
                pool.affine_select(out=own[:, :, :], in_=own[:, :, :], compare_op=ALU.is_ge, fill=0.0,
                                   base=GQ - 1, pattern=[[GQ, NKV], [0, DH]], channel_multiplier=-1).then_inc(own_done, 1)
                pool.wait_ge(table_in, 16)
                pool.wait_ge(zeroed, 4)
                with pool.Fori(0, NS // 2) as j:
                    for u in range(2):
                        b = j * 2 + u
                        pool.wait_ge(pv_done, b + 1)
                        pool.sem_inc(spare, 1)
                        load_pages(pool, table, T["cache_v"], b, V[:, u], v_in[u])
                        pool.dma_start(V[0:1, u, NPAGE, :], T["v_sample"][bass.ds(b, 1), :]).then_inc(v_in[u], 16)

            @block.scalar
            def _(act):
                with act.Fori(0, NS // 2) as j:
                    for u in range(2):
                        b = j * 2 + u
                        for k in range(2 * NGR):
                            grp, kp = divmod(k, 2)
                            w = GRP[grp] * P
                            act.wait_ge(k_turned, 2 * NGR * 2 + b * 2 * NGR + k + 1)
                            act.activation(KT[:, kp, grp * 512:grp * 512 + w], ps_kT[:, k % 2, 0:w], ACT.Copy).then_inc(kT_ready, 1)
                        act.wait_ge(maxed, b + 1)
                        act.activation(s[:, :], s[:, :], ACT.Exp, bias=negmax[:, 0:1], accum_out=total[:, :]).then_inc(exped, 1)
                        act.wait_ge(p_turned, b + 1)
                        act.activation(PT[:, :, :], ps_pT[:, 0:SLOTS * H].rearrange("p (j h) -> p j h", h=H), ACT.Copy).then_inc(pT_ready, 1)
                        act.wait_ge(o_ready, b + 1)
                        act.dma_start(T["o_s"][bass.ds(b, 1), :].rearrange("a (h d) -> (a h) d", d=DH), o[:, :]).then_inc(o_out, 16)

            @block.vector
            def _(dve):
                dve.sem_inc(s_summed, 2 * NGR)
                dve.memset(K[:, :, NPAGE, :], 0.0).then_inc(zeroed, 1)
                dve.memset(V[:, :, NPAGE, :], 0.0).then_inc(zeroed, 1)
                dve.memset(qB[:, 0, :, :], 0.0).then_inc(zeroed, 1)
                dve.memset(qB[:, 1, :, :], 0.0).then_inc(zeroed, 1)
                dve.wait_ge(zeroed, 4)
                dve.wait_ge(q_turned, 1)
                turned = ps_pT[0:DH, 0:NS * H].rearrange("p (b h) -> p b h", h=H)
                for kp in range(2):
                    for half in range(2):
                        heads = slice((2 * kp + half) * GQ, (2 * kp + half + 1) * GQ)
                        dve.tensor_scalar(qB[half * DH:(half + 1) * DH, kp, :, heads], turned[:, :, heads], DH ** -0.5, None,
                                          ALU.mult).then_inc(qB_ready, 1)
                dve.wait_ge(own_done, 3)
                dve.wait_ge(qB_ready, 4)
                with dve.Fori(0, NS // 2) as j:
                    for u in range(2):
                        b = j * 2 + u
                        dve.wait_ge(s_dotted, NGR * b)
                        dve.tensor_copy(qb[:, :, :], qB[:, :, bass.ds(b, 1), :].rearrange("p k a h -> p k (a h)")).then_inc(qb_ready, 1)
                        dve.wait_ge(p_turned, b)
                        dve.wait_ge(k_in[u], (j + 1) * 16 * (NPAGE + 2))
                        for grp in range(NGR):
                            keys = slice(grp * 512, grp * 512 + GRP[grp] * P)
                            dve.wait_ge(s_dotted, NGR * b + grp + 1)
                            dve.tensor_tensor(s[:, keys], ps_s[0:H, (u * NGR + grp) % 2, 0:GRP[grp] * P], hide[:, u, keys], ALU.add).then_inc(s_summed, 1)
                        dve.drain()
                        dve.tensor_reduce(negmax[:, :], s[:, :], AX.X, ALU.max, negate=True).then_inc(maxed, 1)
                        dve.wait_ge(pv_done, 2 + b + 1)
                        dve.wait_ge(exped, b + 1)
                        dve.reciprocal(total[:, :], total[:, :])
                        dve.drain()
                        dve.scalar_tensor_tensor(o_all[:, :, :], ps_o[0:H, 0:NKV * DH].rearrange("p (n d) -> p n d", d=DH), total[:, 0:1],
                                                 own[:, :, :], ALU.mult, ALU.mult).then_inc(o_taken, 1)
                        dve.drain()
                        dve.wait_ge(o_out, 16 * b)
                        dve.tensor_reduce(o[:, :], o_all[:, :, :].rearrange("p n d -> p d n"), AX.X, ALU.add).then_inc(o_ready, 1)
                dve.wait_ge(o_turned, 1)
                dve.tensor_copy(oT[:, :, :], ps_kT[:, 0, 0:KC * NS].rearrange("p (k b) -> p k b", b=NS)).then_inc(oT_ready, 1)
                dve.wait_ge(projected, 1)
                dve.wait_ge(end_in, 16 * (KC + 3))
                dve.tensor_tensor(y[:, :], ps_y[0:NS].rearrange("p a n -> p (a n)"), gate[:, :], ALU.mult)
                dve.drain()
                dve.tensor_tensor(y[:, :], y[:, :], x[:, :], ALU.add).then_inc(y_ready, 1)

            @block.tensor
            def _(pe):
                pe.sem_inc(k_turned, 2 * NGR * 2)
                pe.sem_inc(pv_done, 2)
                pe.wait_ge(q_in, 16 * NS)
                pe.transpose(ps_pT[0:DH, 0:NS * H], q_rows[:, :], ident[:, :]).then_inc(q_turned, 1)
                with pe.Fori(0, NS // 2) as j:
                    for u in range(2):
                        b = j * 2 + u
                        pe.wait_ge(k_in[u], (j + 1) * 16 * (NPAGE + 2))
                        pe.wait_ge(qb_ready, b + 1)

                        def dots(grp):
                            w = GRP[grp] * P
                            pe.wait_ge(kT_ready, 2 * NGR * b + 2 * grp + 2)
                            pe.wait_ge(s_summed, NGR * b + grp + 2 * NGR - 1)
                            for kp in range(2):
                                last = pe.matmul(ps_s[0:H, (u * NGR + grp) % 2, 0:w], qb[:, kp, :], KT[:, kp, grp * 512:grp * 512 + w],
                                                 start=(kp == 0), stop=(kp == 1))
                            last.then_inc(s_dotted, 1)
                        for grp in range(NGR + 1):
                            if grp < NGR:
                                for kp in range(2):
                                    if grp:
                                        pe.wait_ge(kT_ready, 2 * NGR * b + 2 * grp + kp - 1)
                                    else:
                                        pe.wait_ge(kT_ready, 2 * NGR * b)
                                    for a in range(GRP[grp]):
                                        last = pe.transpose(ps_kT[:, kp, a * P:(a + 1) * P], K[:, u, grp * 4 + a, kp * P:(kp + 1) * P], ident[:, :])
                                    last.then_inc(k_turned, 1)
                            if grp:
                                dots(grp - 1)
                        pe.wait_ge(exped, b + 1)
                        pe.sem_inc(spare, 1)
                        for k in range(SLOTS):
                            last = pe.transpose(ps_pT[:, k * H:(k + 1) * H], s[:, k * P:(k + 1) * P], ident[0:H, 0:H])
                        last.then_inc(p_turned, 1)
                        pe.wait_ge(pT_ready, b + 1)
                        pe.wait_ge(v_in[u], (j + 1) * 16 * (NPAGE + 1))
                        pe.wait_ge(o_taken, b)
                        for k in range(SLOTS):
                            last = pe.matmul(ps_o[0:H, 0:NKV * DH], PT[:, k, :], V[:, u, k, :], start=(k == 0), stop=(k == SLOTS - 1))
                        last.then_inc(pv_done, 1)
                pe.wait_ge(rows_in, 16)
                pe.wait_ge(end_in, 16 * (KC + 3))
                for k in range(KC):
                    last = pe.transpose(ps_kT[:, 0, k * NS:(k + 1) * NS], o_rows[:, k * P:(k + 1) * P], ident[0:NS, 0:NS])
                last.then_inc(o_turned, 1)
                pe.wait_ge(oT_ready, 1)
                for half in range(2):
                    for k in range(KC):
                        last = pe.matmul(ps_y[0:NS, half, :], oT[:, k, :], w_out[:, k, half * 512:half * 512 + 512],
                                         start=(k == 0), stop=(k == KC - 1))
                last.then_inc(projected, 1)


def phase_route(nc, T, l, src):
    with ExitStack() as ctx, Semaphores(nc, T["whole_run"], ("scattered",)) as sems:
        def sb(name, shape, dt=F32):
            return ctx.enter_context(nc.sbuf_tensor(f"route{l}_" + name, shape, dt))

        def sem(name):
            return sems(f"route{l}_" + name)

        ident, dest_i, share, blocks = T["ident"], T["dest"], T["share"], T["blocks"]
        NL = NG + NE
        NTT = NT + 1
        wr = sb("wr", [P, KC, NL])
        bias = sb("bias", [P, NL])
        gain = sb("gain", [P, 2, D])
        shift = sb("shift", [P, 2, D])
        x = sb("x", [P, 2, D])
        h = sb("h", [P, 2, D])
        hT = sb("hT", [P, 2, KC, P])
        ss = sb("ss", [P, 2])
        rs = sb("rs", [P, 2])
        logits = sb("logits", [P, NTT, NL])
        best = sb("best", [P, 6, NTT])
        group_is = sb("group_is", [P, NTT, NG])
        allowed = sb("allowed", [P, NTT, NE])
        first_is = sb("first_is", [P, NTT, NE])
        second_is = sb("second_is", [P, NTT, NE])
        tmp = sb("tmp", [P, NTT, NE])
        early = sb("early", [P, NE])
        valid = sb("valid", [P, NTT])
        chosen = sb("chosen", [P, NTT, NE], BF16)
        before = sb("before", [P, P], BF16)
        ones = sb("ones", [P, P], BF16)
        place = sb("place", [P, NTT, NE])
        offset = sb("offset", [P, NTT + 1, NE])
        counts_i = sb("counts_i", [P, NE], I32)
        padded = sb("padded", [P, NE])
        onesf = sb("onesf", [P, NE])
        pend = sb("pend", [P, NE])
        dest = sb("dest", [P, NTT, 2])
        starts = sb("starts", [1, NB])
        passed = sb("passed", [1, NB, NE])
        expert = sb("expert", [1, NB])
        token = sb("token", [P, NTT], I32)
        zeros = sb("zeros", [P, NB], I32)
        psT = ctx.enter_context(nc.psum_tensor(f"route{l}_psT", [P, KC, P], F32))
        psL = ctx.enter_context(nc.psum_tensor(f"route{l}_psL", [P, 2, 512], F32))
        psR = ctx.enter_context(nc.psum_tensor(f"route{l}_psR", [P, 4, 512], F32))
        (w_in, mod_in, squared, rstd, x_used, h_turned, hT_ready, routed, summed, pool_chain, consts, filled, vec,
         group_exp, e_exp, chosen_done, ranked, placed, scattered, spare) = (sem(n) for n in (
             "w_in", "mod_in", "squared", "rstd", "x_used", "h_turned", "hT_ready", "routed", "summed", "pool_chain",
             "consts", "filled", "vec", "group_exp", "e_exp", "chosen_done", "ranked", "placed", "scattered",
             "spare"))
        x_in = [sem("x_in0"), sem("x_in1")]
        h_out = [sem("h_out0"), sem("h_out1")]

        with nc.Block() as block:
            @block.sync
            def _(sp):
                load_modulation(sp, T, l, 4, gain[:, 0], gain[:, 1], mod_in)
                load_modulation(sp, T, l, 3, shift[:, 0], shift[:, 1], mod_in)
                sp.dma_start(h[:, 0, :], T["norm_ffn_g"][l:l + 1, :].broadcast_to([P, D])).then_inc(mod_in, 16)
                for k in range(KC):
                    sp.dma_start(wr[:, k, 0:NG], T["moe_w_group"][l, k * P:(k + 1) * P, :]).then_inc(w_in, 16)
                    sp.dma_start(wr[:, k, NG:NL], T["moe_w_expert"][l, k * P:(k + 1) * P, :]).then_inc(w_in, 16)
                sp.dma_start(bias[:, 0:NG], T["moe_b_group"][l:l + 1, :].broadcast_to([P, NG])).then_inc(w_in, 16)
                sp.dma_start(bias[:, NG:NL], T["moe_b_expert"][l:l + 1, :].broadcast_to([P, NE])).then_inc(w_in, 16)

                def body(t, b, rows):
                    sp.wait_ge(x_used, t + 1)
                    sp.dma_start(x[0:rows, b], T[src][bass.ds(t * P, P)] if rows == P else T[src][SEQ:SEQ + NS]).then_inc(x_in[b], 16)
                two_by_two(sp, body)
                sp.wait_ge(consts, 8)
                sp.dma_start(T["row_tok"].rearrange("(p b) o -> p (b o)", p=P), zeros[:, :]).then_inc(filled, 16)

            @block.gpsimd
            def _(pool):
                pool.memset(before[:, :], 1.0).then_inc(consts, 1)
                pool.memset(ones[:, :], 1.0).then_inc(consts, 1)
                pool.memset(valid[:, :], 1.0).then_inc(consts, 1)
                pool.memset(zeros[:, :], 0).then_inc(consts, 1)
                pool.wait_ge(consts, 4)
                pool.affine_select(out=before[:, :], in_=before[:, :], compare_op=ALU.is_gt, fill=0.0,
                                   base=0, pattern=[[1, P]], channel_multiplier=-1).then_inc(consts, 1)
                pool.affine_select(out=valid[:, :], in_=valid[:, :], compare_op=ALU.is_ge, fill=0.0,
                                   base=NTOK - 1, pattern=[[-P, NTT]], channel_multiplier=-1).then_inc(consts, 1)
                pool.iota(token[:, :], pattern=[[P, NTT]], base=0, channel_multiplier=1).then_inc(consts, 1)
                pool.memset(onesf[:, :], 1.0).then_inc(consts, 1)
                link = Chain(pool, pool_chain)

                def body(t, b, rows):
                    pool.wait_ge(squared, t + 1)
                    norm_rstd(pool, link, rs[0:rows, b:b + 1], ss[0:rows, b:b + 1], T["power"][0:rows]).then_inc(rstd, 1)
                with pool.Fori(0, NT // 2) as j:
                    link.enter(j, 2)
                    body(j * 2, 0, P)
                    body(j * 2 + 1, 1, P)
                    link.leave(NT // 2)
                body(NT, 0, NS)
                pool.wait_ge(placed, 1)
                pool.wait_ge(filled, 16)
                for t in range(NTT):
                    rows = P if t < NT else NS
                    for k in range(2):
                        pool.indirect_dma_start(out=T["row_tok"], out_offset=bass.IndirectOffsetOnAxis(ap=dest_i[0:rows, t, k:k + 1], axis=0),
                                                in_=token[0:rows, t:t + 1], in_offset=None).then_inc(scattered, 16)
                pool.wait_ge(scattered, 16 * 2 * NTT)

            @block.scalar
            def _(act):
                def body(t, b, rows):
                    act.wait_ge(x_in[b], (t - b) * 8 + 16)
                    act.wait_ge(routed, t + 1)
                    act.activation(hT[0:rows, b].rearrange("p k n -> p (k n)"), x[0:rows, b], ACT.Square, scale=D ** -0.5,
                                   accum_out=ss[0:rows, b:b + 1]).then_inc(squared, 1)
                    act.wait_ge(x_used, 2 + t + 1)
                    act.dma_start(T["hs"][bass.ds(t * P, P)] if rows == P else T["hs"][SEQ:SEQ + NS], h[0:rows, b]).then_inc(h_out[b], 16)
                    act.wait_ge(h_turned, 2 + t + 1)
                    act.wait_ge(squared, t + 1)
                    act.activation(hT[:, b, :, 0:rows], psT[:, :, 0:rows], ACT.Copy).then_inc(hT_ready, 1)
                two_by_two(act, body)
                act.wait_ge(vec, 1)
                act.activation(tmp[:, :, 0:NG], tmp[:, :, 0:NG], ACT.Exp).then_inc(group_exp, 1)
                act.wait_ge(vec, 2)
                act.activation(best[:, 4, :], best[:, 4, :], ACT.Exp).then_inc(e_exp, 1)
                act.wait_ge(h_out[0], 16 * (NT // 2 + 1))
                act.wait_ge(h_out[1], 16 * (NT // 2))

            @block.vector
            def _(dve):
                dve.sem_inc(x_used, 2)
                dve.memset(logits[:, NT, :], 0.0)
                for e in range(NE):
                    dve.memset(early[:, e:e + 1], float(NE - e))
                for i in range(NB):
                    dve.memset(starts[0:1, i:i + 1], float(i * BLK))
                dve.wait_ge(mod_in, 16 * 9)
                dve.tensor_tensor(gain[:, 0], gain[:, 0], h[:, 0], ALU.mult)
                dve.tensor_tensor(gain[0:NS, 1], gain[0:NS, 1], h[0:NS, 0], ALU.mult)
                dve.drain()
                dve.wait_ge(w_in, 16 * (2 * KC + 2))

                def body(t, b, rows):
                    s = 0 if rows == P else 1
                    dve.wait_ge(rstd, t + 1)
                    dve.wait_ge(h_turned, t + 1)
                    dve.wait_ge(h_out[b], (t - b) * 8)
                    dve.scalar_tensor_tensor(h[0:rows, b], x[0:rows, b], rs[0:rows, b:b + 1], gain[0:rows, s], ALU.mult, ALU.mult)
                    dve.drain()
                    dve.tensor_tensor(h[0:rows, b], h[0:rows, b], shift[0:rows, s], ALU.add).then_inc(x_used, 1)
                    dve.wait_ge(routed, 2 + t + 1)
                    dve.tensor_tensor(logits[0:rows, bass.ds(t, 1), :].rearrange("p a n -> p (a n)"), psL[0:rows, b, 0:NL],
                                      bias[0:rows, :], ALU.add).then_inc(summed, 1)
                two_by_two(dve, body)
                dve.drain()

                def wide(v, n):
                    return v.rearrange("p (t a) -> p t a", a=1).broadcast_to([P, NTT, n])

                def first_of(values, top, out, n):
                    dve.tensor_tensor(out, values, wide(top, n), ALU.is_equal)
                    dve.drain()
                    dve.tensor_tensor(out, out, early[:, 0:n].rearrange("p (a n) -> p a n", a=1).broadcast_to([P, NTT, n]), ALU.mult)
                    dve.drain()
                    dve.tensor_reduce(best[:, 5, :], out, AX.X, ALU.max)
                    dve.drain()
                    dve.tensor_tensor(out, out, wide(best[:, 5, :], n), ALU.is_equal)
                    dve.drain()
                glog, elog = logits[:, :, 0:NG], logits[:, :, NG:NL]
                dve.tensor_reduce(best[:, 0, :], glog, AX.X, ALU.max)
                dve.drain()
                first_of(glog, best[:, 0, :], group_is[:, :, :], NG)
                dve.tensor_tensor(tmp[:, :, 0:NG], glog, wide(best[:, 0, :], NG), ALU.subtract).then_inc(vec, 1)
                dve.wait_ge(group_exp, 1)
                dve.tensor_reduce(best[:, 1, :], tmp[:, :, 0:NG], AX.X, ALU.add)
                dve.drain()
                dve.tensor_scalar(group_is[:, :, :], group_is[:, :, :], BIG, -BIG, ALU.mult, ALU.add)
                dve.drain()
                dve.tensor_tensor(allowed[:, :, :].rearrange("p t (g e) -> p t g e", g=NG), elog.rearrange("p t (g e) -> p t g e", g=NG),
                                  group_is[:, :, :].rearrange("p t (g a) -> p t g a", a=1).broadcast_to([P, NTT, NG, EPG]), ALU.add)
                dve.drain()
                dve.tensor_reduce(best[:, 2, :], allowed[:, :, :], AX.X, ALU.max)
                dve.drain()
                first_of(allowed[:, :, :], best[:, 2, :], first_is[:, :, :], NE)
                dve.scalar_tensor_tensor(allowed[:, :, :], first_is[:, :, :], -BIG, allowed[:, :, :], ALU.mult, ALU.add)
                dve.drain()
                dve.tensor_reduce(best[:, 3, :], allowed[:, :, :], AX.X, ALU.max)
                dve.drain()
                first_of(allowed[:, :, :], best[:, 3, :], second_is[:, :, :], NE)
                dve.tensor_tensor(best[:, 4, :], best[:, 3, :], best[:, 2, :], ALU.subtract).then_inc(vec, 1)
                dve.wait_ge(e_exp, 1)
                dve.tensor_scalar(best[:, 5, :], best[:, 4, :], 1.0, None, ALU.add)
                dve.drain()
                dve.tensor_tensor(best[:, 5, :], best[:, 5, :], best[:, 1, :], ALU.mult)
                dve.drain()
                dve.reciprocal(share[:, :, 0], best[:, 5, :])
                dve.drain()
                dve.tensor_tensor(share[:, :, 1], share[:, :, 0], best[:, 4, :], ALU.mult)
                dve.tensor_tensor(tmp[:, :, :], first_is[:, :, :], second_is[:, :, :], ALU.add)
                dve.drain()
                dve.wait_ge(consts, 8)
                dve.tensor_tensor(chosen[:, :, :], tmp[:, :, :], wide(valid[:, :], NE), ALU.mult).then_inc(chosen_done, 1)
                dve.wait_ge(ranked, 1)
                half = NTT * NE // 2
                dve.tensor_copy(place[:, :, :].rearrange("p t e -> p (t e)")[:, 0:half], psR[:, 0, 0:half])
                dve.tensor_copy(place[:, :, :].rearrange("p t e -> p (t e)")[:, half:], psR[:, 1, 0:half])
                dve.tensor_copy(tmp[:, :, :].rearrange("p t e -> p (t e)")[:, 0:half], psR[:, 2, 0:half])
                dve.tensor_copy(tmp[:, :, :].rearrange("p t e -> p (t e)")[:, half:], psR[:, 3, 0:half])
                dve.memset(offset[:, 0, :], 0.0)
                dve.drain()
                for t in range(NTT):
                    dve.tensor_tensor(offset[:, t + 1, :], offset[:, t, :], tmp[:, t, :], ALU.add)
                    dve.drain()
                dve.tensor_scalar(counts_i[:, :], offset[:, NTT, :], float(BLK - 1), None, ALU.add)
                dve.drain()
                dve.tensor_scalar(counts_i[:, :], counts_i[:, :], 7, 7, ALU.logical_shift_right, ALU.logical_shift_left)
                dve.drain()
                dve.tensor_copy(padded[:, :], counts_i[:, :])
                dve.drain()
                dve.tensor_tensor_scan(pend[:, :], onesf[:, :], padded[:, :], 0.0, ALU.mult, ALU.add)
                dve.drain()
                dve.tensor_tensor(padded[:, :], pend[:, :], padded[:, :], ALU.subtract)
                dve.drain()
                dve.tensor_tensor(place[:, :, :], place[:, :, :], offset[:, 0:NTT, :], ALU.add)
                dve.drain()
                dve.tensor_tensor(place[:, :, :], place[:, :, :], padded[:, :].rearrange("p (a e) -> p a e", a=1).broadcast_to([P, NTT, NE]), ALU.add)
                dve.drain()
                for k, is_ in enumerate((first_is, second_is)):
                    dve.tensor_tensor(is_[:, :, :], is_[:, :, :], place[:, :, :], ALU.mult)
                    dve.drain()
                    dve.tensor_reduce(dest[:, :, k], is_[:, :, :], AX.X, ALU.add)
                dve.drain()
                dve.tensor_copy(dest_i[:, :, :], dest[:, :, :]).then_inc(placed, 1)
                dve.tensor_tensor(passed[:, :, :], pend[0:1, :].rearrange("p (a e) -> p a e", a=1).broadcast_to([1, NB, NE]),
                                  starts[0:1, :].rearrange("p (b a) -> p b a", a=1).broadcast_to([1, NB, NE]), ALU.is_le)
                dve.drain()
                dve.tensor_reduce(expert[:, :], passed[:, :, :], AX.X, ALU.add)
                dve.drain()
                dve.tensor_scalar(blocks[0:1, :], expert[:, :], float(NE - 1), None, ALU.min)
                dve.drain()

            @block.tensor
            def _(pe):
                pe.sem_inc(routed, 2)
                pe.sem_inc(h_turned, 2)
                pe.wait_ge(w_in, 16 * (2 * KC + 2))

                def body(t, b, rows):
                    pe.wait_ge(x_used, 2 + t + 1)
                    pe.wait_ge(hT_ready, t)
                    pe.sem_inc(spare, 1)
                    for k in range(KC):
                        last = pe.transpose(psT[:, k, 0:rows], h[0:rows, b, k * P:(k + 1) * P], ident[0:rows, 0:rows])
                    last.then_inc(h_turned, 1)
                    pe.wait_ge(hT_ready, t + 1)
                    pe.wait_ge(summed, t - 1) if isinstance(t, int) else pe.wait_ge(summed, t)
                    for k in range(KC):
                        last = pe.matmul(psL[0:rows, b, 0:NL], hT[:, b, k, 0:rows], wr[:, k, :], start=(k == 0), stop=(k == KC - 1))
                    last.then_inc(routed, 1)
                two_by_two(pe, body)
                pe.wait_ge(chosen_done, 1)
                pe.wait_ge(consts, 8)
                flat = chosen[:, :, :].rearrange("p t e -> p (t e)")
                half = NTT * NE // 2
                for k in range(2):
                    pe.matmul(psR[:, k, 0:half], before[:, :], flat[:, k * half:(k + 1) * half], start=True, stop=True)
                    last = pe.matmul(psR[:, 2 + k, 0:half], ones[:, :], flat[:, k * half:(k + 1) * half], start=True, stop=True)
                last.then_inc(ranked, 1)


def phase_experts(nc, T, l):
    with ExitStack() as ctx, Semaphores(nc, T["whole_run"], ("idx_in", "x_in0", "x_in1")) as sems:
        def sb(name, shape, dt=F32):
            return ctx.enter_context(nc.sbuf_tensor(f"experts{l}_" + name, shape, dt))

        def sem(name):
            return sems(f"experts{l}_" + name)

        ident, blocks = T["ident"], T["blocks"]
        KF = FE // P
        idx = sb("idx", [P, NB], I32)
        idx_rows = sb("idx_rows", [NB, P], I32)
        idx_f = sb("idx_f", [NB, P])
        idxb = sb("idxb", [P, 2], I32)
        w1 = sb("w1", [P, 2, KC, 2 * FE])
        w2 = sb("w2", [P, 2, KF, D])
        x = sb("x", [P, 2, D])
        xT = sb("xT", [P, 2, KC, P])
        th = sb("th", [P, 2, FE])
        mid = sb("mid", [P, 2, FE])
        midT = sb("midT", [P, KF, P])
        y = sb("y", [P, 2, D])
        ps_x = ctx.enter_context(nc.psum_tensor(f"experts{l}_ps_x", [P, KC, P], F32))
        ps_gu = ctx.enter_context(nc.psum_tensor(f"experts{l}_ps_gu", [P, 2, 512], F32))
        ps_m = ctx.enter_context(nc.psum_tensor(f"experts{l}_ps_m", [P, 4, P], F32))
        ps_y = ctx.enter_context(nc.psum_tensor(f"experts{l}_ps_y", [P, 2, 512], F32))
        (idx_in, idx_turned, idx_ready, x_turned, xT_ready, up_done, tanhed, silued, midded, mid_turned, midT_ready, down_done,
         y_copied, spare) = (sem(n) for n in (
             "idx_in", "idx_turned", "idx_ready", "x_turned", "xT_ready", "up_done", "tanhed", "silued", "midded", "mid_turned",
             "midT_ready", "down_done", "y_copied", "spare"))
        w1_in = [sem("w1_in0"), sem("w1_in1")]
        w2_in = [sem("w2_in0"), sem("w2_in1")]
        x_in = [sem("x_in0"), sem("x_in1")]
        y_out = [sem("y_out0"), sem("y_out1")]

        def all_blocks(eng, body):
            with eng.Fori(0, NB // 2) as j:
                body(j * 2, 0)
                body(j * 2 + 1, 1)
            body(NB - 1, 0)

        with nc.Block() as block:
            @block.sync
            def _(sp):
                def body(b, u):
                    sp.wait_ge(up_done, b + 1)
                    sp.sem_inc(spare, 1)
                    e = sp.value_load(blocks[0:1, bass.ds(b, 1)] if not isinstance(b, int) else blocks[0:1, b:b + 1], min_val=0, max_val=NE - 1)
                    sp.dma_start(w1[:, u].rearrange("p k n -> p (k n)"),
                                 T["moe_w1"][l, bass.ds(e, 1)].rearrange("a (p k) n -> p (a k n)", k=KC)).then_inc(w1_in[u], 16)
                    sp.wait_ge(down_done, 2 * b + 2)
                    sp.dma_start(w2[:, u].rearrange("p k n -> p (k n)"),
                                 T["moe_w2"][l, bass.ds(e, 1)].rearrange("a (p k) n -> p (a k n)", k=KF)).then_inc(w2_in[u], 16)
                all_blocks(sp, body)

            @block.gpsimd
            def _(pool):
                pool.dma_start(idx_rows[:, :], T["row_tok"].rearrange("(b p) o -> b (p o)", p=P)).then_inc(idx_in, 16)
                pool.wait_ge(idx_turned, 3)

                def body(b, u):
                    pool.wait_ge(x_turned, b + 1)
                    pool.sem_inc(spare, 1)
                    pool.tensor_copy(idxb[:, u:u + 1], idx[:, bass.ds(b, 1)]).then_inc(idx_ready, 1)
                    pool.wait_ge(idx_ready, b + 1)
                    pool.sem_inc(spare, 1)
                    pool.indirect_dma_start(out=x[:, u, :], out_offset=None, in_=T["hs"],
                                            in_offset=bass.IndirectOffsetOnAxis(ap=idxb[:, u:u + 1], axis=0)).then_inc(x_in[u], 16)
                all_blocks(pool, body)

            @block.scalar
            def _(act):
                def body(b, u):
                    act.wait_ge(x_turned, 2 + b + 1)
                    act.activation(xT[:, u], ps_x[:, :, :], ACT.Copy).then_inc(xT_ready, 1)
                    act.wait_ge(up_done, 2 + b + 1)
                    act.wait_ge(silued, b + 1)
                    act.activation(th[:, u], ps_gu[:, u, 0:FE], ACT.Tanh, scale=0.5).then_inc(tanhed, 1)
                    for half in range(2):
                        act.wait_ge(down_done, 4 + 2 * b + half + 1)
                        if half == 0:
                            act.wait_ge(y_out[u], (b - u) * 8)
                        act.activation(y[:, u, half * 512:half * 512 + 512], ps_y[:, half, :], ACT.Copy).then_inc(y_copied, 1)
                    act.wait_ge(y_copied, 2 * b + 2)
                    act.dma_start(T["yb"][bass.ds(b * BLK, BLK), :], y[:, u]).then_inc(y_out[u], 16)
                all_blocks(act, body)
                act.wait_ge(y_out[0], 16 * (NB // 2 + 1))
                act.wait_ge(y_out[1], 16 * (NB // 2))

            @block.vector
            def _(dve):
                dve.sem_inc(silued, 2)
                dve.wait_ge(idx_in, 16)
                dve.tensor_copy(idx_f[:, :], idx_rows[:, :]).then_inc(idx_turned, 1)
                dve.wait_ge(idx_turned, 2)
                dve.tensor_copy(idx[:, :], ps_m[:, 3, 0:NB]).then_inc(idx_turned, 1)

                def body(b, u):
                    g, up = ps_gu[:, u, 0:FE], ps_gu[:, u, FE:]
                    dve.wait_ge(tanhed, b + 1)
                    dve.scalar_tensor_tensor(th[:, u], th[:, u], 1.0, g, ALU.add, ALU.mult)
                    dve.drain()
                    dve.wait_ge(mid_turned, b + 1)
                    dve.scalar_tensor_tensor(mid[:, u], th[:, u], 0.5, up, ALU.mult, ALU.mult).then_inc(silued, 1)
                    dve.wait_ge(mid_turned, 2 + b + 1)
                    dve.wait_ge(down_done, 4 + 2 * b)
                    dve.tensor_copy(midT[:, :, :], ps_m[:, 0:KF, :]).then_inc(midT_ready, 1)
                all_blocks(dve, body)

            @block.tensor
            def _(pe):
                pe.sem_inc(up_done, 2)
                pe.sem_inc(down_done, 4)
                pe.sem_inc(x_turned, 2)
                pe.sem_inc(mid_turned, 2)

                def turn(b, u):
                    pe.wait_ge(x_in[u], (b - u) * 8 + 16)
                    pe.wait_ge(xT_ready, b)
                    rows = x[:, u].rearrange("p (c k) -> p k c", k=KC)
                    for k in range(KC):
                        last = pe.transpose(ps_x[:, k, :], rows[:, k, :], ident[:, :])
                    last.then_inc(x_turned, 1)

                def body(b, u, more=True):
                    pe.wait_ge(xT_ready, b + 1)
                    pe.wait_ge(w1_in[u], (b - u) * 8 + 16)
                    pe.wait_ge(silued, b + 1)
                    for k in range(KC):
                        last = pe.matmul(ps_gu[:, u, :], xT[:, u, k, :], w1[:, u, k, :], start=(k == 0), stop=(k == KC - 1))
                    last.then_inc(up_done, 1)
                    if more:
                        turn(b + 1, 1 - u)
                    pe.wait_ge(silued, 2 + b + 1)
                    pe.wait_ge(midT_ready, b)
                    cols = mid[:, u].rearrange("p (c k) -> p k c", k=KF)
                    for k in range(KF):
                        last = pe.transpose(ps_m[:, k, :], cols[:, k, :], ident[:, :])
                    last.then_inc(mid_turned, 1)
                    pe.wait_ge(midT_ready, b + 1)
                    pe.wait_ge(w2_in[u], (b - u) * 8 + 16)
                    for half in range(2):
                        pe.wait_ge(y_copied, 2 * b if half == 0 else 2 * b)
                        for k in range(KF):
                            last = pe.matmul(ps_y[:, half, :], midT[:, k, :], w2[:, u, k, half * 512:half * 512 + 512],
                                             start=(k == 0), stop=(k == KF - 1))
                        last.then_inc(down_done, 1)
                pe.wait_ge(idx_turned, 1)
                pe.transpose(ps_m[:, 3, 0:NB], idx_f[:, :], ident[0:NB, 0:NB]).then_inc(idx_turned, 1)
                pe.wait_ge(idx_turned, 3)
                turn(0, 0)
                with pe.Fori(0, NB // 2) as j:
                    body(j * 2, 0)
                    body(j * 2 + 1, 1)
                body(NB - 1, 0, more=False)


def phase_combine(nc, T, l, src, dst, final):
    with ExitStack() as ctx, Semaphores(nc, T["whole_run"], ("y_in0", "y_in1")) as sems:
        def sb(name, shape, dt=F32):
            return ctx.enter_context(nc.sbuf_tensor(f"combine{l}_" + name, shape, dt))

        def sem(name):
            return sems(f"combine{l}_" + name)

        dest_i, share = T["dest"], T["share"]
        gate = sb("gate", [P, 2, D])
        g_final = sb("g_final", [P, D])
        idxb = sb("idxb", [P, 2, 2], I32)
        x = sb("x", [P, 2, D])
        y = sb("y", [P, 2, 2, D])
        z = sb("z", [P, 2, D])
        junk = sb("junk", [P, D])
        ss = sb("ss", [P, 2])
        rs = sb("rs", [P, 2])
        (mod_in, idx_ready, added, weighed, squared, rstd, chain, done, spare) = (sem(n) for n in (
            "mod_in", "idx_ready", "added", "weighed", "squared", "rstd", "chain", "done", "spare"))
        x_in = [sem("x_in0"), sem("x_in1")]
        y_in = [sem("y_in0"), sem("y_in1")]
        out_ = [sem("out0"), sem("out1")]

        def share_at(t, rows, k):
            return share[0:rows, bass.ds(t, 1), k]

        with nc.Block() as block:
            @block.sync
            def _(sp):
                load_modulation(sp, T, l, 5, gate[:, 0], gate[:, 1], mod_in)
                sp.dma_start(g_final[:, :], T["norm_final_g"].broadcast_to([P, D])).then_inc(mod_in, 16)

                def body(t, b, rows):
                    sp.wait_ge(done, t + 1)
                    sp.dma_start(x[0:rows, b], T[src][bass.ds(t * P, P)] if rows == P else T[src][SEQ:SEQ + NS]).then_inc(x_in[b], 16)
                two_by_two(sp, body)

            @block.gpsimd
            def _(pool):
                link = Chain(pool, chain)

                def body(t, b, rows):
                    pool.wait_ge(done, t + 1)
                    pool.sem_inc(spare, 1)
                    pool.tensor_copy(idxb[0:rows, b, :], dest_i[0:rows, bass.ds(t, 1), :].rearrange("p a k -> p (a k)")).then_inc(idx_ready, 1)
                    pool.wait_ge(idx_ready, t + 1)
                    pool.sem_inc(spare, 1)
                    for k in range(2):
                        pool.indirect_dma_start(out=y[0:rows, b, k, :], out_offset=None, in_=T["yb"],
                                                in_offset=bass.IndirectOffsetOnAxis(ap=idxb[0:rows, b, k:k + 1], axis=0)).then_inc(y_in[b], 16)

                def norm(t, b, rows):
                    pool.wait_ge(squared, t + 1)
                    norm_rstd(pool, link, rs[0:rows, b:b + 1], ss[0:rows, b:b + 1], T["power"][0:rows]).then_inc(rstd, 1)
                with pool.Fori(0, NT // 2) as j:
                    if final:
                        link.enter(j, 2)
                    body(j * 2, 0, P)
                    body(j * 2 + 1, 1, P)
                    if final:
                        norm(j * 2, 0, P)
                        norm(j * 2 + 1, 1, P)
                        link.leave(NT // 2)
                body(NT, 0, NS)
                if final:
                    norm(NT, 0, NS)

            @block.scalar
            def _(act):
                def body(t, b, rows):
                    act.wait_ge(y_in[b], (t - b) * 16 + 32)
                    act.activation(y[0:rows, b, 0, :], y[0:rows, b, 0, :], ACT.Copy, scale=share_at(t, rows, 0)).then_inc(weighed, 1)
                    if final:
                        act.wait_ge(added, t + 1)
                        act.activation(junk[0:rows, :], z[0:rows, b, :], ACT.Square, scale=D ** -0.5,
                                       accum_out=ss[0:rows, b:b + 1]).then_inc(squared, 1)
                    act.wait_ge(done, 2 + t + 1)
                    out = ((T["y_prompt"][bass.ds(t * P, P)] if rows == P else T["y_sample"]) if final else
                           (T[dst][bass.ds(t * P, P)] if rows == P else T[dst][SEQ:SEQ + NS]))
                    act.dma_start(out, z[0:rows, b, :]).then_inc(out_[b], 16)
                two_by_two(act, body)
                act.wait_ge(out_[0], 16 * (NT // 2 + 1))
                act.wait_ge(out_[1], 16 * (NT // 2))

            @block.vector
            def _(dve):
                dve.sem_inc(done, 2)
                dve.wait_ge(mod_in, 16 * 5)

                def body(t, b, rows):
                    s = 0 if rows == P else 1
                    dve.wait_ge(weighed, t + 1)
                    dve.wait_ge(x_in[b], (t - b) * 8 + 16)
                    dve.wait_ge(out_[b], (t - b) * 8)
                    dve.scalar_tensor_tensor(z[0:rows, b], y[0:rows, b, 1, :], share_at(t, rows, 1), y[0:rows, b, 0, :], ALU.mult, ALU.add)
                    dve.drain()
                    dve.tensor_tensor(z[0:rows, b], z[0:rows, b], gate[0:rows, s], ALU.mult)
                    dve.drain()
                    if not final:
                        dve.tensor_tensor(z[0:rows, b], z[0:rows, b], x[0:rows, b], ALU.add).then_inc(done, 1)
                        return
                    dve.tensor_tensor(z[0:rows, b], z[0:rows, b], x[0:rows, b], ALU.add).then_inc(added, 1)
                    dve.wait_ge(rstd, t + 1)
                    dve.scalar_tensor_tensor(z[0:rows, b], z[0:rows, b], rs[0:rows, b:b + 1], g_final[0:rows], ALU.mult, ALU.mult).then_inc(done, 1)
                two_by_two(dve, body)


WB = 2 * P
NQ = SEQ // WB
GELU_K = math.sqrt(2.0 / math.pi)
GELU_C = 0.044715


def phase_recurrent(nc, T, src, dst):
    with ExitStack() as ctx, Semaphores(nc, T["whole_run"]) as sems:
        def sb(name, shape, dt=F32):
            return ctx.enter_context(nc.sbuf_tensor("recurrent_" + name, shape, dt))

        def sem(name):
            return sems("recurrent_" + name)

        ident = T["ident"]
        w_in = sb("w_in", [P, KC, 2 * D])
        w_out = sb("w_out", [P, KC, D])
        w_a = sb("w_a", [P, KC, P])
        w_x = sb("w_x", [P, KC, P])
        param_rows = sb("param_rows", [8 * KC, P])
        par = sb("par", [P, 8, KC])
        sp = sb("sp", [P, 8, KC])
        state_rows = sb("state_rows", [NS * CONV_W, D])
        state = sb("state", [P, KC, NS * CONV_W])
        gain = sb("gain", [P, D])
        shift = sb("shift", [P, D])
        gate = sb("gate", [P, D])
        x = sb("x", [P, 2, D])
        res = sb("res", [P, D])
        h = sb("h", [P, D])
        hT = sb("hT", [P, KC, WB])
        squares = sb("squares", [P, D], BF16)
        ss = sb("ss", [P, 2])
        rs = sb("rs", [P, 2])
        xcat = sb("xcat", [P, 2, 4 + WB])
        xc = sb("xc", [P, 2, WB])
        gx = sb("gx", [P, 2, WB])
        thr = sb("thr", [P, 2, WB])
        thi = sb("thi", [P, 2, WB])
        a = sb("a", [P, KC, WB])
        root = sb("root", [P, KC, WB])
        v = sb("v", [P, KC, WB])
        g = sb("g", [P, KC, WB])
        carry = sb("carry", [P, CONV_W - 1, KC])
        last_h = sb("last_h", [P, KC])
        xb_s = sb("xb_s", [P, KC, NS])
        h_s = sb("h_s", [P, KC, NS])
        out = sb("out", [P, D])
        norm_g_s = sb("norm_g_s", [NS, D])
        ends = sb("ends", [KC * NS, 2, P])
        end_p = sb("end_p", [KC, 4, P])
        psT = ctx.enter_context(nc.psum_tensor("recurrent_psT", [P, KC, P], F32))
        psAB = ctx.enter_context(nc.psum_tensor("recurrent_psAB", [P, 2, 2, WB], F32))
        psRI = ctx.enter_context(nc.psum_tensor("recurrent_psRI", [P, 2, 2, WB], F32))
        psO = ctx.enter_context(nc.psum_tensor("recurrent_psO", [P, 2, 512], F32))
        (const_in, mod_in, squared, rstd, x_used, h_turned, hT_ready, ab_done, xb_copied, gx_squared, p_done, gth_done,
         gelu_done, conv_done, ri_done, a_done, v_done, sqrt_done, y_done, out_done, o_taken, res_in, res_done, res_out,
         pool_chain, consts, ends_turned, ends_done, ends_out, spare, mod_s) = (sem(n) for n in (
             "const_in", "mod_in", "squared", "rstd", "x_used", "h_turned", "hT_ready", "ab_done", "xb_copied",
             "gx_squared", "p_done", "gth_done", "gelu_done", "conv_done", "ri_done", "a_done", "v_done", "sqrt_done",
             "y_done", "out_done", "o_taken", "res_in", "res_done", "res_out", "pool_chain", "consts", "ends_turned",
             "ends_done", "ends_out", "spare", "mod_s"))
        x_in = [sem("x_in0"), sem("x_in1")]

        def blocks(eng, body, enter=None):
            with eng.Fori(0, NQ) as q:
                body(q, WB, P)
            body(NQ, NS, NS)

        def tiles(q, rows):
            return [(q * 2 + i, i) for i in range(2)] if rows == P else [(2 * NQ, 0)]

        def tile_rows(name, t, rows):
            return T[name][bass.ds(t * P, P)] if rows == P else T[name][SEQ:SEQ + NS]

        with nc.Block() as block:
            @block.sync
            def _(sy):
                def modulation(chunk, tile_, row, rows, s):
                    for half in range(2):
                        part = T["mods"][1, chunk * 2 + half, row:row + rows, :]
                        sy.dma_start(tile_[0:(P if rows == 1 else rows), half * 512:half * 512 + 512],
                                     part.broadcast_to([P, 512]) if rows == 1 else part).then_inc(s, 16)
                for n, name in enumerate(("rec_conv_w", "rec_conv_b", "rec_b_a", "rec_b_x", "rec_lambda")):
                    at = 0 if n == 0 else (CONV_W + n - 1) * KC
                    size = CONV_W * KC if n == 0 else KC
                    sy.dma_start(param_rows[at:at + size, :], T[name].rearrange("v (c p) -> (v c) p", p=P)).then_inc(const_in, 16)
                sy.dma_start(state_rows[0:NS * (CONV_W - 1), :], T["state_conv"].rearrange("b j d -> (b j) d")).then_inc(const_in, 16)
                sy.dma_start(state_rows[NS * (CONV_W - 1):, :], T["state_h"]).then_inc(const_in, 16)
                modulation(1, gain, 0, 1, mod_in)
                modulation(0, shift, 0, 1, mod_in)
                modulation(2, gate, 0, 1, mod_in)
                sy.dma_start(h[:, :], T["norm_mix_g"][1:2, :].broadcast_to([P, D])).then_inc(mod_in, 16)
                for k in range(KC):
                    sy.dma_start(w_in[:, k, :], T["rec_w_in"][k * P:(k + 1) * P, :]).then_inc(const_in, 16)
                sy.dma_start(w_a[:, :, :], T["rec_w_a"].rearrange("c i o -> i c o")).then_inc(const_in, 16)
                sy.dma_start(w_x[:, :, :], T["rec_w_x"].rearrange("c i o -> i c o")).then_inc(const_in, 16)
                for k in range(KC):
                    sy.dma_start(w_out[:, k, :], T["rec_w_out"][k * P:(k + 1) * P, :]).then_inc(const_in, 16)

                def body(q, W, rows):
                    for t, i in tiles(q, rows):
                        sy.wait_ge(x_used, t + 1)
                        sy.dma_start(x[0:rows, i], tile_rows(src, t, rows)).then_inc(x_in[i], 16)
                        if rows == NS:
                            sy.wait_ge(mod_s, 1)
                            modulation(1, gain, 1, NS, mod_in)
                            modulation(0, shift, 1, NS, mod_in)
                            sy.dma_start(norm_g_s[:, :], T["norm_mix_g"][1:2, :].broadcast_to([NS, D])).then_inc(mod_in, 16)
                            sy.wait_ge(res_done, 2 * NQ)
                            modulation(2, gate, 1, NS, mod_in)
                    for t, i in tiles(q, rows):
                        sy.wait_ge(res_done, t)
                        sy.dma_start(res[0:rows, :], tile_rows(src, t, rows)).then_inc(res_in, 16)
                blocks(sy, body)
                sy.wait_ge(ends_done, 2)
                sy.dma_start(T["h_prompt"].rearrange("a (c p) -> (a c) p", p=P), end_p[:, 3, :]).then_inc(ends_out, 16)
                for j in range(CONV_W - 1):
                    sy.dma_start(T["conv_prompt"][j:j + 1, :].rearrange("a (c p) -> (a c) p", p=P), end_p[:, j, :]).then_inc(ends_out, 16)
                for c in range(KC):
                    sy.dma_start(T["h_sample"][:, c * P:(c + 1) * P], ends[c * NS:(c + 1) * NS, 0, :]).then_inc(ends_out, 16)
                    sy.dma_start(T["conv_sample"][:, CONV_W - 2, c * P:(c + 1) * P], ends[c * NS:(c + 1) * NS, 1, :]).then_inc(ends_out, 16)
                sy.dma_start(T["conv_sample"][:, 0:CONV_W - 2, :], T["state_conv"][:, 1:CONV_W - 1, :]).then_inc(ends_out, 16)
                sy.wait_ge(ends_out, 16 * (1 + CONV_W - 1 + 2 * KC + 1))

            @block.gpsimd
            def _(pool):
                link = Chain(pool, pool_chain)

                def body(q, W, rows):
                    for t, i in tiles(q, rows):
                        pool.wait_ge(squared, t + 1)
                        norm_rstd(pool, link, rs[0:rows, i:i + 1], ss[0:rows, i:i + 1], T["power"][0:rows]).then_inc(rstd, 1)
                with pool.Fori(0, NQ) as q:
                    link.enter(q, 2)
                    body(q, WB, P)
                    link.leave(NQ)
                body(NQ, NS, NS)

            @block.scalar
            def _(act):
                act.sem_inc(a_done, 2)
                act.sem_inc(xb_copied, 2)
                act.wait_ge(consts, 1)
                act.activation(sp[:, 1, :], sp[:, 1, :], ACT.Exp, scale=-1.0).then_inc(consts, 1)
                act.wait_ge(consts, 3)

                def body(q, W, rows):
                    for t, i in tiles(q, rows):
                        act.drain()
                        act.wait_ge(x_in[i], 16 * (q + 1))
                        act.activation(squares[0:rows, :], x[0:rows, i], ACT.Square, scale=D ** -0.5, accum_out=ss[0:rows, i:i + 1]).then_inc(squared, 1)
                    for t, i in tiles(q, rows):
                        act.wait_ge(h_turned, t + 1)
                        act.wait_ge(ab_done, q * KC)
                        act.activation(hT[:, :, i * P:i * P + rows], psT[:, :, 0:rows], ACT.Copy).then_inc(hT_ready, 1)

                    def gates(c):
                        n = q * KC + c
                        act.wait_ge(ri_done, 2 + n + 1)
                        act.wait_ge(v_done, n + 1)
                        act.wait_ge(y_done, q * KC)
                        act.activation(thr[:, c % 2, 0:W], psRI[:, c % 2, 0, 0:W], ACT.Tanh, scale=0.5, bias=par[:, 5, c:c + 1])
                        act.activation(thi[:, c % 2, 0:W], psRI[:, c % 2, 1, 0:W], ACT.Tanh, scale=0.5, bias=par[:, 6, c:c + 1])
                        act.drain()
                        act.activation(a[:, c, 0:W], thr[:, c % 2, 0:W], ACT.Exp, scale=sp[:, 5, c:c + 1], bias=sp[:, 5, c:c + 1])
                        act.activation(root[:, c, 0:W], thr[:, c % 2, 0:W], ACT.Tanh, scale=sp[:, 6, c:c + 1], bias=sp[:, 6, c:c + 1])
                        act.drain().then_inc(a_done, 1)
                    for c in range(KC):
                        n = q * KC + c
                        act.wait_ge(ab_done, n + 1)
                        act.wait_ge(conv_done, n + 1)
                        act.activation(xcat[:, c % 2, 4:4 + W], psAB[:, c % 2, 1, 0:W], ACT.Copy).then_inc(xb_copied, 1)
                        act.wait_ge(gelu_done, n + 1)
                        act.activation(gx[:, c % 2, 0:W], psAB[:, c % 2, 0, 0:W], ACT.Square).then_inc(gx_squared, 1)
                        act.wait_ge(p_done, n + 1)
                        act.activation(gx[:, c % 2, 0:W], gx[:, c % 2, 0:W], ACT.Tanh).then_inc(gth_done, 1)
                        if c:
                            gates(c - 1)
                    gates(KC - 1)
                    act.activation(root[:, :, 0:W], root[:, :, 0:W], ACT.Sqrt).then_inc(sqrt_done, 1)
                    for t, i in tiles(q, rows):
                        act.wait_ge(res_done, t + 1)
                        act.dma_start(tile_rows(dst, t, rows), out[0:rows, :]).then_inc(res_out, 16)

                blocks(act, body)
                act.wait_ge(res_out, 16 * (2 * NQ + 1))

            @block.vector
            def _(dve):
                dve.sem_inc(x_used, 2)
                dve.sem_inc(gelu_done, 2)
                dve.sem_inc(conv_done, 2)
                dve.sem_inc(v_done, 2)
                dve.sem_inc(o_taken, 2)
                dve.memset(carry[:, :, :], 0.0)
                dve.memset(last_h[:, :], 0.0)
                dve.wait_ge(ends_turned, 1)
                dve.tensor_copy(par[:, :, :], psT[:, 0:1, 0:8 * KC].rearrange("p a (v c) -> p (a v) c", c=KC))
                dve.drain()
                dve.tensor_scalar(sp[:, 0, :], par[:, 7, :], -1.0, 0.0, ALU.mult, ALU.max)
                dve.drain()
                dve.scalar_tensor_tensor(sp[:, 1, :], sp[:, 0, :], 2.0, par[:, 7, :], ALU.mult, ALU.add).then_inc(consts, 1)
                dve.tensor_scalar(par[:, 5:7, :], par[:, 5:7, :], 0.5, None, ALU.mult)
                dve.wait_ge(consts, 2)
                dve.tensor_scalar(sp[:, 2, :], sp[:, 1, :], 2.0, None, ALU.add)
                dve.drain()
                dve.reciprocal(sp[:, 2, :], sp[:, 2, :])
                dve.drain()
                dve.tensor_tensor(sp[:, 1, :], sp[:, 1, :], sp[:, 2, :], ALU.mult)
                dve.drain()
                dve.tensor_tensor(sp[:, 2, :], sp[:, 1, :], sp[:, 1, :], ALU.mult)
                dve.memset(sp[:, 3, :], 2.0 / 21)
                dve.drain()
                for n in range(19, 0, -2):
                    dve.tensor_tensor(sp[:, 3, :], sp[:, 3, :], sp[:, 2, :], ALU.mult)
                    dve.drain()
                    dve.tensor_scalar(sp[:, 3, :], sp[:, 3, :], 2.0 / n, None, ALU.add)
                    dve.drain()
                dve.tensor_tensor(sp[:, 3, :], sp[:, 3, :], sp[:, 1, :], ALU.mult)
                dve.drain()
                dve.tensor_tensor(sp[:, 3, :], sp[:, 3, :], sp[:, 0, :], ALU.add)
                dve.drain()
                dve.tensor_scalar(sp[:, 5, :], sp[:, 3, :], -RG_C / 2, None, ALU.mult)
                dve.tensor_scalar(sp[:, 6, :], sp[:, 3, :], RG_C / 4, None, ALU.mult)
                dve.drain().then_inc(consts, 1)
                dve.wait_ge(ends_turned, 2)
                dve.tensor_copy(state[:, :, :], psAB[:, 0, 0, :].rearrange("p (k s) -> p k s", k=KC)).then_inc(consts, 1)
                dve.wait_ge(mod_in, 16 * 7)
                dve.tensor_tensor(gain[:, :], gain[:, :], h[:, :], ALU.mult)
                dve.drain()

                def body(q, W, rows):
                    if rows == NS:
                        dve.drain().then_inc(mod_s, 1)
                        dve.wait_ge(mod_in, 16 * 14)
                        dve.tensor_tensor(gain[0:NS, :], gain[0:NS, :], norm_g_s[:, :], ALU.mult)
                        dve.drain()
                    for t, i in tiles(q, rows):
                        dve.wait_ge(rstd, t + 1)
                        dve.wait_ge(h_turned, t)
                        dve.scalar_tensor_tensor(h[0:rows, :], x[0:rows, i], rs[0:rows, i:i + 1], gain[0:rows, :], ALU.mult, ALU.mult)
                        dve.drain()
                        dve.tensor_tensor(h[0:rows, :], h[0:rows, :], shift[0:rows, :], ALU.add).then_inc(x_used, 1)

                    def weigh(c):
                        n = q * KC + c
                        dve.wait_ge(a_done, 2 + n + 1)
                        dve.scalar_tensor_tensor(thi[:, c % 2, 0:W], thi[:, c % 2, 0:W], 1.0, xc[:, c % 2, 0:W], ALU.add, ALU.mult)
                        dve.drain()
                        dve.scalar_tensor_tensor(v[:, c, 0:W], a[:, c, 0:W], 1.0, thi[:, c % 2, 0:W], ALU.add, ALU.mult).then_inc(v_done, 1)
                    for c in range(KC):
                        n = q * KC + c
                        cat, o = xcat[:, c % 2, :], xc[:, c % 2, 0:W]
                        dve.wait_ge(xb_copied, 2 + n + 1)
                        dve.wait_ge(ri_done, n + 1)
                        if rows == P:
                            dve.tensor_copy(cat[:, 1:4], carry[:, :, c])
                            dve.drain()
                            taps = [cat[:, 1 + j:1 + j + W] for j in range(CONV_W)]
                        else:
                            old = state[:, c, 0:NS * (CONV_W - 1)].rearrange("p (b j) -> p j b", j=CONV_W - 1)
                            taps = [old[:, j, :] for j in range(CONV_W - 1)] + [cat[:, 4:4 + W]]
                        dve.tensor_scalar(o, taps[0], par[:, 0, c:c + 1], par[:, 4, c:c + 1], ALU.mult, ALU.add)
                        if rows == P:
                            dve.tensor_copy(carry[:, :, c], cat[:, 1 + W:4 + W])
                        else:
                            dve.tensor_copy(xb_s[:, c, :], cat[:, 4:4 + W])
                        dve.drain()
                        for j in range(1, CONV_W):
                            dve.scalar_tensor_tensor(o, taps[j], par[:, j, c:c + 1], o, ALU.mult, ALU.add)
                            dve.drain()
                        dve.sem_inc(conv_done, 1)
                        dve.wait_ge(gx_squared, n + 1)
                        dve.tensor_scalar(gx[:, c % 2, 0:W], gx[:, c % 2, 0:W], GELU_K * GELU_C, GELU_K, ALU.mult, ALU.add)
                        dve.drain()
                        dve.tensor_tensor(gx[:, c % 2, 0:W], gx[:, c % 2, 0:W], psAB[:, c % 2, 0, 0:W], ALU.mult).then_inc(p_done, 1)
                        if c:
                            weigh(c - 1)
                        dve.wait_ge(gth_done, n + 1)
                        dve.scalar_tensor_tensor(g[:, c, 0:W], gx[:, c % 2, 0:W], 1.0, psAB[:, c % 2, 0, 0:W], ALU.add, ALU.mult).then_inc(gelu_done, 1)
                    weigh(KC - 1)
                    dve.drain()
                    dve.wait_ge(sqrt_done, q + 1)
                    dve.scalar_tensor_tensor(v[:, :, 0:W], root[:, :, 0:W], 0.5, v[:, :, 0:W], ALU.mult, ALU.mult)
                    dve.drain()
                    for c in range(KC):
                        if rows == P:
                            dve.tensor_tensor_scan(root[:, c, 0:W], a[:, c, 0:W], v[:, c, 0:W], last_h[:, c:c + 1], ALU.mult, ALU.add)
                            dve.drain()
                        else:
                            old = state[:, c, NS * (CONV_W - 1):]
                            dve.tensor_tensor(root[:, c, 0:W], a[:, c, 0:W], old, ALU.mult)
                            dve.drain()
                            dve.tensor_tensor(root[:, c, 0:W], root[:, c, 0:W], v[:, c, 0:W], ALU.add)
                            dve.drain()
                            dve.tensor_copy(h_s[:, c, :], root[:, c, 0:W])
                        dve.scalar_tensor_tensor(g[:, c, 0:W], g[:, c, 0:W], 0.5, root[:, c, 0:W], ALU.mult, ALU.mult).then_inc(y_done, 1)
                    if rows == P:
                        dve.tensor_copy(last_h[:, :], root[:, :, W - 1:W].rearrange("p c a -> p (c a)"))
                    for t, i in tiles(q, rows):
                        dve.wait_ge(res_in, 16 * (t + 1))
                        dve.wait_ge(res_out, 16 * t)
                        if rows == NS:
                            dve.wait_ge(mod_in, 16 * 14)
                        for half in range(2):
                            cols = slice(half * 512, half * 512 + 512)
                            dve.wait_ge(out_done, 2 * t + half + 1)
                            dve.tensor_tensor(out[0:rows, cols], psO[0:rows, half, :], gate[0:rows, cols], ALU.mult).then_inc(o_taken, 1)
                        dve.drain()
                        dve.tensor_tensor(out[0:rows, :], out[0:rows, :], res[0:rows, :], ALU.add).then_inc(res_done, 1)
                blocks(dve, body)
                dve.drain().then_inc(ends_done, 1)
                dve.wait_ge(ends_turned, 3)
                dve.tensor_copy(ends[:, :, :], psT[0:KC * NS, 0:2, :])
                dve.tensor_copy(end_p[:, :, :], psO[0:KC, 0, :].rearrange("p (j n) -> p j n", n=P))
                dve.drain().then_inc(ends_done, 1)

            @block.tensor
            def _(pe):
                pe.sem_inc(ri_done, 2)
                pe.wait_ge(const_in, 16 * (7 + 2 * KC + 2))
                pe.transpose(psT[:, 0, 0:8 * KC], param_rows[:, :], ident[0:8 * KC, 0:8 * KC]).then_inc(ends_turned, 1)
                for k in range(KC):
                    last = pe.transpose(psAB[:, 0, 0, k * 32:(k + 1) * 32], state_rows[:, k * P:(k + 1) * P], ident[0:32, 0:32])
                last.then_inc(ends_turned, 1)
                pe.wait_ge(consts, 4)

                def body(q, W, rows):
                    for t, i in tiles(q, rows):
                        pe.wait_ge(x_used, 2 + t + 1)
                        pe.wait_ge(hT_ready, t)
                        pe.sem_inc(spare, 1)
                        for k in range(KC):
                            last = pe.transpose(psT[:, k, 0:rows], h[0:rows, k * P:(k + 1) * P], ident[0:rows, 0:rows])
                        last.then_inc(h_turned, 1)
                        if i == 1 or rows == NS:
                            pe.wait_ge(hT_ready, t + 1)

                    def recur(c):
                        n = q * KC + c
                        pe.wait_ge(conv_done, 2 + n + 1)
                        pe.wait_ge(a_done, n + 1)
                        pe.matmul(psRI[:, c % 2, 0, 0:W], w_a[:, c, :], xc[:, c % 2, 0:W], start=True, stop=True)
                        pe.matmul(psRI[:, c % 2, 1, 0:W], w_x[:, c, :], xc[:, c % 2, 0:W], start=True, stop=True).then_inc(ri_done, 1)
                    for c in range(KC):
                        n = q * KC + c
                        pe.wait_ge(xb_copied, n + 1)
                        pe.wait_ge(gelu_done, n + 1)
                        for part in (1, 0):
                            for k in range(KC):
                                last = pe.matmul(psAB[:, c % 2, part, 0:W], w_in[:, k, part * D + c * P:part * D + (c + 1) * P],
                                                 hT[:, k, 0:W], start=(k == 0), stop=(k == KC - 1))
                        last.then_inc(ab_done, 1)
                        if c:
                            recur(c - 1)
                    recur(KC - 1)
                    pe.wait_ge(y_done, q * KC + KC)
                    for t, i in tiles(q, rows):
                        for half in range(2):
                            pe.wait_ge(o_taken, 2 * t + half + 1)
                            for k in range(KC):
                                last = pe.matmul(psO[0:rows, half, :], g[:, k, i * P:i * P + rows], w_out[:, k, half * 512:half * 512 + 512],
                                                 start=(k == 0), stop=(k == KC - 1))
                            last.then_inc(out_done, 1)
                blocks(pe, body)
                pe.wait_ge(ends_done, 1)
                pe.transpose(psT[0:KC * NS, 0, :], h_s[:, :, :].rearrange("p c b -> p (c b)"), ident[:, :])
                pe.transpose(psT[0:KC * NS, 1, :], xb_s[:, :, :].rearrange("p c b -> p (c b)"), ident[:, :])
                for j in range(CONV_W - 1):
                    pe.transpose(psO[0:KC, 0, j * P:(j + 1) * P], carry[:, j, :], ident[:, :])
                pe.transpose(psO[0:KC, 0, 3 * P:4 * P], last_h[:, :], ident[:, :]).then_inc(ends_turned, 1)


def build(nc, T):
    with ExitStack() as stack:
        T["whole_run"] = stack
        def keep(name, shape, dt=F32):
            T[name] = stack.enter_context(nc.sbuf_tensor(name, shape, dt))
        keep("ident", [P, P])
        keep("power", [P, 3])
        phase_modulation(nc, T)
        with ExitStack() as attn:
            for name, shape in (("KT", [P, NKV // 2, SEQ]), ("kiT", [P, 2, SEQ]), ("V1", [P, NT, NKV, P])):
                T[name] = attn.enter_context(nc.sbuf_tensor(name, shape, F32))
            phase_project(nc, T)
            phase_attend(nc, T)
        phase_sample_index(nc, T)
        phase_sample_attend(nc, T)
        keep("dest", [P, NT + 1, 2], I32)
        keep("share", [P, NT + 1, 2])
        keep("blocks", [1, NB], I32)
        phase_route(nc, T, 0, "xa")
        phase_experts(nc, T, 0)
        phase_combine(nc, T, 0, "xa", "xb", False)
        phase_recurrent(nc, T, "xb", "xa")
        phase_route(nc, T, 1, "xa")
        phase_experts(nc, T, 1)
        phase_combine(nc, T, 1, "xa", None, True)


_INS = ["x_prompt", "x_sample", "cache_k", "cache_v", "cache_kidx", "state_h", "state_conv", "page_table",
        "c_prompt", "c_sample", "ada_w", "ada_b", "norm_mix_g", "norm_ffn_g", "norm_final_g",
        "attn_w_in", "attn_w_out", "rec_w_in", "rec_conv_w", "rec_conv_b", "rec_w_a", "rec_b_a",
        "rec_w_x", "rec_b_x", "rec_lambda", "rec_w_out", "moe_w_group", "moe_b_group",
        "moe_w_expert", "moe_b_expert", "moe_w1", "moe_w2"]
_SHAPES = {
    "x_prompt": (SEQ, D), "x_sample": (NS, D), "state_h": (NS, D), "state_conv": (NS, CONV_W - 1, D),
    "c_prompt": (1, D), "c_sample": (NS, D), "attn_w_in": (D, C_END), "attn_w_out": (D, D),
    "rec_w_in": (D, 2 * D), "rec_conv_w": (CONV_W, D), "rec_conv_b": (1, D),
    "rec_w_a": (KC, P, P), "rec_b_a": (1, D), "rec_w_x": (KC, P, P), "rec_b_x": (1, D), "rec_lambda": (1, D),
    "rec_w_out": (D, D), "norm_final_g": (1, D),
}
_OUTS = [("y_prompt", (SEQ, D), (1, SEQ, D)), ("y_sample", (NS, D), (NS, 1, D)),
         ("k_prompt", (SEQ, NKV * DH), (1, 1, SEQ, NKV, DH)), ("v_prompt", (SEQ, NKV * DH), (1, 1, SEQ, NKV, DH)),
         ("kidx_prompt", (SEQ, IDIM), (1, 1, SEQ, IDIM)), ("h_prompt", (1, D), (1, 1, D)),
         ("conv_prompt", (CONV_W - 1, D), (1, 1, CONV_W - 1, D)),
         ("k_sample", (NS, NKV * DH), (1, NS, 1, NKV, DH)), ("v_sample", (NS, NKV * DH), (1, NS, 1, NKV, DH)),
         ("kidx_sample", (NS, IDIM), (1, NS, 1, IDIM)), ("h_sample", (NS, D), (1, NS, D)),
         ("conv_sample", (NS, CONV_W - 1, D), (1, NS, CONV_W - 1, D))]


def rope_table():
    pos = np.concatenate([np.arange(SEQ), np.full(NS, PAST)]).astype(np.float32)
    inv = np.exp(np.float32(-math.log(500000.0)) * np.arange(HALF, dtype=np.float32) * np.float32(2.0 / ROT))
    ang = pos[:, None] * inv[None, :].astype(np.float32)
    return np.concatenate([np.cos(ang), np.cos(ang), -np.sin(ang), np.sin(ang)], axis=1).astype(np.float32)


def kernel(**inputs):
    import numpy as _np
    import concourse.bacc as _bacc
    from concourse.bass_utils import run_bass_kernel_spmd as _run

    nc = _bacc.Bacc("TRN2", target_bir_lowering=False, num_devices=1)
    arrays, T = {}, {}
    for name in _INS:
        a = _np.ascontiguousarray(inputs[name])
        if name in _SHAPES:
            a = a.reshape(_SHAPES[name])
        if name.startswith("cache"):
            a = a.reshape(a.shape[1], PAGE, -1)
        arrays[name + "_in"] = a
        T[name] = nc.dram_tensor(name + "_in", a.shape, mybir.dt.from_np(a.dtype), kind="ExternalInput").ap()
    arrays["rope_in"] = rope_table()
    T["rope"] = nc.dram_tensor("rope_in", (SEQ + NS, 2 * ROT), F32, kind="ExternalInput").ap()
    for name, shape, _ in _OUTS:
        T[name] = nc.dram_tensor(name + "_out", shape, F32, kind="ExternalOutput").ap()
    for name, shape, dt in (("mods", (2, 12, 1 + NS, 512), F32), ("qs", (SEQ + NS, C_K + 520), F32), ("xa", (SEQ + NS, D), F32), ("scores_s", (NS * SLOTS, P), F32),
                            ("hide_s", (NS, NKEY), F32), ("o_s", (NS, D), F32), ("xb", (NTOK, D), F32), ("hs", (NTOK, D), F32),
                            ("yb", (NB * BLK, D), F32), ("row_tok", (NB * BLK, 1), I32)):
        T[name] = nc.dram_tensor(name + "_scratch", shape, dt).ap()
    build(nc, T)
    r = _run(nc, [arrays], core_ids=[0])
    return tuple(r.results[0][name + "_out"].reshape(shape) for name, _, shape in _OUTS)
```

```python
import math
from contextlib import ExitStack

import concourse.bass as bass
import numpy as np
from concourse import mybir

F32 = mybir.dt.float32
BF16 = mybir.dt.bfloat16
I32 = mybir.dt.int32
ALU = mybir.AluOpType
ACT = mybir.ActivationFunctionType
AX = mybir.AxisListType

P = 128
D = 1024
KC = D // P
SEQ = 2048
NT = SEQ // P
NS = 8
PAST = 2048
PAGE = 128
NPAGE = PAST // PAGE
H, DH, NKV = 16, 64, 4
GQ = H // NKV
IH, IDIM = 8, 64
IDX_SCALE = float((IH * IDIM) ** -0.5)
TOPK = 256
ROT = DH // 4
HALF = ROT // 2
C_K, C_V, C_QI, C_KI, C_WI, C_END = 1024, 1280, 1536, 2048, 2112, 2120
EPS = 1e-6
CONV_W = 4
RG_C = 8.0
NE, NG, EPG = 32, 4, 8
FE = 256
BLK = 128
NTOK = SEQ + NS
NB = -(-(2 * NTOK) // BLK) + NE
NPAIR = -(-NB // 2)
MIN_BLOCKS = 2 * -(-(2 * NTOK) // (2 * BLK))
NBR = 2 * NPAIR + 2
PLAN_START, PLAN_LAST, PLAN_END = NB, NB + NE, NB + NE + 1
MASKED = -1.0e30
TAKEN = -3.0e38
BIG = 1.0e30


class Semaphores:

    def __init__(self, nc, whole_run, pool_dma=()):
        self.nc, self.ctx, self.all = nc, ExitStack(), []
        self.whole_run, self.pool_dma = whole_run, pool_dma

    def __enter__(self):
        return self

    def __call__(self, name):
        held = self.whole_run if name.split("_", 1)[1] in self.pool_dma else self.ctx
        self.all.append(held.enter_context(self.nc.semaphore(name)))
        return self.all[-1]

    def __exit__(self, *failure):
        if failure[0] is None:
            for s in self.all:
                self.nc.sync.sem_clear(s)
            self.nc.all_engine_barrier()
        self.ctx.close()


class Chain:

    def __init__(self, eng, sem):
        self.eng, self.sem, self.base, self.n = eng, sem, 0, 0

    def __call__(self, ins):
        self.n += 1
        ins.then_inc(self.sem, 1)
        self.eng.wait_ge(self.sem, self.base + self.n)

    def enter(self, i, per):
        self.outer, self.per = self.base + self.n, per
        self.base, self.n = self.outer + i * per, 0

    def leave(self, turns):
        assert self.n == self.per, (self.n, self.per)
        self.base, self.n = self.outer + turns * self.per, 0


def two_by_two(eng, body):
    with eng.Fori(0, NT // 2) as j:
        body(j * 2, 0, P)
        body(j * 2 + 1, 1, P)
    body(NT, 0, NS)


def with_next(eng, body):
    body(0, 0, P, P)
    body(1, 1, P, P)
    with eng.Fori(1, NT // 2 - 1) as j:
        body(j * 2, 0, P, P)
        body(j * 2 + 1, 1, P, P)
    body(NT - 2, 0, P, P)
    body(NT - 1, 1, P, NS)
    body(NT, 0, NS, 0)


def rows_of(prompt, sample, t, rows):
    return prompt[bass.ds(t * P, P)] if rows == P else sample[0:NS]


def phase_modulation(nc, T):
    with ExitStack() as ctx, Semaphores(nc, T["whole_run"]) as sems:
        def sb(name, shape, dt=F32):
            return ctx.enter_context(nc.sbuf_tensor("modulation_" + name, shape, dt))

        def sem(name):
            return sems("modulation_" + name)

        R = 1 + NS
        cond = sb("cond", [R, D])
        cond_tanh = sb("cond_tanh", [R, D])
        condT = sb("condT", [P, KC, R])
        bias = sb("bias", [R, 2, 6 * D])
        slab = sb("slab", [P, 4, KC, 512])
        res = sb("res", [R, 2, 512])
        ident = T["ident"]
        psT = ctx.enter_context(nc.psum_tensor("modulation_psT", [P, KC, R], F32))
        ps = ctx.enter_context(nc.psum_tensor("modulation_ps", [P, 2, 512], F32))
        cond_in, bias_in = sem("cond_in"), sem("bias_in")
        slab_in = [sem(f"slab_in{i}") for i in range(4)]
        tanh_done, silu_done, turned, condT_done, bias_done = (sem(n) for n in ("tanh", "silu", "turned", "condT", "biasd"))
        slab_used, summed, res_out0, res_out1 = (sem(n) for n in ("slab_used", "summed", "res_out0", "res_out1"))
        res_out = [res_out0, res_out1]
        ident_done = sem("ident")

        with nc.Block() as block:
            @block.sync
            def _(sp):
                sp.dma_start(cond[0:1, :], T["c_prompt"]).then_inc(cond_in, 16)
                sp.dma_start(cond[1:R, :], T["c_sample"]).then_inc(cond_in, 16)
                for l in range(2):
                    sp.dma_start(bias[:, l, :], T["ada_b"][l:l + 1, :].broadcast_to([R, 6 * D])).then_inc(bias_in, 16)
                for l in range(2):
                    w = T["ada_w"][l].rearrange("(k p) n -> p k n", p=P)
                    with sp.Fori(0, 3) as j:
                        for u in range(4):
                            sp.wait_ge(slab_used, l * 12 + j * 4 + u + 1)
                            sp.dma_start(slab[:, u], w[:, :, bass.ds((j * 4 + u) * 512, 512)]).then_inc(slab_in[u], 16)

            @block.gpsimd
            def _(pool):
                pool.memset(T["power"][:, 0:1], -0.5).then_inc(ident_done, 1)
                pool.memset(T["power"][:, 1:2], 0.5).then_inc(ident_done, 1)
                pool.memset(T["power"][:, 2:3], EPS).then_inc(ident_done, 1)
                pool.memset(ident[:, :], 0.0).then_inc(ident_done, 1)
                pool.wait_ge(ident_done, 4)
                pool.affine_select(out=ident[:, :], in_=ident[:, :], compare_op=ALU.not_equal, fill=1.0,
                                   base=0, pattern=[[-1, P]], channel_multiplier=1).then_inc(ident_done, 1)

            @block.scalar
            def _(act):
                act.wait_ge(cond_in, 32)
                act.activation(cond_tanh[:, :], cond[:, :], ACT.Tanh, scale=0.5).then_inc(tanh_done, 1)
                for l in range(2):
                    with act.Fori(0, 3) as j:
                        for u in range(4):
                            n = j * 4 + u
                            act.wait_ge(summed, 2 + l * 12 + n + 1)
                            act.dma_start(T["mods"][l, bass.ds(n, 1)].rearrange("a r d -> r a d"),
                                          res[:, u % 2:u % 2 + 1, :]).then_inc(res_out[u % 2], 16)
                act.wait_ge(res_out[0], 12 * 16)
                act.wait_ge(res_out[1], 12 * 16)

            @block.vector
            def _(dve):
                dve.sem_inc(summed, 2)
                dve.wait_ge(tanh_done, 1)
                dve.scalar_tensor_tensor(cond[:, :], cond_tanh[:, :], 1.0, cond[:, :], ALU.add, ALU.mult).then_inc(silu_done, 1)
                dve.wait_ge(turned, 1)
                dve.tensor_scalar(condT[:, :, :], psT[:, :, :], 0.5, None, ALU.mult).then_inc(condT_done, 1)
                dve.wait_ge(bias_in, 32)
                for chunk in (1, 4):
                    dve.tensor_scalar(bias[:, :, chunk * D:(chunk + 1) * D], bias[:, :, chunk * D:(chunk + 1) * D],
                                      1.0, None, ALU.add).then_inc(bias_done, 1)
                dve.wait_ge(bias_done, 2)
                for l in range(2):
                    with dve.Fori(0, 3) as j:
                        for u in range(4):
                            n = j * 4 + u
                            dve.wait_ge(slab_used, 4 + l * 12 + n + 1)
                            dve.wait_ge(res_out[u % 2], (l * 6 + j * 2 + u // 2) * 16)
                            dve.tensor_tensor(res[:, u % 2], ps[0:R, u % 2, :], bias[:, l, bass.ds(n * 512, 512)],
                                              ALU.add).then_inc(summed, 1)

            @block.tensor
            def _(pe):
                pe.sem_inc(slab_used, 4)
                pe.wait_ge(silu_done, 1)
                pe.wait_ge(ident_done, 5)
                for k in range(KC):
                    last = pe.transpose(psT[:, k, :], cond[:, k * P:(k + 1) * P], ident[0:R, 0:R])
                last.then_inc(turned, 1)
                pe.wait_ge(condT_done, 1)
                for l in range(2):
                    with pe.Fori(0, 3) as j:
                        for u in range(4):
                            pe.wait_ge(slab_in[u], (l * 3 + j + 1) * 16)
                            pe.wait_ge(summed, l * 12 + j * 4 + u + 1)
                            for k in range(KC):
                                last = pe.matmul(ps[0:R, u % 2, :], condT[:, k, :], slab[:, u, k, :], start=(k == 0), stop=(k == KC - 1))
                            last.then_inc(slab_used, 1)


def norm_rstd(pool, link, rs, ss, power):
    link(pool.tensor_tensor(rs, ss, power[:, 2:3], ALU.add))
    return pool.tensor_tensor(rs, rs, power[:, 0:1], ALU.pow)


def norm_modulate(dve, link, h, x, rs, gain, shift):
    link(dve.scalar_tensor_tensor(h, x, rs, gain, ALU.mult, ALU.mult))
    return dve.tensor_tensor(h, h, shift, ALU.add)


def load_modulation(eng, T, l, chunk, prompt_tile, sample_tile, sem):
    for half in range(2):
        cols = slice(half * 512, half * 512 + 512)
        eng.dma_start(prompt_tile[:, cols], T["mods"][l, chunk * 2 + half, 0:1, :].broadcast_to([P, 512])).then_inc(sem, 16)
        eng.dma_start(sample_tile[0:NS, cols], T["mods"][l, chunk * 2 + half, 1:1 + NS, :]).then_inc(sem, 16)


def phase_project(nc, T):
    with ExitStack() as ctx, Semaphores(nc, T["whole_run"], ("w_in", "out_done0", "out_done1")) as sems:
        def sb(name, shape, dt=F32):
            return ctx.enter_context(nc.sbuf_tensor("project_" + name, shape, dt))

        def sem(name):
            return sems("project_" + name)

        w = sb("w", [P, KC, C_END])
        gain = sb("gain", [P, 2, D])
        shift = sb("shift", [P, 2, D])
        x = sb("x", [P, 2, D])
        h = sb("h", [P, 2, D])
        hT = sb("hT", [P, 2, KC, P])
        proj = sb("proj", [P, 2, C_END])
        rope = sb("rope", [P, NT + 1, 2 * ROT])
        rot = sb("rot", [P, 29, ROT])
        ss = sb("ss", [P, 2])
        rs = sb("rs", [P, 2])
        ident, KT, kiT, V1 = T["ident"], T["KT"], T["kiT"], T["V1"]
        psT = ctx.enter_context(nc.psum_tensor("project_psT", [P, KC, P], F32))
        pj = ctx.enter_context(nc.psum_tensor("project_pj", [P, 4, 512], F32))
        psK = ctx.enter_context(nc.psum_tensor("project_psK", [P, 4, P], F32))

        w_in, mod_in, zeroed = sem("w_in"), sem("mod_in"), sem("zeroed")
        x_in = [sem("x_in0"), sem("x_in1")]
        out_done = [sem("out_done0"), sem("out_done1")]
        squared, x_used, h_turned, hT_ready, proj_done, evac, roped, k_turned, kT_copied, v_copied, spare = (
            sem(n) for n in ("squared", "x_used", "h_turned", "hT_ready", "proj_done", "evac", "roped",
                             "k_turned", "kT_copied", "v_copied", "spare"))
        rstd_done = sem("rstd_done")
        CH = [(0, 512), (512, 1024), (1024, 1536), (1536, 2048), (2048, C_END)]
        NCH = len(CH)

        with nc.Block() as block:
            @block.sync
            def _(sp):
                load_modulation(sp, T, 0, 1, gain[:, 0], gain[:, 1], mod_in)
                load_modulation(sp, T, 0, 0, shift[:, 0], shift[:, 1], mod_in)
                sp.dma_start(rope[:, 0:NT], T["rope"][0:SEQ].rearrange("(t p) r -> p t r", p=P)).then_inc(mod_in, 16)
                sp.dma_start(rope[0:NS, NT], T["rope"][SEQ:SEQ + NS]).then_inc(mod_in, 16)
                sp.dma_start(h[:, 0, :], T["norm_mix_g"][0:1, :].broadcast_to([P, D])).then_inc(mod_in, 16)

                def body(t, b, rows):
                    sp.wait_ge(x_used, t + 1)
                    sp.dma_start(x[0:rows, b], rows_of(T["x_prompt"], T["x_sample"], t, rows)).then_inc(x_in[b], 16)
                two_by_two(sp, body)

            @block.gpsimd
            def _(pool):
                for k in range(KC):
                    pool.dma_start(w[:, k, :], T["attn_w_in"].rearrange("(k p) n -> p k n", p=P)[:, k, :]).then_inc(w_in, 16)
                pool.memset(V1[:, :, :, DH:P], 1.0).then_inc(v_copied, 1)

                def link(_):
                    pool.drain()

                def start(t, b, rows):
                    pool.wait_ge(w_in, 16 * KC)
                    pool.wait_ge(squared, t + 1)
                    norm_rstd(pool, link, rs[0:rows, b:b + 1], ss[0:rows, b:b + 1],
                              T["power"][0:rows]).then_inc(rstd_done, 1)

                def store(t, b, rows):
                    pool.wait_ge(roped, t + 1)
                    pool.wait_ge(w_in, 16 * KC)
                    if rows == P:
                        pool.tensor_copy(V1[:, bass.ds(t, 1), :, 0:DH],
                                         proj[:, b:b + 1, C_V:C_QI].rearrange("p a (n d) -> p a n d", d=DH)).then_inc(v_copied, 1)
                    k_out, v_out, ki_out, q_out = (
                        (T["k_prompt"][bass.ds(t * P, P)], T["v_prompt"][bass.ds(t * P, P)],
                         T["kidx_prompt"][bass.ds(t * P, P)], T["qs"][bass.ds(t * P, P)]) if rows == P else
                        (T["k_sample"][:, :], T["v_sample"][:, :], T["kidx_sample"][:, :], T["qs"][SEQ:SEQ + NS]))
                    for dst, c0, c1 in ((k_out, C_K, C_V), (v_out, C_V, C_QI), (ki_out, C_KI, C_WI),
                                        (q_out[:, 0:C_K], 0, C_K), (q_out[:, C_K:C_K + 512], C_QI, C_KI),
                                        (q_out[:, C_K + 512:C_K + 520], C_WI, C_END)):
                        pool.dma_start(dst, proj[0:rows, b, c0:c1]).then_inc(out_done[b], 16)

                def body(t, b, rows, ahead):
                    if ahead:
                        start(t + 1, 1 - b, ahead)
                    store(t, b, rows)
                start(0, 0, P)
                with_next(pool, body)
                pool.wait_ge(v_copied, 1 + NT)
                for b in range(2):
                    pool.wait_ge(out_done[b], 16 * 6 * (NT // 2 + 1 - b))

            @block.scalar
            def _(act):
                def start(t, b, rows):
                    act.wait_ge(x_in[b], (t - b) * 8 + 16)
                    act.wait_ge(proj_done, t * NCH + NCH)
                    act.activation(hT[0:rows, b].rearrange("p k n -> p (k n)"), x[0:rows, b], ACT.Square, scale=D ** -0.5,
                                   accum_out=ss[0:rows, b:b + 1]).then_inc(squared, 1)

                def keep_turned(t, b, rows):
                    act.wait_ge(h_turned, 2 + t + 1)
                    act.wait_ge(squared, t + 1)
                    act.activation(hT[:, b, :, 0:rows], psT[:, :, 0:rows], ACT.Copy).then_inc(hT_ready, 1)

                def keep_keys(t):
                    act.wait_ge(k_turned, 2 + t + 1)
                    act.activation(KT[:, :, bass.ds(t * P, P)], psK[:, 0:2, :], ACT.Copy).then_inc(kT_copied, 1)
                    act.wait_ge(zeroed, 2)
                    for half in range(2):
                        act.activation(kiT[half * DH:(half + 1) * DH, half, bass.ds(t * P, P)], psK[0:DH, 2, :],
                                       ACT.Copy).then_inc(kT_copied, 1)

                def body(t, b, rows, ahead):
                    if ahead:
                        start(t + 1, 1 - b, ahead)
                    for c, (c0, c1) in enumerate(CH):
                        act.wait_ge(proj_done, 2 * NCH + t * NCH + c + 1)
                        if c == 0:
                            act.wait_ge(out_done[b], (t - b) * 48)
                            act.wait_ge(k_turned, t + 1)
                            act.wait_ge(v_copied, t)
                        bank = c % 4
                        act.activation(proj[0:rows, b, c0:c1], pj[0:rows, bank, 0:c1 - c0], ACT.Copy).then_inc(evac, 1)
                        if c == 1 and not (isinstance(t, int) and t == 0):
                            keep_keys(t - 1)
                        if c == 3 and ahead:
                            keep_turned(t + 1, 1 - b, ahead)
                act.sem_inc(evac, 4)
                start(0, 0, P)
                keep_turned(0, 0, P)
                with_next(act, body)

            @block.vector
            def _(dve):
                def link(_):
                    dve.drain()
                dve.sem_inc(x_used, 2)
                dve.memset(kiT[DH:P, 0, :], 0.0).then_inc(zeroed, 1)
                dve.memset(kiT[0:DH, 1, :], 0.0).then_inc(zeroed, 1)
                dve.wait_ge(mod_in, 16 * 11)
                for b in range(2):
                    link(dve.tensor_tensor(gain[:, b], gain[:, b], h[:, 0], ALU.mult)) if b == 0 else link(
                        dve.tensor_tensor(gain[0:NS, b], gain[0:NS, b], h[0:NS, 0], ALU.mult))

                def normed(t, b, rows):
                    s = 0 if rows == P else 1
                    dve.wait_ge(rstd_done, t + 1)
                    dve.wait_ge(h_turned, 2 + t - 1)
                    norm_modulate(dve, link, h[0:rows, b], x[0:rows, b], rs[0:rows, b:b + 1],
                                  gain[0:rows, s], shift[0:rows, s]).then_inc(x_used, 1)

                def body(t, b, rows, ahead):
                    if ahead:
                        normed(t + 1, 1 - b, ahead)
                    dve.wait_ge(evac, 4 + t * NCH + NCH)
                    for c0, nh, r0 in ((0, H + NKV, 0), (C_QI, IH + 1, H + NKV)):
                        head = proj[0:rows, b, c0:c0 + nh * DH].rearrange("p (h d) -> p h d", d=DH)
                        tmp = rot[0:rows, r0:r0 + nh, :]

                        def table(a):
                            v = rope[0:rows, bass.ds(t, 1), a:a + HALF]
                            return v.broadcast_to([rows, nh, HALF])
                        dve.tensor_tensor(tmp[:, :, 0:HALF], head[:, :, HALF:ROT], table(2 * HALF), ALU.mult)
                        link(dve.tensor_tensor(tmp[:, :, HALF:ROT], head[:, :, 0:HALF], table(3 * HALF), ALU.mult))
                        link(dve.tensor_tensor(head[:, :, 0:HALF], head[:, :, 0:HALF], table(0), ALU.mult))
                        link(dve.tensor_tensor(head[:, :, HALF:ROT], head[:, :, HALF:ROT], table(HALF), ALU.mult))
                        last = dve.tensor_tensor(head[:, :, 0:ROT], head[:, :, 0:ROT], tmp, ALU.add)
                        if r0 == 0:
                            link(last)
                    last.then_inc(roped, 1)
                normed(0, 0, P)
                with_next(dve, body)

            @block.tensor
            def _(pe):
                pe.sem_inc(proj_done, 2 * NCH)
                pe.sem_inc(k_turned, 2)
                pe.sem_inc(h_turned, 2)
                pe.wait_ge(w_in, 16 * KC)

                def turn(t, b, rows):
                    pe.wait_ge(x_used, 2 + t + 1)
                    pe.wait_ge(hT_ready, t)
                    pe.sem_inc(spare, 1)
                    for k in range(KC):
                        last = pe.transpose(psT[:, k, 0:rows], h[0:rows, b, k * P:(k + 1) * P], ident[0:rows, 0:rows])
                    last.then_inc(h_turned, 1)

                def turn_keys(t, b):
                    pe.wait_ge(roped, t + 1)
                    pe.wait_ge(kT_copied, 3 * t)
                    for n in range(NKV // 2):
                        pe.transpose(psK[:, n, :], proj[:, b, C_K + n * P:C_K + (n + 1) * P], ident[:, :])
                    pe.transpose(psK[0:DH, 2, :], proj[:, b, C_KI:C_WI], ident[:, :]).then_inc(k_turned, 1)

                def body(t, b, rows, ahead):
                    pe.wait_ge(hT_ready, t + 1)
                    for c, (c0, c1) in enumerate(CH):
                        bank = c % 4
                        pe.wait_ge(evac, 4 + t * NCH if c < 4 else 4 + t * NCH + 1)
                        for k in range(KC):
                            last = pe.matmul(pj[0:rows, bank, 0:c1 - c0], hT[:, b, k, 0:rows], w[:, k, c0:c1],
                                             start=(k == 0), stop=(k == KC - 1))
                        last.then_inc(proj_done, 1)
                        if c == 1 and not (isinstance(t, int) and t == 0):
                            turn_keys(t - 1, 1 - b)
                        if c == 3 and ahead:
                            turn(t + 1, 1 - b, ahead)
                turn(0, 0, P)
                with_next(pe, body)


def cum(per, t):
    return sum(per[:t])


def phase_attend(nc, T):
    with ExitStack() as ctx, Semaphores(nc, T["whole_run"], ("y_out",)) as sems:
        def sb(name, shape, dt=F32):
            return ctx.enter_context(nc.sbuf_tensor("attend_" + name, shape, dt))

        def sem(name):
            return sems("attend_" + name)

        ident, KT, kiT, V1 = T["ident"], T["KT"], T["kiT"], T["V1"]
        KTb = sb("KTb", [P, NKV // 2, SEQ], BF16)
        w_out = sb("w_out", [P, KC, D])
        gate = sb("gate", [P, D])
        identb4 = sb("identb4", [P, GQ, P], BF16)
        onesb = sb("onesb", [P, P], BF16)
        causal = sb("causal", [P, P])
        q_rows = sb("q_rows", [P, D])
        qi_rows = sb("qi_rows", [P, 520])
        wi = sb("wi", [P, IH])
        qT = sb("qT", [P, H, P])
        qTb = sb("qTb", [P, H, P], BF16)
        qiT = sb("qiT", [P, IH // 2, P])
        score = sb("score", [P, SEQ])
        relu = sb("relu", [P, 4, 512])
        top8 = sb("top8", [P, 8])
        hide = sb("hide", [P, SEQ], BF16)
        mx = sb("mx", [P, H, 2])
        negmax = sb("negmax", [P, H])
        diag = sb("diag", [P, H, P], BF16)
        PT = sb("PT", [P, 4, 512])
        oT = sb("oT", [P, KC, P])
        total = sb("total", [P, KC, P])
        x = sb("x", [P, D])
        y = sb("y", [P, D])
        big = ctx.enter_context(nc.psum_tensor("attend_big", [P, 4, 512], F32))
        flat = big[:, :, :].rearrange("p a n -> p (a n)")
        dots = ctx.enter_context(nc.psum_tensor("attend_dots", [P, 2, 512], F32))
        turned = dots[:, :, :].rearrange("p a (k q) -> p (a k) q", q=P)
        po = ctx.enter_context(nc.psum_tensor("attend_po", [P, 2, 512], F32))

        (const_in, q_in, qi_in, x_in, q_turned, qT_ready, qTb_ready, qi_turned, qiT_ready, unit_filled, maxed, negmax_done,
         diag_done, dotted, relud, summed, scored, hidden, st_filled, exped, pv_done, o_copied, o_normed,
         projected, y_copied, y_done, y_out, consts, spare) = (sem(n) for n in (
             "const_in", "q_in", "qi_in", "x_in", "q_turned", "qT_ready", "qTb_ready", "qi_turned", "qiT_ready", "unit_filled",
             "maxed", "negmax_done", "diag_done", "dotted", "relud", "summed", "scored", "hidden", "st_filled",
             "exped", "pv_done", "o_copied", "o_normed", "projected", "y_copied", "y_done",
             "y_out", "consts", "spare"))
        L = [P * (t + 1) for t in range(NT)]
        U = [H * (1 if l <= 1024 else 2) for l in L]
        I = [IH * -(-l // 512) for l in L]
        S = [NKV * l // P for l in L]

        def pieces(t):
            cuts = [slice(a, min(a + 512, L[t])) for a in range(0, L[t], 512)]
            return [(h * len(cuts) + b, keys) for h in range(IH) for b, keys in enumerate(cuts)]

        def all_chosen(t):
            return L[t] <= TOPK

        with nc.Block() as block:
            @block.sync
            def _(sp):
                for k in range(KC):
                    sp.dma_start(w_out[:, k, :], T["attn_w_out"][k * P:(k + 1) * P, :]).then_inc(const_in, 16)
                for half in range(2):
                    sp.dma_start(gate[:, half * 512:half * 512 + 512],
                                 T["mods"][0, 4 + half, 0:1, :].broadcast_to([P, 512])).then_inc(const_in, 16)
                sp.dma_start(qi_rows[:, :], T["qs"][0:P, D:D + 520]).then_inc(qi_in, 16)
                sp.dma_start(q_rows[:, :], T["qs"][0:P, 0:D]).then_inc(q_in, 16)

                def body(t):
                    if t + 1 < NT:
                        sp.wait_ge(scored, t + 1)
                        sp.wait_ge(qi_turned, t + 1)
                        sp.dma_start(qi_rows[:, :], T["qs"][bass.ds(t * P + P, P), D:D + 520]).then_inc(qi_in, 16)
                        sp.wait_ge(q_turned, t + 1)
                        sp.sem_inc(spare, 1)
                        sp.dma_start(q_rows[:, :], T["qs"][bass.ds(t * P + P, P), 0:D]).then_inc(q_in, 16)
                    sp.wait_ge(y_done, t)
                    sp.dma_start(x[:, :], T["x_prompt"][bass.ds(t * P, P), :]).then_inc(x_in, 16)
                for t in range(NT):
                    body(t)

            @block.gpsimd
            def _(pool):
                pool.memset(onesb[:, :], 1.0).then_inc(consts, 1)
                pool.memset(causal[:, :], 0.0).then_inc(consts, 1)
                pool.wait_ge(consts, 2)
                pool.affine_select(out=causal[:, :], in_=causal[:, :], compare_op=ALU.is_ge, fill=MASKED,
                                   base=0, pattern=[[-1, P]], channel_multiplier=1).then_inc(consts, 1)
                for n in range(GQ):
                    pool.tensor_copy(identb4[:, n, :], ident[:, :]).then_inc(consts, 1)
                for n in range(NKV // 2):
                    pool.tensor_copy(KTb[:, n, :], KT[:, n, :]).then_inc(consts, 1)
                pool.memset(qT[:, :, :], 0.0).then_inc(consts, 1)
                pool.memset(qTb[:, :, :], 0.0).then_inc(consts, 1)

                def body(t):
                    pool.wait_ge(negmax_done, t + 1)
                    pool.tensor_tensor(diag[:, :, :], identb4[:, 0:1, :].broadcast_to([P, H, P]),
                                       negmax[:, :].rearrange("p (h a) -> p h a", a=1).broadcast_to([P, H, P]), ALU.mult).then_inc(diag_done, 1)
                    if t > 0:
                        residual(t - 1)

                def residual(t):
                    pool.wait_ge(y_copied, 2 * (t + 1))
                    pool.tensor_tensor(y[:, :], y[:, :], gate[:, :], ALU.mult)
                    pool.drain()
                    pool.wait_ge(x_in, 16 * (t + 1))
                    pool.tensor_tensor(y[:, :], y[:, :], x[:, :], ALU.add).then_inc(y_done, 1)
                    pool.wait_ge(y_done, t + 1)
                    pool.sem_inc(spare, 1)
                    pool.dma_start(T["xa"][bass.ds(t * P, P), :], y[:, :]).then_inc(y_out, 16)
                pool.wait_ge(const_in, 16 * (KC + 2))
                for t in range(NT):
                    body(t)
                residual(NT - 1)
                pool.wait_ge(y_out, 16 * NT)

            @block.scalar
            def _(act):
                act.sem_inc(relud, 2)
                act.sem_inc(exped, 4)

                def index(t):
                    act.wait_ge(qi_turned, t + 1)
                    act.activation(qiT[:, :, :], dots[:, 0, :].rearrange("p (k q) -> p k q", q=P), ACT.Copy).then_inc(qiT_ready, 1)
                    for k, keys in pieces(t):
                        n = cum(I, t) + k
                        act.wait_ge(dotted, n + 1)
                        act.wait_ge(summed, n + 1)
                        act.activation(relu[:, k % 4, 0:keys.stop - keys.start], dots[:, k % 2, 0:keys.stop - keys.start], ACT.Relu).then_inc(relud, 1)

                def turned_queries(dst, k):
                    n, half = divmod(k, 2)
                    return act.activation(dst[(n % 2) * DH:(n % 2 + 1) * DH, n * GQ + half:(n + 1) * GQ:2, :],
                                          turned[half * DH:(half + 1) * DH, n * GQ // 2:(n + 1) * GQ // 2], ACT.Copy, scale=DH ** -0.5)

                def body(t):
                    act.wait_ge(pv_done, 4 + cum(S, t))
                    for k in range(8):
                        turned_queries(qT, k).then_inc(qT_ready, 1)
                    if t + 1 < NT:
                        index(t + 1)
                    if t > 0:
                        projection(t - 1)

                    def copy_out(n):
                        act.wait_ge(pv_done, 4 + cum(S, t) + (n + 1) * S[t] // NKV)
                        heads = po[:, n % 2, :].rearrange("p (h q) -> p h q", q=P)
                        for half in range(2):
                            for dst, a in ((oT, 0), (total, DH)):
                                act.activation(dst[half * DH:(half + 1) * DH, n * GQ // 2:(n + 1) * GQ // 2, :],
                                               heads[a:a + DH, half:GQ:2, :], ACT.Copy).then_inc(o_copied, 1)
                    per = S[t] // NKV
                    for k in range(S[t]):
                        act.wait_ge(st_filled, cum(S, t) + k + 1)
                        act.wait_ge(pv_done, cum(S, t) + k + 1)
                        act.activation(PT[:, k % 4, :], big[:, k % 4, :], ACT.Exp).then_inc(exped, 1)
                        if k >= 3:
                            next_queries(t, k - 3)
                        for n in range(NKV - 1):
                            if k == (n + 1) * per + 2:
                                copy_out(n)
                    for n in range(NKV):
                        if (n + 1) * per + 2 >= S[t]:
                            copy_out(n)
                    for k in range(max(S[t] - 3, 0), 8):
                        next_queries(t, k)

                def next_queries(t, k):
                    if k < 8 and t + 1 < NT:
                        if k == 0:
                            act.wait_ge(q_turned, t + 2)
                        turned_queries(qTb, k).then_inc(qTb_ready, 1)

                def projection(t):
                    for half in range(2):
                        act.wait_ge(projected, 2 * t + half + 1)
                        if half == 0:
                            act.wait_ge(y_out, 16 * t)
                        act.activation(y[:, half * 512:half * 512 + 512], big[:, 2 + half, :], ACT.Copy).then_inc(y_copied, 1)
                act.wait_ge(consts, 7 + GQ)
                index(0)
                act.wait_ge(q_turned, 1)
                for k in range(8):
                    turned_queries(qTb, k).then_inc(qTb_ready, 1)
                for t in range(NT):
                    body(t)
                projection(NT - 1)

            @block.vector
            def _(dve):
                dve.sem_inc(maxed, 2)
                dve.sem_inc(summed, 4)
                dve.wait_ge(consts, 7 + GQ)

                def normalise(t):
                    dve.wait_ge(o_copied, 4 * NKV * (t + 1))
                    dve.reciprocal(total[:, :, :], total[:, :, :])
                    dve.drain()
                    dve.tensor_tensor(oT[:, :, :], oT[:, :, :], total[:, :, :], ALU.mult).then_inc(o_normed, 1)

                def index(t):
                    n0 = cum(I, t)
                    w = L[t]
                    dve.wait_ge(qi_in, 16 * (t + 1))
                    dve.tensor_scalar(wi[:, :], qi_rows[:, 512:520], IDX_SCALE, None, ALU.mult)
                    dve.drain()
                    for k, keys in pieces(t):
                        h = k // (I[t] // IH)
                        dst, part = score[:, keys], relu[:, k % 4, 0:keys.stop - keys.start]
                        dve.wait_ge(relud, 2 + n0 + k + 1)
                        if h == 0:
                            dve.tensor_scalar(dst, part, wi[:, 0:1], None, ALU.mult).then_inc(summed, 1)
                        else:
                            dve.wait_ge(summed, 4 + n0 + k - I[t] // IH + 1)
                            dve.scalar_tensor_tensor(dst, part, wi[:, h:h + 1], dst, ALU.mult, ALU.add).then_inc(summed, 1)
                    dve.drain()
                    dve.tensor_tensor(score[:, w - P:w], score[:, w - P:w], causal[:, :], ALU.add).then_inc(scored, 1)
                    if not all_chosen(t):
                        with dve.Fori(0, TOPK // 8):
                            dve.drain()
                            dve.max(top8[:, :], score[:, 0:w])
                            dve.drain()
                            dve.match_replace(score[:, 0:w], top8[:, :], score[:, 0:w], TAKEN)
                    dve.drain()
                    dve.wait_ge(pv_done, 4 + n_before(t))
                    if all_chosen(t):
                        dve.memset(hide[:, 0:w], 0.0)
                    else:
                        dve.tensor_scalar(hide[:, 0:w], score[:, 0:w], TAKEN / 2, -BIG, ALU.is_gt, ALU.mult)
                    dve.drain()
                    dve.tensor_tensor(hide[:, w - P:w], hide[:, w - P:w], causal[:, :], ALU.add).then_inc(hidden, 1)

                def n_before(t):
                    return cum(S, t)

                def body(t):
                    nu = U[t] // H
                    for k in range(U[t]):
                        h, u = divmod(k, nu)
                        wide = min(1024, L[t] - 1024 * u)
                        dve.wait_ge(unit_filled, cum(U, t) + k + 1)
                        dve.tensor_reduce(mx[:, h, u:u + 1], flat[:, 1024 * (k % 2):1024 * (k % 2) + wide], AX.X, ALU.max).then_inc(maxed, 1)
                    dve.drain()
                    dve.tensor_reduce(negmax[:, :], mx[:, :, 0:nu], AX.X, ALU.max, negate=True).then_inc(negmax_done, 1)
                    if t > 0:
                        normalise(t - 1)
                    if t + 1 < NT:
                        index(t + 1)
                index(0)
                for t in range(NT):
                    body(t)
                normalise(NT - 1)

            @block.tensor
            def _(pe):
                pe.sem_inc(pv_done, 4)
                pe.wait_ge(consts, 7 + GQ)
                pe.wait_ge(const_in, 16 * (KC + 2))

                def index(t):
                    n0 = cum(I, t)
                    pe.wait_ge(qi_in, 16 * (t + 1))
                    pe.wait_ge(relud, 2 + n0)
                    for k in range(IH // 2):
                        last = pe.transpose(dots[:, 0, k * P:(k + 1) * P], qi_rows[:, k * P:(k + 1) * P], ident[:, :])
                    last.then_inc(qi_turned, 1)
                    pe.wait_ge(qiT_ready, t + 1)
                    for k, keys in pieces(t):
                        h = k // (I[t] // IH)
                        pe.wait_ge(relud, n0 + k + 1)
                        pe.matmul(dots[:, k % 2, 0:keys.stop - keys.start], qiT[:, h // 2, :], kiT[:, h % 2, keys], start=True, stop=True).then_inc(dotted, 1)

                def body(t):
                    pe.wait_ge(qTb_ready, 8 * (t + 1))
                    pe.wait_ge(hidden, t + 1)
                    nu = U[t] // H
                    for k in range(U[t]):
                        h, u = divmod(k, nu)
                        wide = min(1024, L[t] - 1024 * u)
                        pe.wait_ge(maxed, cum(U, t) + k + 1)
                        for b in range(-(-wide // 512)):
                            n = min(512, wide - b * 512)
                            keys = slice(u * 1024 + b * 512, u * 1024 + b * 512 + n)
                            bank = big[:, 2 * (k % 2) + b, 0:n]
                            pe.matmul(bank, identb4[:, 0, :], hide[:, keys], start=True, stop=False)
                            last = pe.matmul(bank, qTb[:, h, :], KTb[:, h // GQ // 2, keys], start=False, stop=True)
                        last.then_inc(unit_filled, 1)
                    pe.wait_ge(qT_ready, 8 * (t + 1))
                    if t + 1 < NT:
                        index(t + 1)
                    if t > 0:
                        project(t - 1)
                    if t + 1 < NT:
                        pe.wait_ge(relud, 2 + cum(I, t + 1) + I[t + 1])
                        turn_queries(t + 1)
                    per = S[t] // NKV
                    pe.wait_ge(diag_done, t + 1)
                    pe.wait_ge(maxed, 2 + cum(U, t) + U[t])
                    pe.wait_ge(y_copied, 2 * t)

                    def transposed(k):
                        n, b = divmod(k, per)
                        pe.wait_ge(exped, cum(S, t) + k + 1)
                        bank = big[:, k % 4, :]
                        keys = slice(b * P, (b + 1) * P)
                        pe.matmul(bank, hide[:, keys], identb4[:, :, :].rearrange("p a q -> p (a q)"), start=True, stop=False)
                        pe.matmul(bank, onesb[:, :], diag[:, n * GQ:(n + 1) * GQ, :].rearrange("p a q -> p (a q)"), start=False, stop=False)
                        pe.matmul(bank, KT[:, n // 2, keys], qT[:, n * GQ:(n + 1) * GQ, :].rearrange("p a q -> p (a q)"),
                                  start=False, stop=True).then_inc(st_filled, 1)

                    def with_values(k):
                        n, b = divmod(k, per)
                        pe.wait_ge(exped, 4 + cum(S, t) + k + 1)
                        if b == 0:
                            pe.wait_ge(o_copied, 4 * (NKV * t + max(n - 1, 0)))
                        pe.matmul(po[:, n % 2, :], V1[:, b, n, :], PT[:, k % 4, :], start=(b == 0), stop=(b == per - 1)).then_inc(pv_done, 1)
                    for k in range(S[t] + 2):
                        if k < S[t]:
                            transposed(k)
                        if k >= 2:
                            with_values(k - 2)

                def turn_queries(t):
                    pe.wait_ge(q_in, 16 * (t + 1))
                    for k in range(KC):
                        last = pe.transpose(turned[:, k, :], q_rows[:, k * P:(k + 1) * P], ident[:, :])
                    last.then_inc(q_turned, 1)

                def project(t):
                    pe.wait_ge(o_normed, t + 1)
                    for half in range(2):
                        for k in range(KC):
                            last = pe.matmul(big[:, 2 + half, :], oT[:, k, :], w_out[:, k, half * 512:half * 512 + 512],
                                             start=(k == 0), stop=(k == KC - 1))
                        last.then_inc(projected, 1)
                index(0)
                pe.wait_ge(relud, 2 + I[0])
                turn_queries(0)
                for t in range(NT):
                    body(t)
                project(NT - 1)


SLOTS = NPAGE + 1
NKEY = SLOTS * P


def load_pages(eng, table, cache, b, dst, sem):
    for j in range(NPAGE):
        page = eng.value_load(table[0:1, bass.ds(b * NPAGE + j, 1)], min_val=0, max_val=cache.shape[0] - 1)
        eng.dma_start(dst[:, j, :], cache[bass.ds(page, 1)].rearrange("a t c -> (a t) c")).then_inc(sem, 16)


def phase_sample_index(nc, T):
    with ExitStack() as ctx, Semaphores(nc, T["whole_run"]) as sems:
        def sb(name, shape, dt=F32):
            return ctx.enter_context(nc.sbuf_tensor("index_" + name, shape, dt))

        def sem(name):
            return sems("index_" + name)

        ident = T["ident"]
        pairs = (SLOTS + 1) // 2
        table = sb("table", [1, NS * NPAGE], I32)
        qi_rows = sb("qi_rows", [NS * IH, IDIM])
        weights = sb("weights", [P, NS, IH])
        kis = sb("kis", [P, 2, 2 * pairs, IDIM])
        kiT = sb("kiT", [P, pairs, P])
        qi2 = sb("qi2", [P, NS, 2 * IH])
        weighed = sb("weighed", [P, SLOTS, IH])
        score = sb("score", [P, NS, SLOTS])
        unseen = sb("unseen", [P, SLOTS])
        turned = sb("turned", [P, 2, P])
        rows = sb("rows", [NS, NKEY])
        top8 = sb("top8", [NS, 8])
        ps_kiT = ctx.enter_context(nc.psum_tensor("index_ps_kiT", [P, 3, 512], F32))
        ps_dot = ctx.enter_context(nc.psum_tensor("index_ps_dot", [P, 512], F32))
        ps_misc = ctx.enter_context(nc.psum_tensor("index_ps_misc", [P, 4, P], F32))
        (table_in, in_, zeroed, kis_used, spare, kiT_ready, dotted, summed, q_turned, q_ready, masked, sc_turned,
         sc_copied, sc_out, rows_in, hidden, hide_out) = (sem(n) for n in (
             "table_in", "in", "zeroed", "kis_used", "spare", "kiT_ready", "dotted", "summed", "q_turned",
             "q_ready", "masked", "sc_turned", "sc_copied", "sc_out", "rows_in", "hidden", "hide_out"))
        kis_in = [sem("kis_in0"), sem("kis_in1")]
        first = 7 * SLOTS

        with nc.Block() as block:
            @block.sync
            def _(sp):
                sp.dma_start(table[0:1, :], T["page_table"].rearrange("b (o j) -> o b j", o=1)).then_inc(table_in, 16)
                for b in range(NS):
                    sp.dma_start(qi_rows[b * IH:(b + 1) * IH, :],
                                 T["qs"][SEQ + b:SEQ + b + 1, D:D + 512].rearrange("a (h d) -> (a h) d", d=IDIM)).then_inc(in_, 16)
                sp.dma_start(weights[:, :, :], T["qs"][SEQ:SEQ + NS, D + 512:D + 520].rearrange("b (o h) -> o b h", o=1)
                             .broadcast_to([P, NS, IH])).then_inc(in_, 16)
                sp.wait_ge(table_in, 16)
                sp.wait_ge(zeroed, 3)
                with sp.Fori(0, NS // 2) as j:
                    for u in range(2):
                        b = j * 2 + u
                        sp.wait_ge(kis_used, b + 1)
                        sp.sem_inc(spare, 1)
                        load_pages(sp, table, T["cache_kidx"], b, kis[:, u], kis_in[u])
                        sp.dma_start(kis[0:1, u, NPAGE, :], T["kidx_sample"][bass.ds(b, 1), :]).then_inc(kis_in[u], 16)
                for k, (a, z) in enumerate(((0, first), (first, NS * SLOTS))):
                    sp.wait_ge(sc_copied, k + 1)
                    sp.dma_start(T["scores_s"][a:z, :], turned[0:z - a, k, :]).then_inc(sc_out, 16)
                sp.wait_ge(sc_out, 32)
                sp.dma_start(rows[:, :], T["scores_s"].rearrange("(b j) k -> b (j k)", b=NS)).then_inc(rows_in, 16)
                sp.wait_ge(hidden, 1)
                sp.dma_start(T["hide_s"], rows[:, :]).then_inc(hide_out, 16)
                sp.wait_ge(hide_out, 16)

            @block.gpsimd
            def _(pool):
                pool.memset(unseen[:, :], 0.0).then_inc(masked, 1)
                pool.wait_ge(masked, 1)
                pool.affine_select(out=unseen[:, :], in_=unseen[:, :], compare_op=ALU.is_ge, fill=MASKED,
                                   base=PAST, pattern=[[-P, SLOTS]], channel_multiplier=-1).then_inc(masked, 1)

            @block.scalar
            def _(act):
                with act.Fori(0, NS) as b:
                    act.wait_ge(kis_used, 2 + b + 1)
                    act.activation(kiT[:, 0:8, :], ps_kiT[:, 0:2, :].rearrange("p a (k q) -> p (a k) q", q=P), ACT.Copy).then_inc(kiT_ready, 1)
                    act.activation(kiT[:, 8, :], ps_kiT[:, 2, 0:P], ACT.Copy).then_inc(kiT_ready, 1)

            @block.vector
            def _(dve):
                dve.memset(kis[:, :, NPAGE:, :], 0.0).then_inc(zeroed, 1)
                dve.memset(qi2[0:DH, :, IH:], 0.0).then_inc(zeroed, 1)
                dve.memset(qi2[DH:P, :, 0:IH], 0.0).then_inc(zeroed, 1)
                dve.wait_ge(in_, 16 * (NS + 1))
                dve.tensor_scalar(weights[:, :, :], weights[:, :, :], IDX_SCALE, None, ALU.mult)
                dve.wait_ge(q_turned, 1)
                for half in range(2):
                    dve.tensor_copy(qi2[half * DH:(half + 1) * DH, :, half * IH:(half + 1) * IH],
                                    ps_misc[0:IDIM, 0, 0:NS * IH].rearrange("p (b h) -> p b h", h=IH)).then_inc(q_ready, 1)
                dve.drain()
                with dve.Fori(0, NS) as b:
                    dve.wait_ge(dotted, b + 1)
                    dve.scalar_tensor_tensor(weighed[:, :, :], ps_dot[:, 0:SLOTS * IH].rearrange("p (j h) -> p j h", h=IH), 0.0,
                                             weights[:, bass.ds(b, 1), :].broadcast_to([P, SLOTS, IH]), ALU.max, ALU.mult).then_inc(summed, 1)
                    dve.drain()
                    dve.tensor_reduce(score[:, bass.ds(b, 1), :].rearrange("p a j -> p (a j)"), weighed[:, :, :], AX.X, ALU.add)
                    dve.drain()
                dve.wait_ge(masked, 2)
                dve.tensor_tensor(score[:, :, :], score[:, :, :], unseen[:, :].rearrange("p (a j) -> p a j", a=1).broadcast_to([P, NS, SLOTS]),
                                  ALU.add).then_inc(masked, 1)
                for k, n in enumerate((first, NS * SLOTS - first)):
                    dve.wait_ge(sc_turned, 2)
                    dve.tensor_copy(turned[0:n, k, :], ps_misc[0:n, 1 + k, :]).then_inc(sc_copied, 1)
                dve.wait_ge(rows_in, 16)
                with dve.Fori(0, TOPK // 8):
                    dve.drain()
                    dve.max(top8[:, :], rows[:, :])
                    dve.drain()
                    dve.match_replace(rows[:, :], top8[:, :], rows[:, :], TAKEN)
                dve.drain()
                dve.tensor_scalar(rows[:, :], rows[:, :], TAKEN / 2, -BIG, ALU.is_gt, ALU.mult).then_inc(hidden, 1)

            @block.tensor
            def _(pe):
                pe.sem_inc(kis_used, 2)
                pe.wait_ge(in_, 16 * (NS + 1))
                pe.transpose(ps_misc[0:IDIM, 0, 0:NS * IH], qi_rows[:, :], ident[0:NS * IH, 0:NS * IH]).then_inc(q_turned, 1)
                pe.wait_ge(q_ready, 2)
                pe.wait_ge(zeroed, 3)
                with pe.Fori(0, NS // 2) as j:
                    for u in range(2):
                        b = j * 2 + u
                        pe.wait_ge(kis_in[u], (j + 1) * 16 * (NPAGE + 1))
                        pe.wait_ge(kiT_ready, 2 * b)
                        for k in range(pairs):
                            last = pe.transpose(ps_kiT[:, k // 4, (k % 4) * P:(k % 4 + 1) * P],
                                                kis[:, u, 2 * k:2 * k + 2, :].rearrange("p a d -> p (a d)"), ident[:, :])
                            if k == pairs - 1:
                                last.then_inc(kis_used, 1)
                        pe.wait_ge(kiT_ready, 2 * b + 2)
                        pe.wait_ge(summed, b)
                        for k in range(pairs):
                            last = pe.matmul(ps_dot[:, k * 2 * IH:(k + 1) * 2 * IH], kiT[:, k, :],
                                             qi2[:, bass.ds(b, 1), :].rearrange("p a h -> p (a h)"), start=True, stop=True)
                        last.then_inc(dotted, 1)
                pe.wait_ge(masked, 3)
                flat = score[:, :, :].rearrange("p b j -> p (b j)")
                pe.transpose(ps_misc[0:first, 1, :], flat[:, 0:first], ident[:, :]).then_inc(sc_turned, 1)
                pe.transpose(ps_misc[0:NS * SLOTS - first, 2, :], flat[:, first:], ident[:, :]).then_inc(sc_turned, 1)


def phase_sample_attend(nc, T):
    with ExitStack() as ctx, Semaphores(nc, T["whole_run"], ("v_in0", "v_in1")) as sems:
        def sb(name, shape, dt=F32):
            return ctx.enter_context(nc.sbuf_tensor("sample_" + name, shape, dt))

        def sem(name):
            return sems("sample_" + name)

        ident = T["ident"]
        table = sb("table", [1, NS * NPAGE], I32)
        q_rows = sb("q_rows", [NS * H, DH])
        qB = sb("qB", [P, 2, NS, H])
        qb = sb("qb", [P, 2, H])
        K = sb("K", [P, 2, SLOTS, NKV * DH])
        V = sb("V", [P, 2, SLOTS, NKV * DH])
        KT = sb("KT", [P, 2, NKEY])
        hide = sb("hide", [H, 2, NKEY])
        s = sb("s", [H, NKEY])
        negmax = sb("negmax", [H, 1])
        total = sb("total", [H, 1])
        PT = sb("PT", [P, SLOTS, H])
        own = sb("own", [H, NKV, DH])
        o_all = sb("o_all", [H, NKV, DH])
        o = sb("o", [H, DH])
        w_out = sb("w_out", [P, KC, D])
        o_rows = sb("o_rows", [NS, D])
        oT = sb("oT", [P, KC, NS])
        x = sb("x", [NS, D])
        y = sb("y", [NS, D])
        gate = sb("gate", [NS, D])
        ps_kT = ctx.enter_context(nc.psum_tensor("sample_ps_kT", [P, 2, 512], F32))
        ps_s = ctx.enter_context(nc.psum_tensor("sample_ps_s", [P, 2, 512], F32))
        ps_pT = ctx.enter_context(nc.psum_tensor("sample_ps_pT", [P, 512], F32))
        ps_o = ctx.enter_context(nc.psum_tensor("sample_ps_o", [P, 512], F32))
        ps_y = ctx.enter_context(nc.psum_tensor("sample_ps_y", [P, 2, 512], F32))
        (table_in, q_in, end_in, zeroed, q_turned, qB_ready, qb_ready, k_turned, kT_ready, s_dotted, s_summed, maxed,
         exped, p_turned, pT_ready, pv_done, o_taken, o_ready, o_out, own_done, rows_in, o_turned, oT_ready, projected,
         y_ready, y_out) = (sem(n) for n in (
             "table_in", "q_in", "end_in", "zeroed", "q_turned", "qB_ready", "qb_ready", "k_turned", "kT_ready",
             "s_dotted", "s_summed", "maxed", "exped", "p_turned", "pT_ready", "pv_done", "o_taken", "o_ready",
             "o_out", "own_done", "rows_in", "o_turned", "oT_ready", "projected", "y_ready", "y_out"))
        k_in = [sem("k_in0"), sem("k_in1")]
        v_in = [sem("v_in0"), sem("v_in1")]
        spare = sem("spare")
        GRP = [4, 4, 4, 4, 1]
        NGR = len(GRP)

        with nc.Block() as block:
            @block.sync
            def _(sp):
                sp.dma_start(table[0:1, :], T["page_table"].rearrange("b (o j) -> o b j", o=1)).then_inc(table_in, 16)
                for b in range(NS):
                    sp.dma_start(q_rows[b * H:(b + 1) * H, :],
                                 T["qs"][SEQ + b:SEQ + b + 1, 0:D].rearrange("a (h d) -> (a h) d", d=DH)).then_inc(q_in, 16)
                sp.wait_ge(table_in, 16)
                sp.wait_ge(zeroed, 4)
                with sp.Fori(0, NS // 2) as j:
                    for u in range(2):
                        b = j * 2 + u
                        sp.wait_ge(k_turned, 2 * NGR * (b + 1))
                        sp.sem_inc(spare, 1)
                        sp.wait_ge(s_summed, NGR * (b + 1))
                        sp.sem_inc(spare, 1)
                        load_pages(sp, table, T["cache_k"], b, K[:, u], k_in[u])
                        sp.dma_start(K[0:1, u, NPAGE, :], T["k_sample"][bass.ds(b, 1), :]).then_inc(k_in[u], 16)
                        sp.dma_start(hide[:, u, :], T["hide_s"][bass.ds(b, 1), :].broadcast_to([H, NKEY])).then_inc(k_in[u], 16)
                for k in range(KC):
                    sp.dma_start(w_out[:, k, :], T["attn_w_out"][k * P:(k + 1) * P, :]).then_inc(end_in, 16)
                sp.dma_start(x[:, :], T["x_sample"]).then_inc(end_in, 16)
                for half in range(2):
                    sp.dma_start(gate[:, half * 512:half * 512 + 512], T["mods"][0, 4 + half, 1:1 + NS, :]).then_inc(end_in, 16)
                sp.wait_ge(o_out, 16 * NS)
                sp.dma_start(o_rows[:, :], T["o_s"]).then_inc(rows_in, 16)
                sp.wait_ge(y_ready, 1)
                sp.dma_start(T["xa"][SEQ:SEQ + NS, :], y[:, :]).then_inc(y_out, 16)
                sp.wait_ge(y_out, 16)

            @block.gpsimd
            def _(pool):
                pool.memset(own[:, :, :], 1.0).then_inc(own_done, 1)
                pool.wait_ge(own_done, 1)
                pool.affine_select(out=own[:, :, :], in_=own[:, :, :], compare_op=ALU.is_ge, fill=0.0,
                                   base=0, pattern=[[-GQ, NKV], [0, DH]], channel_multiplier=1).then_inc(own_done, 1)
                pool.wait_ge(own_done, 2)
                pool.affine_select(out=own[:, :, :], in_=own[:, :, :], compare_op=ALU.is_ge, fill=0.0,
                                   base=GQ - 1, pattern=[[GQ, NKV], [0, DH]], channel_multiplier=-1).then_inc(own_done, 1)
                pool.wait_ge(table_in, 16)
                pool.wait_ge(zeroed, 4)
                with pool.Fori(0, NS // 2) as j:
                    for u in range(2):
                        b = j * 2 + u
                        pool.wait_ge(pv_done, b + 1)
                        pool.sem_inc(spare, 1)
                        load_pages(pool, table, T["cache_v"], b, V[:, u], v_in[u])
                        pool.dma_start(V[0:1, u, NPAGE, :], T["v_sample"][bass.ds(b, 1), :]).then_inc(v_in[u], 16)

            @block.scalar
            def _(act):
                with act.Fori(0, NS // 2) as j:
                    for u in range(2):
                        b = j * 2 + u
                        for k in range(2 * NGR):
                            grp, kp = divmod(k, 2)
                            w = GRP[grp] * P
                            act.wait_ge(k_turned, 2 * NGR * 2 + b * 2 * NGR + k + 1)
                            act.activation(KT[:, kp, grp * 512:grp * 512 + w], ps_kT[:, k % 2, 0:w], ACT.Copy).then_inc(kT_ready, 1)
                        act.wait_ge(maxed, b + 1)
                        act.activation(s[:, :], s[:, :], ACT.Exp, bias=negmax[:, 0:1], accum_out=total[:, :]).then_inc(exped, 1)
                        act.wait_ge(p_turned, b + 1)
                        act.activation(PT[:, :, :], ps_pT[:, 0:SLOTS * H].rearrange("p (j h) -> p j h", h=H), ACT.Copy).then_inc(pT_ready, 1)
                        act.wait_ge(o_ready, b + 1)
                        act.dma_start(T["o_s"][bass.ds(b, 1), :].rearrange("a (h d) -> (a h) d", d=DH), o[:, :]).then_inc(o_out, 16)

            @block.vector
            def _(dve):
                dve.sem_inc(s_summed, 2 * NGR)
                dve.memset(K[:, :, NPAGE, :], 0.0).then_inc(zeroed, 1)
                dve.memset(V[:, :, NPAGE, :], 0.0).then_inc(zeroed, 1)
                dve.memset(qB[:, 0, :, :], 0.0).then_inc(zeroed, 1)
                dve.memset(qB[:, 1, :, :], 0.0).then_inc(zeroed, 1)
                dve.wait_ge(zeroed, 4)
                dve.wait_ge(q_turned, 1)
                turned = ps_pT[0:DH, 0:NS * H].rearrange("p (b h) -> p b h", h=H)
                for kp in range(2):
                    for half in range(2):
                        heads = slice((2 * kp + half) * GQ, (2 * kp + half + 1) * GQ)
                        dve.tensor_scalar(qB[half * DH:(half + 1) * DH, kp, :, heads], turned[:, :, heads], DH ** -0.5, None,
                                          ALU.mult).then_inc(qB_ready, 1)
                dve.wait_ge(own_done, 3)
                dve.wait_ge(qB_ready, 4)
                with dve.Fori(0, NS // 2) as j:
                    for u in range(2):
                        b = j * 2 + u
                        dve.wait_ge(s_dotted, NGR * b)
                        dve.tensor_copy(qb[:, :, :], qB[:, :, bass.ds(b, 1), :].rearrange("p k a h -> p k (a h)")).then_inc(qb_ready, 1)
                        dve.wait_ge(p_turned, b)
                        dve.wait_ge(k_in[u], (j + 1) * 16 * (NPAGE + 2))
                        for grp in range(NGR):
                            keys = slice(grp * 512, grp * 512 + GRP[grp] * P)
                            dve.wait_ge(s_dotted, NGR * b + grp + 1)
                            dve.tensor_tensor(s[:, keys], ps_s[0:H, (u * NGR + grp) % 2, 0:GRP[grp] * P], hide[:, u, keys], ALU.add).then_inc(s_summed, 1)
                        dve.drain()
                        dve.tensor_reduce(negmax[:, :], s[:, :], AX.X, ALU.max, negate=True).then_inc(maxed, 1)
                        dve.wait_ge(pv_done, 2 + b + 1)
                        dve.wait_ge(exped, b + 1)
                        dve.reciprocal(total[:, :], total[:, :])
                        dve.drain()
                        dve.scalar_tensor_tensor(o_all[:, :, :], ps_o[0:H, 0:NKV * DH].rearrange("p (n d) -> p n d", d=DH), total[:, 0:1],
                                                 own[:, :, :], ALU.mult, ALU.mult).then_inc(o_taken, 1)
                        dve.drain()
                        dve.wait_ge(o_out, 16 * b)
                        dve.tensor_reduce(o[:, :], o_all[:, :, :].rearrange("p n d -> p d n"), AX.X, ALU.add).then_inc(o_ready, 1)
                dve.wait_ge(o_turned, 1)
                dve.tensor_copy(oT[:, :, :], ps_kT[:, 0, 0:KC * NS].rearrange("p (k b) -> p k b", b=NS)).then_inc(oT_ready, 1)
                dve.wait_ge(projected, 1)
                dve.wait_ge(end_in, 16 * (KC + 3))
                dve.tensor_tensor(y[:, :], ps_y[0:NS].rearrange("p a n -> p (a n)"), gate[:, :], ALU.mult)
                dve.drain()
                dve.tensor_tensor(y[:, :], y[:, :], x[:, :], ALU.add).then_inc(y_ready, 1)

            @block.tensor
            def _(pe):
                pe.sem_inc(k_turned, 2 * NGR * 2)
                pe.sem_inc(pv_done, 2)
                pe.wait_ge(q_in, 16 * NS)
                pe.transpose(ps_pT[0:DH, 0:NS * H], q_rows[:, :], ident[:, :]).then_inc(q_turned, 1)
                with pe.Fori(0, NS // 2) as j:
                    for u in range(2):
                        b = j * 2 + u
                        pe.wait_ge(k_in[u], (j + 1) * 16 * (NPAGE + 2))
                        pe.wait_ge(qb_ready, b + 1)

                        def dots(grp):
                            w = GRP[grp] * P
                            pe.wait_ge(kT_ready, 2 * NGR * b + 2 * grp + 2)
                            pe.wait_ge(s_summed, NGR * b + grp + 2 * NGR - 1)
                            for kp in range(2):
                                last = pe.matmul(ps_s[0:H, (u * NGR + grp) % 2, 0:w], qb[:, kp, :], KT[:, kp, grp * 512:grp * 512 + w],
                                                 start=(kp == 0), stop=(kp == 1))
                            last.then_inc(s_dotted, 1)
                        for grp in range(NGR + 1):
                            if grp < NGR:
                                for kp in range(2):
                                    if grp:
                                        pe.wait_ge(kT_ready, 2 * NGR * b + 2 * grp + kp - 1)
                                    else:
                                        pe.wait_ge(kT_ready, 2 * NGR * b)
                                    for a in range(GRP[grp]):
                                        last = pe.transpose(ps_kT[:, kp, a * P:(a + 1) * P], K[:, u, grp * 4 + a, kp * P:(kp + 1) * P], ident[:, :])
                                    last.then_inc(k_turned, 1)
                            if grp:
                                dots(grp - 1)
                        pe.wait_ge(exped, b + 1)
                        pe.sem_inc(spare, 1)
                        for k in range(SLOTS):
                            last = pe.transpose(ps_pT[:, k * H:(k + 1) * H], s[:, k * P:(k + 1) * P], ident[0:H, 0:H])
                        last.then_inc(p_turned, 1)
                        pe.wait_ge(pT_ready, b + 1)
                        pe.wait_ge(v_in[u], (j + 1) * 16 * (NPAGE + 1))
                        pe.wait_ge(o_taken, b)
                        for k in range(SLOTS):
                            last = pe.matmul(ps_o[0:H, 0:NKV * DH], PT[:, k, :], V[:, u, k, :], start=(k == 0), stop=(k == SLOTS - 1))
                        last.then_inc(pv_done, 1)
                pe.wait_ge(rows_in, 16)
                pe.wait_ge(end_in, 16 * (KC + 3))
                for k in range(KC):
                    last = pe.transpose(ps_kT[:, 0, k * NS:(k + 1) * NS], o_rows[:, k * P:(k + 1) * P], ident[0:NS, 0:NS])
                last.then_inc(o_turned, 1)
                pe.wait_ge(oT_ready, 1)
                for half in range(2):
                    for k in range(KC):
                        last = pe.matmul(ps_y[0:NS, half, :], oT[:, k, :], w_out[:, k, half * 512:half * 512 + 512],
                                         start=(k == 0), stop=(k == KC - 1))
                last.then_inc(projected, 1)


def phase_route(nc, T, l, src):
    with ExitStack() as ctx, Semaphores(nc, T["whole_run"], ("scattered",)) as sems:
        def sb(name, shape, dt=F32):
            return ctx.enter_context(nc.sbuf_tensor(f"route{l}_" + name, shape, dt))

        def sem(name):
            return sems(f"route{l}_" + name)

        ident, dest_i, share, plan = T["ident"], T["dest"], T["share"], T["plan"]
        NL = NG + NE
        NTT = NT + 1
        wr = sb("wr", [P, KC, NL])
        bias = sb("bias", [P, NL])
        gain = sb("gain", [P, 2, D])
        shift = sb("shift", [P, 2, D])
        x = sb("x", [P, 2, D])
        h = sb("h", [P, 2, D])
        hT = sb("hT", [P, 2, KC, P])
        ss = sb("ss", [P, 2])
        rs = sb("rs", [P, 2])
        logits = sb("logits", [P, NTT, NL])
        best = sb("best", [P, 6, NTT])
        group_is = sb("group_is", [P, NTT, NG])
        allowed = sb("allowed", [P, NTT, NE])
        first_is = sb("first_is", [P, NTT, NE])
        second_is = sb("second_is", [P, NTT, NE])
        tmp = sb("tmp", [P, NTT, NE])
        early = sb("early", [P, NE])
        valid = sb("valid", [P, NTT])
        chosen = sb("chosen", [P, NTT, NE], BF16)
        before = sb("before", [P, P], BF16)
        ones = sb("ones", [P, P], BF16)
        place = sb("place", [P, NTT, NE])
        offset = sb("offset", [P, NTT + 1, NE])
        counts_i = sb("counts_i", [P, NE], I32)
        padded = sb("padded", [P, NE])
        onesf = sb("onesf", [P, NE])
        pend = sb("pend", [P, NE])
        dest = sb("dest", [P, NTT, 2])
        starts = sb("starts", [1, NB])
        passed = sb("passed", [1, NB, NE])
        expert = sb("expert", [1, NB])
        token = sb("token", [P, NTT], I32)
        zeros = sb("zeros", [P, NBR], I32)
        blank = sb("blank", [P, D])
        psT = ctx.enter_context(nc.psum_tensor(f"route{l}_psT", [P, KC, P], F32))
        psL = ctx.enter_context(nc.psum_tensor(f"route{l}_psL", [P, 2, 512], F32))
        psR = ctx.enter_context(nc.psum_tensor(f"route{l}_psR", [P, 4, 512], F32))
        (w_in, mod_in, squared, rstd, x_used, h_turned, hT_ready, routed, summed, pool_chain, consts, filled, vec,
         group_exp, e_exp, chosen_done, ranked, placed, scattered, spare) = (sem(n) for n in (
             "w_in", "mod_in", "squared", "rstd", "x_used", "h_turned", "hT_ready", "routed", "summed", "pool_chain",
             "consts", "filled", "vec", "group_exp", "e_exp", "chosen_done", "ranked", "placed", "scattered",
             "spare"))
        blanked = sem("blanked")
        x_in = [sem("x_in0"), sem("x_in1")]
        h_out = [sem("h_out0"), sem("h_out1")]

        with nc.Block() as block:
            @block.sync
            def _(sp):
                load_modulation(sp, T, l, 4, gain[:, 0], gain[:, 1], mod_in)
                load_modulation(sp, T, l, 3, shift[:, 0], shift[:, 1], mod_in)
                sp.dma_start(h[:, 0, :], T["norm_ffn_g"][l:l + 1, :].broadcast_to([P, D])).then_inc(mod_in, 16)
                for k in range(KC):
                    sp.dma_start(wr[:, k, 0:NG], T["moe_w_group"][l, k * P:(k + 1) * P, :]).then_inc(w_in, 16)
                    sp.dma_start(wr[:, k, NG:NL], T["moe_w_expert"][l, k * P:(k + 1) * P, :]).then_inc(w_in, 16)
                sp.dma_start(bias[:, 0:NG], T["moe_b_group"][l:l + 1, :].broadcast_to([P, NG])).then_inc(w_in, 16)
                sp.dma_start(bias[:, NG:NL], T["moe_b_expert"][l:l + 1, :].broadcast_to([P, NE])).then_inc(w_in, 16)

                def body(t, b, rows):
                    sp.wait_ge(x_used, t + 1)
                    sp.dma_start(x[0:rows, b], T[src][bass.ds(t * P, P)] if rows == P else T[src][SEQ:SEQ + NS]).then_inc(x_in[b], 16)
                two_by_two(sp, body)
                sp.wait_ge(consts, 8)
                sp.dma_start(T["row_tok"].rearrange("(p b) o -> p (b o)", p=P), zeros[:, :]).then_inc(filled, 16)
                if l == 0:
                    for b in range(MIN_BLOCKS, 2 * NPAIR):
                        sp.dma_start(T["yb"][b * BLK:(b + 1) * BLK], blank[:, :]).then_inc(blanked, 16)
                    sp.wait_ge(blanked, 16 * (2 * NPAIR - MIN_BLOCKS))

            @block.gpsimd
            def _(pool):
                pool.memset(before[:, :], 1.0).then_inc(consts, 1)
                pool.memset(ones[:, :], 1.0).then_inc(consts, 1)
                pool.memset(valid[:, :], 1.0).then_inc(consts, 1)
                pool.memset(blank[:, :], 0.0)
                pool.memset(zeros[:, :], 0).then_inc(consts, 1)
                pool.wait_ge(consts, 4)
                pool.affine_select(out=before[:, :], in_=before[:, :], compare_op=ALU.is_gt, fill=0.0,
                                   base=0, pattern=[[1, P]], channel_multiplier=-1).then_inc(consts, 1)
                pool.affine_select(out=valid[:, :], in_=valid[:, :], compare_op=ALU.is_ge, fill=0.0,
                                   base=NTOK - 1, pattern=[[-P, NTT]], channel_multiplier=-1).then_inc(consts, 1)
                pool.iota(token[:, :], pattern=[[P, NTT]], base=0, channel_multiplier=1).then_inc(consts, 1)
                pool.memset(onesf[:, :], 1.0).then_inc(consts, 1)
                link = Chain(pool, pool_chain)

                def body(t, b, rows):
                    pool.wait_ge(squared, t + 1)
                    norm_rstd(pool, link, rs[0:rows, b:b + 1], ss[0:rows, b:b + 1], T["power"][0:rows]).then_inc(rstd, 1)
                with pool.Fori(0, NT // 2) as j:
                    link.enter(j, 2)
                    body(j * 2, 0, P)
                    body(j * 2 + 1, 1, P)
                    link.leave(NT // 2)
                body(NT, 0, NS)
                pool.wait_ge(placed, 1)
                pool.wait_ge(filled, 16)
                for t in range(NTT):
                    rows = P if t < NT else NS
                    for k in range(2):
                        pool.indirect_dma_start(out=T["row_tok"], out_offset=bass.IndirectOffsetOnAxis(ap=dest_i[0:rows, t, k:k + 1], axis=0),
                                                in_=token[0:rows, t:t + 1], in_offset=None).then_inc(scattered, 16)
                pool.wait_ge(scattered, 16 * 2 * NTT)

            @block.scalar
            def _(act):
                def body(t, b, rows):
                    act.wait_ge(x_in[b], (t - b) * 8 + 16)
                    act.wait_ge(routed, t + 1)
                    act.activation(hT[0:rows, b].rearrange("p k n -> p (k n)"), x[0:rows, b], ACT.Square, scale=D ** -0.5,
                                   accum_out=ss[0:rows, b:b + 1]).then_inc(squared, 1)
                    act.wait_ge(x_used, 2 + t + 1)
                    act.dma_start(T["hs"][bass.ds(t * P, P)] if rows == P else T["hs"][SEQ:SEQ + NS], h[0:rows, b]).then_inc(h_out[b], 16)
                    act.wait_ge(h_turned, 2 + t + 1)
                    act.wait_ge(squared, t + 1)
                    act.activation(hT[:, b, :, 0:rows], psT[:, :, 0:rows], ACT.Copy).then_inc(hT_ready, 1)
                two_by_two(act, body)
                act.wait_ge(vec, 1)
                act.activation(tmp[:, :, 0:NG], tmp[:, :, 0:NG], ACT.Exp).then_inc(group_exp, 1)
                act.wait_ge(vec, 2)
                act.activation(best[:, 4, :], best[:, 4, :], ACT.Exp).then_inc(e_exp, 1)
                act.wait_ge(h_out[0], 16 * (NT // 2 + 1))
                act.wait_ge(h_out[1], 16 * (NT // 2))

            @block.vector
            def _(dve):
                dve.sem_inc(x_used, 2)
                dve.memset(logits[:, NT, :], 0.0)
                for e in range(NE):
                    dve.memset(early[:, e:e + 1], float(NE - e))
                for i in range(NB):
                    dve.memset(starts[0:1, i:i + 1], float(i * BLK))
                dve.wait_ge(mod_in, 16 * 9)
                dve.tensor_tensor(gain[:, 0], gain[:, 0], h[:, 0], ALU.mult)
                dve.tensor_tensor(gain[0:NS, 1], gain[0:NS, 1], h[0:NS, 0], ALU.mult)
                dve.drain()
                dve.wait_ge(w_in, 16 * (2 * KC + 2))

                def body(t, b, rows):
                    s = 0 if rows == P else 1
                    dve.wait_ge(rstd, t + 1)
                    dve.wait_ge(h_turned, t + 1)
                    dve.wait_ge(h_out[b], (t - b) * 8)
                    dve.scalar_tensor_tensor(h[0:rows, b], x[0:rows, b], rs[0:rows, b:b + 1], gain[0:rows, s], ALU.mult, ALU.mult)
                    dve.drain()
                    dve.tensor_tensor(h[0:rows, b], h[0:rows, b], shift[0:rows, s], ALU.add).then_inc(x_used, 1)
                    dve.wait_ge(routed, 2 + t + 1)
                    dve.tensor_tensor(logits[0:rows, bass.ds(t, 1), :].rearrange("p a n -> p (a n)"), psL[0:rows, b, 0:NL],
                                      bias[0:rows, :], ALU.add).then_inc(summed, 1)
                two_by_two(dve, body)
                dve.drain()

                def wide(v, n):
                    return v.rearrange("p (t a) -> p t a", a=1).broadcast_to([P, NTT, n])

                def first_of(values, top, out, n):
                    dve.tensor_tensor(out, values, wide(top, n), ALU.is_equal)
                    dve.drain()
                    dve.tensor_tensor(out, out, early[:, 0:n].rearrange("p (a n) -> p a n", a=1).broadcast_to([P, NTT, n]), ALU.mult)
                    dve.drain()
                    dve.tensor_reduce(best[:, 5, :], out, AX.X, ALU.max)
                    dve.drain()
                    dve.tensor_tensor(out, out, wide(best[:, 5, :], n), ALU.is_equal)
                    dve.drain()
                glog, elog = logits[:, :, 0:NG], logits[:, :, NG:NL]
                dve.tensor_reduce(best[:, 0, :], glog, AX.X, ALU.max)
                dve.drain()
                first_of(glog, best[:, 0, :], group_is[:, :, :], NG)
                dve.tensor_tensor(tmp[:, :, 0:NG], glog, wide(best[:, 0, :], NG), ALU.subtract).then_inc(vec, 1)
                dve.wait_ge(group_exp, 1)
                dve.tensor_reduce(best[:, 1, :], tmp[:, :, 0:NG], AX.X, ALU.add)
                dve.drain()
                dve.tensor_scalar(group_is[:, :, :], group_is[:, :, :], BIG, -BIG, ALU.mult, ALU.add)
                dve.drain()
                dve.tensor_tensor(allowed[:, :, :].rearrange("p t (g e) -> p t g e", g=NG), elog.rearrange("p t (g e) -> p t g e", g=NG),
                                  group_is[:, :, :].rearrange("p t (g a) -> p t g a", a=1).broadcast_to([P, NTT, NG, EPG]), ALU.add)
                dve.drain()
                dve.tensor_reduce(best[:, 2, :], allowed[:, :, :], AX.X, ALU.max)
                dve.drain()
                first_of(allowed[:, :, :], best[:, 2, :], first_is[:, :, :], NE)
                dve.scalar_tensor_tensor(allowed[:, :, :], first_is[:, :, :], -BIG, allowed[:, :, :], ALU.mult, ALU.add)
                dve.drain()
                dve.tensor_reduce(best[:, 3, :], allowed[:, :, :], AX.X, ALU.max)
                dve.drain()
                first_of(allowed[:, :, :], best[:, 3, :], second_is[:, :, :], NE)
                dve.tensor_tensor(best[:, 4, :], best[:, 3, :], best[:, 2, :], ALU.subtract).then_inc(vec, 1)
                dve.wait_ge(e_exp, 1)
                dve.tensor_scalar(best[:, 5, :], best[:, 4, :], 1.0, None, ALU.add)
                dve.drain()
                dve.tensor_tensor(best[:, 5, :], best[:, 5, :], best[:, 1, :], ALU.mult)
                dve.drain()
                dve.reciprocal(share[:, :, 0], best[:, 5, :])
                dve.drain()
                dve.tensor_tensor(share[:, :, 1], share[:, :, 0], best[:, 4, :], ALU.mult)
                dve.tensor_tensor(tmp[:, :, :], first_is[:, :, :], second_is[:, :, :], ALU.add)
                dve.drain()
                dve.wait_ge(consts, 8)
                dve.tensor_tensor(chosen[:, :, :], tmp[:, :, :], wide(valid[:, :], NE), ALU.mult).then_inc(chosen_done, 1)
                dve.wait_ge(ranked, 1)
                half = NTT * NE // 2
                dve.tensor_copy(place[:, :, :].rearrange("p t e -> p (t e)")[:, 0:half], psR[:, 0, 0:half])
                dve.tensor_copy(place[:, :, :].rearrange("p t e -> p (t e)")[:, half:], psR[:, 1, 0:half])
                dve.tensor_copy(tmp[:, :, :].rearrange("p t e -> p (t e)")[:, 0:half], psR[:, 2, 0:half])
                dve.tensor_copy(tmp[:, :, :].rearrange("p t e -> p (t e)")[:, half:], psR[:, 3, 0:half])
                dve.memset(offset[:, 0, :], 0.0)
                dve.drain()
                for t in range(NTT):
                    dve.tensor_tensor(offset[:, t + 1, :], offset[:, t, :], tmp[:, t, :], ALU.add)
                    dve.drain()
                dve.tensor_scalar(counts_i[:, :], offset[:, NTT, :], float(BLK - 1), None, ALU.add)
                dve.drain()
                dve.tensor_scalar(counts_i[:, :], counts_i[:, :], 7, 7, ALU.logical_shift_right, ALU.logical_shift_left)
                dve.drain()
                dve.tensor_copy(padded[:, :], counts_i[:, :])
                dve.drain()
                dve.tensor_tensor_scan(pend[:, :], onesf[:, :], padded[:, :], 0.0, ALU.mult, ALU.add)
                dve.drain()
                dve.tensor_tensor(padded[:, :], pend[:, :], padded[:, :], ALU.subtract)
                dve.drain()
                dve.tensor_tensor(place[:, :, :], place[:, :, :], offset[:, 0:NTT, :], ALU.add)
                dve.drain()
                dve.tensor_tensor(place[:, :, :], place[:, :, :], padded[:, :].rearrange("p (a e) -> p a e", a=1).broadcast_to([P, NTT, NE]), ALU.add)
                dve.drain()
                for k, is_ in enumerate((first_is, second_is)):
                    dve.tensor_tensor(is_[:, :, :], is_[:, :, :], place[:, :, :], ALU.mult)
                    dve.drain()
                    dve.tensor_reduce(dest[:, :, k], is_[:, :, :], AX.X, ALU.add)
                dve.drain()
                dve.tensor_copy(dest_i[:, :, :], dest[:, :, :]).then_inc(placed, 1)
                dve.tensor_tensor(passed[:, :, :], pend[0:1, :].rearrange("p (a e) -> p a e", a=1).broadcast_to([1, NB, NE]),
                                  starts[0:1, :].rearrange("p (b a) -> p b a", a=1).broadcast_to([1, NB, NE]), ALU.is_le)
                dve.drain()
                dve.tensor_reduce(expert[:, :], passed[:, :, :], AX.X, ALU.add)
                dve.drain()
                dve.tensor_scalar(plan[0:1, 0:NB], expert[:, :], float(NE - 1), None, ALU.min)
                dve.tensor_scalar(plan[0:1, PLAN_START:PLAN_LAST], padded[0:1, :], 1.0 / BLK, None, ALU.mult)
                dve.tensor_scalar(counts_i[0:1, 0:1], pend[0:1, NE - 1:NE], float(-BLK), None, ALU.add)
                dve.drain()
                dve.tensor_scalar(plan[0:1, PLAN_LAST:PLAN_END], counts_i[0:1, 0:1], 8, None, ALU.logical_shift_right)
                dve.drain()

            @block.tensor
            def _(pe):
                pe.sem_inc(routed, 2)
                pe.sem_inc(h_turned, 2)
                pe.wait_ge(w_in, 16 * (2 * KC + 2))

                def body(t, b, rows):
                    pe.wait_ge(x_used, 2 + t + 1)
                    pe.wait_ge(hT_ready, t)
                    pe.sem_inc(spare, 1)
                    for k in range(KC):
                        last = pe.transpose(psT[:, k, 0:rows], h[0:rows, b, k * P:(k + 1) * P], ident[0:rows, 0:rows])
                    last.then_inc(h_turned, 1)
                    pe.wait_ge(hT_ready, t + 1)
                    pe.wait_ge(summed, t - 1) if isinstance(t, int) else pe.wait_ge(summed, t)
                    for k in range(KC):
                        last = pe.matmul(psL[0:rows, b, 0:NL], hT[:, b, k, 0:rows], wr[:, k, :], start=(k == 0), stop=(k == KC - 1))
                    last.then_inc(routed, 1)
                two_by_two(pe, body)
                pe.wait_ge(chosen_done, 1)
                pe.wait_ge(consts, 8)
                flat = chosen[:, :, :].rearrange("p t e -> p (t e)")
                half = NTT * NE // 2
                for k in range(2):
                    pe.matmul(psR[:, k, 0:half], before[:, :], flat[:, k * half:(k + 1) * half], start=True, stop=True)
                    last = pe.matmul(psR[:, 2 + k, 0:half], ones[:, :], flat[:, k * half:(k + 1) * half], start=True, stop=True)
                last.then_inc(ranked, 1)


def phase_experts(nc, T, l):
    with ExitStack() as ctx, Semaphores(nc, T["whole_run"], ("idx_in", "x_in0", "x_in1")) as sems:
        def sb(name, shape, dt=F32):
            return ctx.enter_context(nc.sbuf_tensor(f"experts{l}_" + name, shape, dt))

        def sem(name):
            return sems(f"experts{l}_" + name)

        ident, plan = T["ident"], T["plan"]
        KF = FE // P
        idx = sb("idx", [P, NBR], I32)
        idx_rows = sb("idx_rows", [NBR, P], I32)
        idx_f = sb("idx_f", [NBR, P])
        idxb = sb("idxb", [P, 2], I32)
        w1 = sb("w1", [P, 2, KC, 2 * FE])
        w2 = sb("w2", [P, 2, KF, D])
        x = sb("x", [P, 2, D])
        xT = sb("xT", [P, 2, KC, P])
        th = sb("th", [P, 2, FE])
        mid = sb("mid", [P, 2, FE])
        midT = sb("midT", [P, KF, P])
        y = sb("y", [P, 2, D])
        ps_x = ctx.enter_context(nc.psum_tensor(f"experts{l}_ps_x", [P, KC, P], F32))
        ps_gu = ctx.enter_context(nc.psum_tensor(f"experts{l}_ps_gu", [P, 2, 512], F32))
        ps_m = ctx.enter_context(nc.psum_tensor(f"experts{l}_ps_m", [P, 4, P], F32))
        ps_y = ctx.enter_context(nc.psum_tensor(f"experts{l}_ps_y", [P, 2, 512], F32))
        (idx_in, idx_turned, idx_ready, x_turned, xT_ready, up_done, tanhed, silued, mid_turned, midT_ready, down_done,
         y_copied, spare) = (sem(n) for n in (
             "idx_in", "idx_turned", "idx_ready", "x_turned", "xT_ready", "up_done", "tanhed", "silued", "mid_turned",
             "midT_ready", "down_done", "y_copied", "spare"))
        w1_in = [sem("w1_in0"), sem("w1_in1")]
        w2_in = [sem("w2_in0"), sem("w2_in1")]
        x_in = [sem("x_in0"), sem("x_in1")]
        y_out = [sem("y_out0"), sem("y_out1")]

        def last_pair(eng):
            return eng.value_load(plan[0:1, PLAN_LAST:PLAN_END], min_val=0, max_val=NPAIR - 1)

        def all_pairs(eng, body, last):
            body(0, 0, True)
            body(1, 1, False)
            with eng.Fori(1, NPAIR) as j:
                with eng.If(j <= last):
                    body(j * 2, 0, False)
                    body(j * 2 + 1, 1, False)

        with nc.Block() as block:
            @block.sync
            def _(sp):
                def load(e, slot):
                    sp.dma_start(w1[:, slot].rearrange("p k n -> p (k n)"),
                                 T["moe_w1"][l, bass.ds(e, 1)].rearrange("a (p k) n -> p (a k n)", k=KC)).then_inc(w1_in[slot], 16)

                def load2(e, slot):
                    sp.dma_start(w2[:, slot].rearrange("p k n -> p (k n)"),
                                 T["moe_w2"][l, bass.ds(e, 1)].rearrange("a (p k) n -> p (a k n)", k=KF)).then_inc(w2_in[slot], 16)
                for e in range(2):
                    load(e, e)
                    load2(e, e)
                with sp.Fori(1, NE // 2) as j:
                    for slot in range(2):
                        before = sp.value_load(plan[0:1, bass.ds(j * 2 + (PLAN_START + slot - 1), 1)], min_val=0, max_val=NB)
                        sp.wait_ge(up_done, before + 2)
                        load(j * 2 + slot, slot)
                        sp.wait_ge(down_done, before * 2 + 2)
                        load2(j * 2 + slot, slot)

            @block.gpsimd
            def _(pool):
                last_ = last_pair(pool)
                pool.dma_start(idx_rows[:, :], T["row_tok"].rearrange("(b p) o -> b (p o)", p=P)).then_inc(idx_in, 16)
                pool.wait_ge(idx_turned, 3)

                def fetch(b, u):
                    pool.tensor_copy(idxb[:, u:u + 1], idx[:, bass.ds(b, 1)] if not isinstance(b, int) else idx[:, b:b + 1]).then_inc(idx_ready, 1)
                    pool.wait_ge(idx_ready, b + 1)
                    pool.sem_inc(spare, 1)
                    pool.indirect_dma_start(out=x[:, u, :], out_offset=None, in_=T["hs"],
                                            in_offset=bass.IndirectOffsetOnAxis(ap=idxb[:, u:u + 1], axis=0)).then_inc(x_in[u], 16)

                def body(b, u, first):
                    pool.wait_ge(x_turned, b + 1)
                    pool.sem_inc(spare, 1)
                    fetch(b + 2, u)
                fetch(0, 0)
                fetch(1, 1)
                all_pairs(pool, body, last_)
                for u in range(2):
                    pool.wait_ge(x_in[u], last_ * 16 + 32)
                    pool.sem_inc(spare, 1)

            @block.scalar
            def _(act):
                last_ = last_pair(act)
                act.wait_ge(x_turned, 1)
                act.activation(xT[:, 0], ps_x[:, :, :], ACT.Copy).then_inc(xT_ready, 1)

                def finish(b, u):
                    for half in range(2):
                        act.wait_ge(down_done, 2 + 2 * b + half + 1)
                        if half == 0:
                            act.wait_ge(y_out[u], (b - u) * 8)
                        act.activation(y[:, u, half * 512:half * 512 + 512], ps_y[:, half, :], ACT.Copy).then_inc(y_copied, 1)
                    act.wait_ge(y_copied, 2 * b + 4)
                    act.dma_start(T["yb"][bass.ds(b * BLK, BLK), :], y[:, u]).then_inc(y_out[u], 16)

                def body(b, u, first):
                    act.wait_ge(up_done, 2 + b + 1)
                    act.wait_ge(silued, b + 1)
                    act.activation(th[:, u], ps_gu[:, u, 0:FE], ACT.Tanh, scale=0.5).then_inc(tanhed, 1)
                    if not first:
                        finish(b - 1, 1 - u)
                    act.wait_ge(x_turned, b + 2)
                    act.activation(xT[:, 1 - u], ps_x[:, :, :], ACT.Copy).then_inc(xT_ready, 1)
                all_pairs(act, body, last_)
                finish(last_ * 2 + 1, 1)
                act.wait_ge(y_out[0], last_ * 16 + 16)
                act.sem_inc(spare, 1)
                act.wait_ge(y_out[1], last_ * 16 + 16)
                act.sem_inc(spare, 1)

            @block.vector
            def _(dve):
                last_ = last_pair(dve)
                dve.sem_inc(silued, 2)
                dve.wait_ge(idx_in, 16)
                dve.tensor_copy(idx_f[:, :], idx_rows[:, :]).then_inc(idx_turned, 1)
                dve.wait_ge(idx_turned, 2)
                dve.tensor_copy(idx[:, :], ps_m[:, 3, 0:NBR]).then_inc(idx_turned, 1)

                def body(b, u, first):
                    g, up = ps_gu[:, u, 0:FE], ps_gu[:, u, FE:]
                    dve.wait_ge(tanhed, b + 1)
                    dve.scalar_tensor_tensor(th[:, u], th[:, u], 1.0, g, ALU.add, ALU.mult)
                    dve.drain()
                    dve.scalar_tensor_tensor(mid[:, u], th[:, u], 0.5, up, ALU.mult, ALU.mult).then_inc(silued, 1)
                    dve.wait_ge(mid_turned, b + 1)
                    dve.tensor_copy(midT[:, :, :], ps_m[:, 0:KF, :]).then_inc(midT_ready, 1)
                all_pairs(dve, body, last_)

            @block.tensor
            def _(pe):
                last_ = last_pair(pe)
                pe.sem_inc(up_done, 2)
                pe.sem_inc(down_done, 2)
                pe.sem_inc(y_copied, 2)

                def weights(b, sems_):
                    e = pe.value_load(plan[0:1, bass.ds(b, 1)] if not isinstance(b, int) else plan[0:1, b:b + 1], min_val=0, max_val=NE - 1)
                    pe.wait_ge(sems_[0], ((e >> 1) << 4) + 16)
                    pe.wait_ge(sems_[1], ((e + 1) >> 1) << 4)
                    return e & 1

                def turn(b, u):
                    pe.wait_ge(x_in[u], (b - u) * 8 + 16)
                    pe.wait_ge(xT_ready, b)
                    rows = x[:, u].rearrange("p (c k) -> p k c", k=KC)
                    for k in range(KC):
                        last = pe.transpose(ps_x[:, k, :], rows[:, k, :], ident[:, :])
                    last.then_inc(x_turned, 1)

                def down(b):
                    slot = weights(b, w2_in)
                    pe.wait_ge(midT_ready, b + 1)
                    for half in range(2):
                        pe.wait_ge(y_copied, 2 * b + half + 1)
                        for k in range(KF):
                            last = pe.matmul(ps_y[:, half, :], midT[:, k, :],
                                             w2[:, bass.ds(slot, 1), k, half * 512:half * 512 + 512].rearrange("p a n -> p (a n)"),
                                             start=(k == 0), stop=(k == KF - 1))
                        last.then_inc(down_done, 1)

                def body(b, u, first):
                    pe.wait_ge(xT_ready, b + 1)
                    pe.wait_ge(silued, b + 1)
                    slot = weights(b, w1_in)
                    for k in range(KC):
                        last = pe.matmul(ps_gu[:, u, :], xT[:, u, k, :],
                                         w1[:, bass.ds(slot, 1), k, :].rearrange("p a n -> p (a n)"), start=(k == 0), stop=(k == KC - 1))
                    last.then_inc(up_done, 1)
                    if not first:
                        down(b - 1)
                    turn(b + 1, 1 - u)
                    pe.wait_ge(silued, 2 + b + 1)
                    if not first:
                        pe.wait_ge(midT_ready, b)
                    cols = mid[:, u].rearrange("p (c k) -> p k c", k=KF)
                    for k in range(KF):
                        last = pe.transpose(ps_m[:, k, :], cols[:, k, :], ident[:, :])
                    last.then_inc(mid_turned, 1)
                pe.wait_ge(idx_turned, 1)
                pe.transpose(ps_m[:, 3, 0:NBR], idx_f[:, :], ident[0:NBR, 0:NBR]).then_inc(idx_turned, 1)
                pe.wait_ge(idx_turned, 3)
                turn(0, 0)
                all_pairs(pe, body, last_)
                down(last_ * 2 + 1)


def phase_combine(nc, T, l, src, dst, final):
    with ExitStack() as ctx, Semaphores(nc, T["whole_run"], ("y_in0", "y_in1")) as sems:
        def sb(name, shape, dt=F32):
            return ctx.enter_context(nc.sbuf_tensor(f"combine{l}_" + name, shape, dt))

        def sem(name):
            return sems(f"combine{l}_" + name)

        dest_i, share = T["dest"], T["share"]
        gate = sb("gate", [P, 2, D])
        g_final = sb("g_final", [P, D])
        idxb = sb("idxb", [P, 2, 2], I32)
        x = sb("x", [P, 2, D])
        y = sb("y", [P, 2, 2, D])
        z = sb("z", [P, 2, D])
        junk = sb("junk", [P, D])
        ss = sb("ss", [P, 2])
        rs = sb("rs", [P, 2])
        (mod_in, idx_ready, added, weighed, squared, rstd, chain, done, spare) = (sem(n) for n in (
            "mod_in", "idx_ready", "added", "weighed", "squared", "rstd", "chain", "done", "spare"))
        x_in = [sem("x_in0"), sem("x_in1")]
        y_in = [sem("y_in0"), sem("y_in1")]
        out_ = [sem("out0"), sem("out1")]

        def share_at(t, rows, k):
            return share[0:rows, bass.ds(t, 1), k]

        with nc.Block() as block:
            @block.sync
            def _(sp):
                if not final:
                    for k in range(KC):
                        sp.dma_start(T["rec_w_in_sb"][:, k, :], T["rec_w_in"][k * P:(k + 1) * P, :]).then_inc(T["rec_w_loaded"], 16)
                    for k in range(KC):
                        sp.dma_start(T["rec_w_out_sb"][:, k, :], T["rec_w_out"][k * P:(k + 1) * P, :]).then_inc(T["rec_w_loaded"], 16)
                load_modulation(sp, T, l, 5, gate[:, 0], gate[:, 1], mod_in)
                sp.dma_start(g_final[:, :], T["norm_final_g"].broadcast_to([P, D])).then_inc(mod_in, 16)

                def body(t, b, rows):
                    sp.wait_ge(done, t + 1)
                    sp.dma_start(x[0:rows, b], T[src][bass.ds(t * P, P)] if rows == P else T[src][SEQ:SEQ + NS]).then_inc(x_in[b], 16)
                two_by_two(sp, body)

            @block.gpsimd
            def _(pool):
                link = Chain(pool, chain)

                def body(t, b, rows):
                    pool.wait_ge(done, t + 1)
                    pool.sem_inc(spare, 1)
                    pool.tensor_copy(idxb[0:rows, b, :], dest_i[0:rows, bass.ds(t, 1), :].rearrange("p a k -> p (a k)")).then_inc(idx_ready, 1)
                    pool.wait_ge(idx_ready, t + 1)
                    pool.sem_inc(spare, 1)
                    for k in range(2):
                        pool.indirect_dma_start(out=y[0:rows, b, k, :], out_offset=None, in_=T["yb"],
                                                in_offset=bass.IndirectOffsetOnAxis(ap=idxb[0:rows, b, k:k + 1], axis=0)).then_inc(y_in[b], 16)

                def norm(t, b, rows):
                    pool.wait_ge(squared, t + 1)
                    norm_rstd(pool, link, rs[0:rows, b:b + 1], ss[0:rows, b:b + 1], T["power"][0:rows]).then_inc(rstd, 1)
                with pool.Fori(0, NT // 2) as j:
                    if final:
                        link.enter(j, 2)
                    body(j * 2, 0, P)
                    body(j * 2 + 1, 1, P)
                    if final:
                        norm(j * 2, 0, P)
                        norm(j * 2 + 1, 1, P)
                        link.leave(NT // 2)
                body(NT, 0, NS)
                if final:
                    norm(NT, 0, NS)

            @block.scalar
            def _(act):
                def body(t, b, rows):
                    act.wait_ge(y_in[b], (t - b) * 16 + 32)
                    act.activation(y[0:rows, b, 0, :], y[0:rows, b, 0, :], ACT.Copy, scale=share_at(t, rows, 0)).then_inc(weighed, 1)
                    if final:
                        act.wait_ge(added, t + 1)
                        act.activation(junk[0:rows, :], z[0:rows, b, :], ACT.Square, scale=D ** -0.5,
                                       accum_out=ss[0:rows, b:b + 1]).then_inc(squared, 1)
                    act.wait_ge(done, 2 + t + 1)
                    out = ((T["y_prompt"][bass.ds(t * P, P)] if rows == P else T["y_sample"]) if final else
                           (T[dst][bass.ds(t * P, P)] if rows == P else T[dst][SEQ:SEQ + NS]))
                    act.dma_start(out, z[0:rows, b, :]).then_inc(out_[b], 16)
                two_by_two(act, body)
                act.wait_ge(out_[0], 16 * (NT // 2 + 1))
                act.wait_ge(out_[1], 16 * (NT // 2))

            @block.vector
            def _(dve):
                dve.sem_inc(done, 2)
                dve.wait_ge(mod_in, 16 * 5)

                def body(t, b, rows):
                    s = 0 if rows == P else 1
                    dve.wait_ge(weighed, t + 1)
                    dve.wait_ge(x_in[b], (t - b) * 8 + 16)
                    dve.wait_ge(out_[b], (t - b) * 8)
                    dve.scalar_tensor_tensor(z[0:rows, b], y[0:rows, b, 1, :], share_at(t, rows, 1), y[0:rows, b, 0, :], ALU.mult, ALU.add)
                    dve.drain()
                    dve.tensor_tensor(z[0:rows, b], z[0:rows, b], gate[0:rows, s], ALU.mult)
                    dve.drain()
                    if not final:
                        dve.tensor_tensor(z[0:rows, b], z[0:rows, b], x[0:rows, b], ALU.add).then_inc(done, 1)
                        return
                    dve.tensor_tensor(z[0:rows, b], z[0:rows, b], x[0:rows, b], ALU.add).then_inc(added, 1)
                    dve.wait_ge(rstd, t + 1)
                    dve.scalar_tensor_tensor(z[0:rows, b], z[0:rows, b], rs[0:rows, b:b + 1], g_final[0:rows], ALU.mult, ALU.mult).then_inc(done, 1)
                two_by_two(dve, body)


WB = 2 * P
NQ = SEQ // WB
GELU_K = math.sqrt(2.0 / math.pi)
GELU_C = 0.044715


def phase_recurrent(nc, T, src, dst):
    with ExitStack() as ctx, Semaphores(nc, T["whole_run"]) as sems:
        def sb(name, shape, dt=F32):
            return ctx.enter_context(nc.sbuf_tensor("recurrent_" + name, shape, dt))

        def sem(name):
            return sems("recurrent_" + name)

        ident = T["ident"]
        w_in, w_out, w_loaded = T["rec_w_in_sb"], T["rec_w_out_sb"], T["rec_w_loaded"]
        w_a = sb("w_a", [P, KC, P])
        w_x = sb("w_x", [P, KC, P])
        param_rows = sb("param_rows", [8 * KC, P])
        par = sb("par", [P, 8, KC])
        sp = sb("sp", [P, 8, KC])
        state_rows = sb("state_rows", [NS * CONV_W, D])
        state = sb("state", [P, KC, NS * CONV_W])
        gain = sb("gain", [P, D])
        shift = sb("shift", [P, D])
        gate = sb("gate", [P, D])
        x = sb("x", [P, 2, D])
        res = sb("res", [P, D])
        h = sb("h", [P, 2, D])
        hT = sb("hT", [P, KC, WB])
        squares = sb("squares", [P, D], BF16)
        ss = sb("ss", [P, 2])
        rs = sb("rs", [P, 2])
        xcat = sb("xcat", [P, 2, 4 + WB])
        xc = sb("xc", [P, 2, WB])
        gx = sb("gx", [P, 2, WB])
        thr = sb("thr", [P, 2, WB])
        thi = sb("thi", [P, 2, WB])
        a = sb("a", [P, KC, WB])
        root = sb("root", [P, KC, WB])
        v = sb("v", [P, KC, WB])
        g = sb("g", [P, KC, WB])
        carry = sb("carry", [P, CONV_W - 1, KC])
        last_h = sb("last_h", [P, KC])
        xb_s = sb("xb_s", [P, KC, NS])
        h_s = sb("h_s", [P, KC, NS])
        out = sb("out", [P, D])
        norm_g_s = sb("norm_g_s", [NS, D])
        ends = sb("ends", [KC * NS, 2, P])
        end_p = sb("end_p", [KC, 4, P])
        psT = ctx.enter_context(nc.psum_tensor("recurrent_psT", [P, KC, P], F32))
        psAB = ctx.enter_context(nc.psum_tensor("recurrent_psAB", [P, 2, 2, WB], F32))
        psRI = ctx.enter_context(nc.psum_tensor("recurrent_psRI", [P, 2, 2, WB], F32))
        psO = ctx.enter_context(nc.psum_tensor("recurrent_psO", [P, 2, 512], F32))
        (const_in, mod_in, squared, rstd, x_used, h_turned, hT_ready, ab_done, xb_copied, gx_squared, p_done, gth_done,
         gelu_done, conv_done, ri_done, a_done, v_done, sqrt_done, y_done, out_done, o_taken, res_in, res_done, res_out,
         pool_chain, consts, ends_turned, ends_done, ends_out, spare, mod_s) = (sem(n) for n in (
             "const_in", "mod_in", "squared", "rstd", "x_used", "h_turned", "hT_ready", "ab_done", "xb_copied",
             "gx_squared", "p_done", "gth_done", "gelu_done", "conv_done", "ri_done", "a_done", "v_done", "sqrt_done",
             "y_done", "out_done", "o_taken", "res_in", "res_done", "res_out", "pool_chain", "consts", "ends_turned",
             "ends_done", "ends_out", "spare", "mod_s"))
        x_in = [sem("x_in0"), sem("x_in1")]

        def blocks(eng, body, start=lambda q, W, rows: None):
            start(0, WB, P)
            with eng.Fori(0, NQ - 1) as q:
                body(q, WB, P, True)
            body(NQ - 1, WB, P, False)
            start(NQ, NS, NS)
            body(NQ, NS, NS, False)

        def tiles(q, rows):
            return [(q * 2 + i, i) for i in range(2)] if rows == P else [(2 * NQ, 0)]

        def tile_rows(name, t, rows):
            return T[name][bass.ds(t * P, P)] if rows == P else T[name][SEQ:SEQ + NS]

        with nc.Block() as block:
            @block.sync
            def _(sy):
                def modulation(chunk, tile_, row, rows, s):
                    for half in range(2):
                        part = T["mods"][1, chunk * 2 + half, row:row + rows, :]
                        sy.dma_start(tile_[0:(P if rows == 1 else rows), half * 512:half * 512 + 512],
                                     part.broadcast_to([P, 512]) if rows == 1 else part).then_inc(s, 16)
                for n, name in enumerate(("rec_conv_w", "rec_conv_b", "rec_b_a", "rec_b_x", "rec_lambda")):
                    at = 0 if n == 0 else (CONV_W + n - 1) * KC
                    size = CONV_W * KC if n == 0 else KC
                    sy.dma_start(param_rows[at:at + size, :], T[name].rearrange("v (c p) -> (v c) p", p=P)).then_inc(const_in, 16)
                sy.dma_start(state_rows[0:NS * (CONV_W - 1), :], T["state_conv"].rearrange("b j d -> (b j) d")).then_inc(const_in, 16)
                sy.dma_start(state_rows[NS * (CONV_W - 1):, :], T["state_h"]).then_inc(const_in, 16)
                modulation(1, gain, 0, 1, mod_in)
                modulation(0, shift, 0, 1, mod_in)
                modulation(2, gate, 0, 1, mod_in)
                sy.dma_start(h[:, 0], T["norm_mix_g"][1:2, :].broadcast_to([P, D])).then_inc(mod_in, 16)
                sy.dma_start(w_a[:, :, :], T["rec_w_a"].rearrange("c i o -> i c o")).then_inc(const_in, 16)
                sy.dma_start(w_x[:, :, :], T["rec_w_x"].rearrange("c i o -> i c o")).then_inc(const_in, 16)

                def start(q, W, rows):
                    for t, i in tiles(q, rows):
                        sy.wait_ge(x_used, t + 1)
                        sy.dma_start(x[0:rows, i], tile_rows(src, t, rows)).then_inc(x_in[i], 16)
                        if rows == NS:
                            sy.wait_ge(mod_s, 1)
                            modulation(1, gain, 1, NS, mod_in)
                            modulation(0, shift, 1, NS, mod_in)
                            sy.dma_start(norm_g_s[:, :], T["norm_mix_g"][1:2, :].broadcast_to([NS, D])).then_inc(mod_in, 16)
                            sy.wait_ge(res_done, 2 * NQ)
                            modulation(2, gate, 1, NS, mod_in)

                def body(q, W, rows, ahead):
                    if ahead:
                        start(q + 1, W, rows)
                    for t, i in tiles(q, rows):
                        sy.wait_ge(res_done, t)
                        sy.dma_start(res[0:rows, :], tile_rows(src, t, rows)).then_inc(res_in, 16)
                blocks(sy, body, start)
                sy.wait_ge(ends_done, 2)
                sy.dma_start(T["h_prompt"].rearrange("a (c p) -> (a c) p", p=P), end_p[:, 3, :]).then_inc(ends_out, 16)
                for j in range(CONV_W - 1):
                    sy.dma_start(T["conv_prompt"][j:j + 1, :].rearrange("a (c p) -> (a c) p", p=P), end_p[:, j, :]).then_inc(ends_out, 16)
                for c in range(KC):
                    sy.dma_start(T["h_sample"][:, c * P:(c + 1) * P], ends[c * NS:(c + 1) * NS, 0, :]).then_inc(ends_out, 16)
                    sy.dma_start(T["conv_sample"][:, CONV_W - 2, c * P:(c + 1) * P], ends[c * NS:(c + 1) * NS, 1, :]).then_inc(ends_out, 16)
                sy.dma_start(T["conv_sample"][:, 0:CONV_W - 2, :], T["state_conv"][:, 1:CONV_W - 1, :]).then_inc(ends_out, 16)
                sy.wait_ge(ends_out, 16 * (1 + CONV_W - 1 + 2 * KC + 1))

            @block.gpsimd
            def _(pool):
                link = Chain(pool, pool_chain)

                def body(q, W, rows):
                    for t, i in tiles(q, rows):
                        pool.wait_ge(squared, t + 1)
                        norm_rstd(pool, link, rs[0:rows, i:i + 1], ss[0:rows, i:i + 1], T["power"][0:rows]).then_inc(rstd, 1)
                with pool.Fori(0, NQ) as q:
                    link.enter(q, 2)
                    body(q, WB, P)
                    link.leave(NQ)
                body(NQ, NS, NS)

            @block.scalar
            def _(act):
                act.sem_inc(a_done, 2)
                act.sem_inc(xb_copied, 2)
                act.wait_ge(consts, 1)
                act.activation(sp[:, 1, :], sp[:, 1, :], ACT.Exp, scale=-1.0).then_inc(consts, 1)
                act.wait_ge(consts, 3)

                def squares_of(q, rows):
                    for t, i in tiles(q, rows):
                        act.drain()
                        act.wait_ge(x_in[i], 16 * (q + 1))
                        act.activation(squares[0:rows, :], x[0:rows, i], ACT.Square, scale=D ** -0.5, accum_out=ss[0:rows, i:i + 1]).then_inc(squared, 1)

                def keep_turned(q, rows):
                    for t, i in tiles(q, rows):
                        act.wait_ge(h_turned, 1 + t + 1)
                        act.wait_ge(ab_done, q * KC)
                        act.activation(hT[:, :, i * P:i * P + rows], psT[:, :, 0:rows], ACT.Copy).then_inc(hT_ready, 1)

                def start(q, W, rows):
                    squares_of(q, rows)
                    keep_turned(q, rows)

                def body(q, W, rows, ahead):
                    def gates(c):
                        n = q * KC + c
                        act.wait_ge(ri_done, 2 + n + 1)
                        act.wait_ge(v_done, n + 1)
                        act.wait_ge(y_done, q * KC)
                        act.activation(thr[:, c % 2, 0:W], psRI[:, c % 2, 0, 0:W], ACT.Tanh, scale=0.5, bias=par[:, 5, c:c + 1])
                        act.activation(thi[:, c % 2, 0:W], psRI[:, c % 2, 1, 0:W], ACT.Tanh, scale=0.5, bias=par[:, 6, c:c + 1])
                        act.drain()
                        act.activation(a[:, c, 0:W], thr[:, c % 2, 0:W], ACT.Exp, scale=sp[:, 5, c:c + 1], bias=sp[:, 5, c:c + 1])
                        act.activation(root[:, c, 0:W], thr[:, c % 2, 0:W], ACT.Tanh, scale=sp[:, 6, c:c + 1], bias=sp[:, 6, c:c + 1])
                        act.drain().then_inc(a_done, 1)
                    for c in range(KC):
                        n = q * KC + c
                        act.wait_ge(ab_done, n + 1)
                        act.wait_ge(conv_done, n + 1)
                        act.activation(xcat[:, c % 2, 4:4 + W], psAB[:, c % 2, 1, 0:W], ACT.Copy).then_inc(xb_copied, 1)
                        act.wait_ge(gelu_done, n + 1)
                        act.activation(gx[:, c % 2, 0:W], psAB[:, c % 2, 0, 0:W], ACT.Square).then_inc(gx_squared, 1)
                        act.wait_ge(p_done, n + 1)
                        act.activation(gx[:, c % 2, 0:W], gx[:, c % 2, 0:W], ACT.Tanh).then_inc(gth_done, 1)
                        if ahead and c == KC - 1:
                            squares_of(q + 1, rows)
                        if c:
                            gates(c - 1)
                    gates(KC - 1)
                    if ahead:
                        keep_turned(q + 1, rows)
                    act.activation(root[:, :, 0:W], root[:, :, 0:W], ACT.Sqrt).then_inc(sqrt_done, 1)
                    for t, i in tiles(q, rows):
                        act.wait_ge(res_done, t + 1)
                        act.dma_start(tile_rows(dst, t, rows), out[0:rows, :]).then_inc(res_out, 16)

                blocks(act, body, start)
                act.wait_ge(res_out, 16 * (2 * NQ + 1))

            @block.vector
            def _(dve):
                dve.sem_inc(x_used, 2)
                dve.sem_inc(gelu_done, 2)
                dve.sem_inc(conv_done, 2)
                dve.sem_inc(v_done, 2)
                dve.sem_inc(o_taken, 2)
                dve.memset(carry[:, :, :], 0.0)
                dve.memset(last_h[:, :], 0.0)
                dve.wait_ge(ends_turned, 1)
                dve.tensor_copy(par[:, :, :], psT[:, 0:1, 0:8 * KC].rearrange("p a (v c) -> p (a v) c", c=KC))
                dve.drain()
                dve.tensor_scalar(sp[:, 0, :], par[:, 7, :], -1.0, 0.0, ALU.mult, ALU.max)
                dve.drain()
                dve.scalar_tensor_tensor(sp[:, 1, :], sp[:, 0, :], 2.0, par[:, 7, :], ALU.mult, ALU.add).then_inc(consts, 1)
                dve.tensor_scalar(par[:, 5:7, :], par[:, 5:7, :], 0.5, None, ALU.mult)
                dve.wait_ge(consts, 2)
                dve.tensor_scalar(sp[:, 2, :], sp[:, 1, :], 2.0, None, ALU.add)
                dve.drain()
                dve.reciprocal(sp[:, 2, :], sp[:, 2, :])
                dve.drain()
                dve.tensor_tensor(sp[:, 1, :], sp[:, 1, :], sp[:, 2, :], ALU.mult)
                dve.drain()
                dve.tensor_tensor(sp[:, 2, :], sp[:, 1, :], sp[:, 1, :], ALU.mult)
                dve.memset(sp[:, 3, :], 2.0 / 21)
                dve.drain()
                for n in range(19, 0, -2):
                    dve.tensor_tensor(sp[:, 3, :], sp[:, 3, :], sp[:, 2, :], ALU.mult)
                    dve.drain()
                    dve.tensor_scalar(sp[:, 3, :], sp[:, 3, :], 2.0 / n, None, ALU.add)
                    dve.drain()
                dve.tensor_tensor(sp[:, 3, :], sp[:, 3, :], sp[:, 1, :], ALU.mult)
                dve.drain()
                dve.tensor_tensor(sp[:, 3, :], sp[:, 3, :], sp[:, 0, :], ALU.add)
                dve.drain()
                dve.tensor_scalar(sp[:, 5, :], sp[:, 3, :], -RG_C / 2, None, ALU.mult)
                dve.tensor_scalar(sp[:, 6, :], sp[:, 3, :], RG_C / 4, None, ALU.mult)
                dve.drain().then_inc(consts, 1)
                dve.wait_ge(ends_turned, 2)
                dve.tensor_copy(state[:, :, :], psAB[:, 0, 0, :].rearrange("p (k s) -> p k s", k=KC)).then_inc(consts, 1)
                dve.wait_ge(mod_in, 16 * 7)
                dve.tensor_tensor(gain[:, :], gain[:, :], h[:, 0], ALU.mult)
                dve.drain()

                def start(q, W, rows):
                    if rows == NS:
                        dve.drain().then_inc(mod_s, 1)
                        dve.wait_ge(mod_in, 16 * 14)
                        dve.tensor_tensor(gain[0:NS, :], gain[0:NS, :], norm_g_s[:, :], ALU.mult)
                        dve.drain()
                    for t, i in tiles(q, rows):
                        dve.wait_ge(rstd, t + 1)
                        dve.wait_ge(h_turned, t)
                        dve.scalar_tensor_tensor(h[0:rows, i], x[0:rows, i], rs[0:rows, i:i + 1], gain[0:rows, :], ALU.mult, ALU.mult)
                        dve.drain()
                        dve.tensor_tensor(h[0:rows, i], h[0:rows, i], shift[0:rows, :], ALU.add).then_inc(x_used, 1)

                def body(q, W, rows, ahead):
                    def weigh(c):
                        n = q * KC + c
                        dve.wait_ge(a_done, 2 + n + 1)
                        dve.scalar_tensor_tensor(thi[:, c % 2, 0:W], thi[:, c % 2, 0:W], 1.0, xc[:, c % 2, 0:W], ALU.add, ALU.mult)
                        dve.drain()
                        dve.scalar_tensor_tensor(v[:, c, 0:W], a[:, c, 0:W], 1.0, thi[:, c % 2, 0:W], ALU.add, ALU.mult).then_inc(v_done, 1)
                    for c in range(KC):
                        n = q * KC + c
                        cat, o = xcat[:, c % 2, :], xc[:, c % 2, 0:W]
                        dve.wait_ge(xb_copied, 2 + n + 1)
                        dve.wait_ge(ri_done, n + 1)
                        if rows == P:
                            dve.tensor_copy(cat[:, 1:4], carry[:, :, c])
                            dve.drain()
                            taps = [cat[:, 1 + j:1 + j + W] for j in range(CONV_W)]
                        else:
                            old = state[:, c, 0:NS * (CONV_W - 1)].rearrange("p (b j) -> p j b", j=CONV_W - 1)
                            taps = [old[:, j, :] for j in range(CONV_W - 1)] + [cat[:, 4:4 + W]]
                        dve.tensor_scalar(o, taps[0], par[:, 0, c:c + 1], par[:, 4, c:c + 1], ALU.mult, ALU.add)
                        if rows == P:
                            dve.tensor_copy(carry[:, :, c], cat[:, 1 + W:4 + W])
                        else:
                            dve.tensor_copy(xb_s[:, c, :], cat[:, 4:4 + W])
                        dve.drain()
                        for j in range(1, CONV_W):
                            dve.scalar_tensor_tensor(o, taps[j], par[:, j, c:c + 1], o, ALU.mult, ALU.add)
                            dve.drain()
                        dve.sem_inc(conv_done, 1)
                        dve.wait_ge(gx_squared, n + 1)
                        dve.tensor_scalar(gx[:, c % 2, 0:W], gx[:, c % 2, 0:W], GELU_K * GELU_C, GELU_K, ALU.mult, ALU.add)
                        dve.drain()
                        dve.tensor_tensor(gx[:, c % 2, 0:W], gx[:, c % 2, 0:W], psAB[:, c % 2, 0, 0:W], ALU.mult).then_inc(p_done, 1)
                        if c:
                            weigh(c - 1)
                        dve.wait_ge(gth_done, n + 1)
                        dve.scalar_tensor_tensor(g[:, c, 0:W], gx[:, c % 2, 0:W], 1.0, psAB[:, c % 2, 0, 0:W], ALU.add, ALU.mult).then_inc(gelu_done, 1)
                    if ahead:
                        start(q + 1, W, rows)
                    weigh(KC - 1)
                    dve.drain()
                    dve.wait_ge(sqrt_done, q + 1)
                    dve.scalar_tensor_tensor(v[:, :, 0:W], root[:, :, 0:W], 0.5, v[:, :, 0:W], ALU.mult, ALU.mult)
                    dve.drain()
                    for c in range(KC):
                        if rows == P:
                            dve.tensor_tensor_scan(root[:, c, 0:W], a[:, c, 0:W], v[:, c, 0:W], last_h[:, c:c + 1], ALU.mult, ALU.add)
                            dve.drain()
                        else:
                            old = state[:, c, NS * (CONV_W - 1):]
                            dve.tensor_tensor(root[:, c, 0:W], a[:, c, 0:W], old, ALU.mult)
                            dve.drain()
                            dve.tensor_tensor(root[:, c, 0:W], root[:, c, 0:W], v[:, c, 0:W], ALU.add)
                            dve.drain()
                            dve.tensor_copy(h_s[:, c, :], root[:, c, 0:W])
                        dve.scalar_tensor_tensor(g[:, c, 0:W], g[:, c, 0:W], 0.5, root[:, c, 0:W], ALU.mult, ALU.mult).then_inc(y_done, 1)
                    if rows == P:
                        dve.tensor_copy(last_h[:, :], root[:, :, W - 1:W].rearrange("p c a -> p (c a)"))
                    for t, i in tiles(q, rows):
                        dve.wait_ge(res_in, 16 * (t + 1))
                        dve.wait_ge(res_out, 16 * t)
                        if rows == NS:
                            dve.wait_ge(mod_in, 16 * 14)
                        for half in range(2):
                            cols = slice(half * 512, half * 512 + 512)
                            dve.wait_ge(out_done, 2 * t + half + 1)
                            dve.tensor_tensor(out[0:rows, cols], psO[0:rows, half, :], gate[0:rows, cols], ALU.mult).then_inc(o_taken, 1)
                        dve.drain()
                        dve.tensor_tensor(out[0:rows, :], out[0:rows, :], res[0:rows, :], ALU.add).then_inc(res_done, 1)
                blocks(dve, body, start)
                dve.drain().then_inc(ends_done, 1)
                dve.wait_ge(ends_turned, 3)
                dve.tensor_copy(ends[:, :, :], psT[0:KC * NS, 0:2, :])
                dve.tensor_copy(end_p[:, :, :], psO[0:KC, 0, :].rearrange("p (j n) -> p j n", n=P))
                dve.drain().then_inc(ends_done, 1)

            @block.tensor
            def _(pe):
                pe.sem_inc(ri_done, 2)
                pe.sem_inc(h_turned, 1)
                pe.wait_ge(const_in, 16 * (7 + 2))
                pe.wait_ge(w_loaded, 16 * 2 * KC)
                pe.transpose(psT[:, 0, 0:8 * KC], param_rows[:, :], ident[0:8 * KC, 0:8 * KC]).then_inc(ends_turned, 1)
                for k in range(KC):
                    last = pe.transpose(psAB[:, 0, 0, k * 32:(k + 1) * 32], state_rows[:, k * P:(k + 1) * P], ident[0:32, 0:32])
                last.then_inc(ends_turned, 1)
                pe.wait_ge(consts, 4)

                def project(q, W, chunks):
                    for c in chunks:
                        n = q * KC + c
                        pe.wait_ge(xb_copied, n + 1)
                        pe.wait_ge(gelu_done, n + 1)
                        for part in (1, 0):
                            for k in range(KC):
                                last = pe.matmul(psAB[:, c % 2, part, 0:W], w_in[:, k, part * D + c * P:part * D + (c + 1) * P],
                                                 hT[:, k, 0:W], start=(k == 0), stop=(k == KC - 1))
                        last.then_inc(ab_done, 1)

                def start(q, W, rows):
                    for t, i in tiles(q, rows):
                        pe.wait_ge(x_used, 2 + t + 1)
                        pe.wait_ge(hT_ready, t)
                        pe.sem_inc(spare, 1)
                        for k in range(KC):
                            last = pe.transpose(psT[:, k, 0:rows], h[0:rows, i, k * P:(k + 1) * P], ident[0:rows, 0:rows])
                        last.then_inc(h_turned, 1)
                        if i == 1 or rows == NS:
                            pe.wait_ge(hT_ready, t + 1)
                    project(q, W, (0, 1))

                def body(q, W, rows, ahead):
                    for c in range(KC):
                        if c > 1:
                            project(q, W, (c,))
                        if c:
                            recur(q, W, c - 1)
                    recur(q, W, KC - 1)
                    if ahead:
                        start(q + 1, W, rows)
                    pe.wait_ge(y_done, q * KC + KC)
                    for t, i in tiles(q, rows):
                        for half in range(2):
                            pe.wait_ge(o_taken, 2 * t + half + 1)
                            for k in range(KC):
                                last = pe.matmul(psO[0:rows, half, :], g[:, k, i * P:i * P + rows], w_out[:, k, half * 512:half * 512 + 512],
                                                 start=(k == 0), stop=(k == KC - 1))
                            last.then_inc(out_done, 1)

                def recur(q, W, c):
                    n = q * KC + c
                    pe.wait_ge(conv_done, 2 + n + 1)
                    pe.wait_ge(a_done, n + 1)
                    pe.matmul(psRI[:, c % 2, 0, 0:W], w_a[:, c, :], xc[:, c % 2, 0:W], start=True, stop=True)
                    pe.matmul(psRI[:, c % 2, 1, 0:W], w_x[:, c, :], xc[:, c % 2, 0:W], start=True, stop=True).then_inc(ri_done, 1)
                blocks(pe, body, start)
                pe.wait_ge(ends_done, 1)
                pe.transpose(psT[0:KC * NS, 0, :], h_s[:, :, :].rearrange("p c b -> p (c b)"), ident[:, :])
                pe.transpose(psT[0:KC * NS, 1, :], xb_s[:, :, :].rearrange("p c b -> p (c b)"), ident[:, :])
                for j in range(CONV_W - 1):
                    pe.transpose(psO[0:KC, 0, j * P:(j + 1) * P], carry[:, j, :], ident[:, :])
                pe.transpose(psO[0:KC, 0, 3 * P:4 * P], last_h[:, :], ident[:, :]).then_inc(ends_turned, 1)


def build(nc, T):
    with ExitStack() as stack:
        T["whole_run"] = stack
        def keep(name, shape, dt=F32):
            T[name] = stack.enter_context(nc.sbuf_tensor(name, shape, dt))
        keep("ident", [P, P])
        keep("power", [P, 3])
        phase_modulation(nc, T)
        with ExitStack() as attn:
            for name, shape in (("KT", [P, NKV // 2, SEQ]), ("kiT", [P, 2, SEQ]), ("V1", [P, NT, NKV, P])):
                T[name] = attn.enter_context(nc.sbuf_tensor(name, shape, F32))
            phase_project(nc, T)
            phase_attend(nc, T)
        phase_sample_index(nc, T)
        phase_sample_attend(nc, T)
        keep("dest", [P, NT + 1, 2], I32)
        keep("share", [P, NT + 1, 2])
        keep("plan", [1, PLAN_END], I32)
        phase_route(nc, T, 0, "xa")
        phase_experts(nc, T, 0)
        with ExitStack() as rec:
            for name, shape in (("rec_w_in_sb", [P, KC, 2 * D]), ("rec_w_out_sb", [P, KC, D])):
                T[name] = rec.enter_context(nc.sbuf_tensor(name, shape, F32))
            T["rec_w_loaded"] = stack.enter_context(nc.semaphore("rec_w_loaded"))
            phase_combine(nc, T, 0, "xa", "xb", False)
            phase_recurrent(nc, T, "xb", "xa")
        phase_route(nc, T, 1, "xa")
        phase_experts(nc, T, 1)
        phase_combine(nc, T, 1, "xa", None, True)


_INS = ["x_prompt", "x_sample", "cache_k", "cache_v", "cache_kidx", "state_h", "state_conv", "page_table",
        "c_prompt", "c_sample", "ada_w", "ada_b", "norm_mix_g", "norm_ffn_g", "norm_final_g",
        "attn_w_in", "attn_w_out", "rec_w_in", "rec_conv_w", "rec_conv_b", "rec_w_a", "rec_b_a",
        "rec_w_x", "rec_b_x", "rec_lambda", "rec_w_out", "moe_w_group", "moe_b_group",
        "moe_w_expert", "moe_b_expert", "moe_w1", "moe_w2"]
_SHAPES = {
    "x_prompt": (SEQ, D), "x_sample": (NS, D), "state_h": (NS, D), "state_conv": (NS, CONV_W - 1, D),
    "c_prompt": (1, D), "c_sample": (NS, D), "attn_w_in": (D, C_END), "attn_w_out": (D, D),
    "rec_w_in": (D, 2 * D), "rec_conv_w": (CONV_W, D), "rec_conv_b": (1, D),
    "rec_w_a": (KC, P, P), "rec_b_a": (1, D), "rec_w_x": (KC, P, P), "rec_b_x": (1, D), "rec_lambda": (1, D),
    "rec_w_out": (D, D), "norm_final_g": (1, D),
}
_OUTS = [("y_prompt", (SEQ, D), (1, SEQ, D)), ("y_sample", (NS, D), (NS, 1, D)),
         ("k_prompt", (SEQ, NKV * DH), (1, 1, SEQ, NKV, DH)), ("v_prompt", (SEQ, NKV * DH), (1, 1, SEQ, NKV, DH)),
         ("kidx_prompt", (SEQ, IDIM), (1, 1, SEQ, IDIM)), ("h_prompt", (1, D), (1, 1, D)),
         ("conv_prompt", (CONV_W - 1, D), (1, 1, CONV_W - 1, D)),
         ("k_sample", (NS, NKV * DH), (1, NS, 1, NKV, DH)), ("v_sample", (NS, NKV * DH), (1, NS, 1, NKV, DH)),
         ("kidx_sample", (NS, IDIM), (1, NS, 1, IDIM)), ("h_sample", (NS, D), (1, NS, D)),
         ("conv_sample", (NS, CONV_W - 1, D), (1, NS, CONV_W - 1, D))]


def rope_table():
    pos = np.concatenate([np.arange(SEQ), np.full(NS, PAST)]).astype(np.float32)
    inv = np.exp(np.float32(-math.log(500000.0)) * np.arange(HALF, dtype=np.float32) * np.float32(2.0 / ROT))
    ang = pos[:, None] * inv[None, :].astype(np.float32)
    return np.concatenate([np.cos(ang), np.cos(ang), -np.sin(ang), np.sin(ang)], axis=1).astype(np.float32)


def kernel(**inputs):
    import numpy as _np
    import concourse.bacc as _bacc
    from concourse.bass_utils import run_bass_kernel_spmd as _run

    nc = _bacc.Bacc("TRN2", target_bir_lowering=False, num_devices=1)
    arrays, T = {}, {}
    for name in _INS:
        a = _np.ascontiguousarray(inputs[name])
        if name in _SHAPES:
            a = a.reshape(_SHAPES[name])
        if name.startswith("cache"):
            a = a.reshape(a.shape[1], PAGE, -1)
        arrays[name + "_in"] = a
        T[name] = nc.dram_tensor(name + "_in", a.shape, mybir.dt.from_np(a.dtype), kind="ExternalInput").ap()
    arrays["rope_in"] = rope_table()
    T["rope"] = nc.dram_tensor("rope_in", (SEQ + NS, 2 * ROT), F32, kind="ExternalInput").ap()
    for name, shape, _ in _OUTS:
        T[name] = nc.dram_tensor(name + "_out", shape, F32, kind="ExternalOutput").ap()
    for name, shape, dt in (("mods", (2, 12, 1 + NS, 512), F32), ("qs", (SEQ + NS, C_K + 520), F32), ("xa", (SEQ + NS, D), F32), ("scores_s", (NS * SLOTS, P), F32),
                            ("hide_s", (NS, NKEY), F32), ("o_s", (NS, D), F32), ("xb", (NTOK, D), F32), ("hs", (NTOK, D), F32),
                            ("yb", (2 * NPAIR * BLK, D), F32), ("row_tok", (NBR * BLK, 1), I32)):
        T[name] = nc.dram_tensor(name + "_scratch", shape, dt).ap()
    build(nc, T)
    r = _run(nc, [arrays], core_ids=[0])
    return tuple(r.results[0][name + "_out"].reshape(shape) for name, _, shape in _OUTS)
```
